# Optimizing a Trainium2 kernel written in Bass

```python
import math
import jax
import jax.numpy as jnp
from jax import lax
import numpy as np

D_MODEL = 1024
BATCH = 1
SEQ = 256
DEPTH = 2
DEC_BATCH = 8
DEC_SEQ = 8
PAST_LEN = 1024
PAGE_SIZE = 128

N_A_LAYERS = DEPTH // 2
SSM_GROUP = 16
N_GROUPS = D_MODEL // SSM_GROUP
SSM_STATE = 64
DT_MIN = 1e-3
DT_MAX = 1e-1
N_HEADS = 16
HEAD_DIM = D_MODEL // N_HEADS
N_KV_HEADS = 4
GQA_GROUP = N_HEADS // N_KV_HEADS
CMP_BLOCK = 32
CMP_STRIDE = 16
CMP_HIDDEN = 2 * HEAD_DIM
SEL_BLOCK = 64
N_SEL = 16
WINDOW = 512
WIN_QBLOCK = 128
SEL_QBLOCK = 32
ROPE_THETA = 10000.0
D_FF = 2816
CONV_WIDTH = 3
EPS = 1e-6
NEG = -1e30

kernel_name = 'yoco_s5_nsa_convffn_step'

def rms_norm(x, g):
    x32 = x.astype(jnp.float32)
    y = x32 * lax.rsqrt(jnp.mean(x32 * x32, axis=-1, keepdims=True) + EPS)
    return (y * g.astype(jnp.float32)).astype(x.dtype)

def adaln(c, w, b, n):
    return jnp.split(jax.nn.silu(c) @ w + b, n, axis=-1)

def modulate(h, shift, scale):
    return h * (1.0 + scale[:, None, :]) + shift[:, None, :]

def rope(x, pos):
    half = x.shape[-1] // 2
    freqs = ROPE_THETA ** (-jnp.arange(half, dtype=jnp.float32) / half)
    ang = pos.astype(jnp.float32)[:, None] * freqs[None, :]
    cos = jnp.cos(ang)[None, :, None, :]
    sin = jnp.sin(ang)[None, :, None, :]
    x1, x2 = x[..., :half], x[..., half:]
    return jnp.concatenate([x1 * cos - x2 * sin, x2 * cos + x1 * sin], axis=-1).astype(x.dtype)

def cmul(ar, ai, br, bi):
    return ar * br - ai * bi, ar * bi + ai * br

def s5_mixer(h, lam_re, lam_im, log_dt, b_re, b_im, c_re, c_im, d_skip, w_glu, b_glu, h0):
    f32 = jnp.float32
    bsz, seq, _ = h.shape
    h32 = h.astype(f32)
    u = h32.reshape(bsz, seq, N_GROUPS, SSM_GROUP)
    dt = jnp.exp(log_dt.astype(f32))[:, None]
    lr, li = lam_re.astype(f32), lam_im.astype(f32)
    mag = jnp.exp(lr * dt)
    a_re, a_im = mag * jnp.cos(li * dt), mag * jnp.sin(li * dt)
    den = lr * lr + li * li
    z_re, z_im = cmul(a_re - 1.0, a_im, lr / den, -li / den)
    bu_re, bu_im = cmul(z_re, z_im,
                        jnp.einsum('blgc,gpc->blgp', u, b_re.astype(f32)),
                        jnp.einsum('blgc,gpc->blgp', u, b_im.astype(f32)))
    a_shape = (1, seq) + a_re.shape

    def combine(e1, e2):
        a1r, a1i, b1r, b1i = e1
        a2r, a2i, b2r, b2i = e2
        ar, ai = cmul(a2r, a2i, a1r, a1i)
        br, bi = cmul(a2r, a2i, b1r, b1i)
        return ar, ai, br + b2r, bi + b2i

    acc_re, acc_im, s_re, s_im = lax.associative_scan(
        combine, (jnp.broadcast_to(a_re, a_shape), jnp.broadcast_to(a_im, a_shape), bu_re, bu_im), axis=1)
    if h0 is not None:
        p_re, p_im = cmul(acc_re, acc_im, h0[0].astype(f32)[:, None], h0[1].astype(f32)[:, None])
        s_re, s_im = s_re + p_re, s_im + p_im
    y = (jnp.einsum('blgp,gcp->blgc', s_re, c_re.astype(f32))
         - jnp.einsum('blgp,gcp->blgc', s_im, c_im.astype(f32)))
    y = y.reshape(bsz, seq, D_MODEL) + d_skip.astype(f32) * h32
    g = jax.nn.gelu(y)
    out = g * jax.nn.sigmoid(g @ w_glu.astype(f32) + b_glu.astype(f32))
    return out.astype(h.dtype), s_re[:, -1], s_im[:, -1]

def conv_ffn(h, w_up, conv_w, conv_b, w_down, prefix):
    seq = h.shape[1]
    up = h @ w_up
    ext = jnp.concatenate([prefix.astype(up.dtype), up], axis=1)
    conv = conv_b
    for k in range(CONV_WIDTH):
        conv = conv + conv_w[k] * ext[:, k:k + seq]
    a, g = jnp.split(conv, 2, axis=-1)
    out = (jax.nn.silu(g) * a) @ w_down
    return out, ext[:, -(CONV_WIDTH - 1):]

def shared_kv(x, c, pos, p):
    bsz, seq, _ = x.shape
    shift, scale = adaln(c, p['w_mod_kv'], p['b_mod_kv'], 2)
    h = modulate(rms_norm(x, p['norm_kv']), shift, scale)
    kv = (h @ p['w_kv']).reshape(bsz, seq, 6, N_KV_HEADS, HEAD_DIM)
    rows = jnp.stack([kv[:, :, 0], kv[:, :, 1], rope(kv[:, :, 2], pos), kv[:, :, 3]], axis=2)
    win_rows = jnp.stack([rope(kv[:, :, 4], pos), kv[:, :, 5]], axis=2)
    return rows, win_rows

def compress(rows, pe, w1, b1, w2):
    t = rows.shape[1]
    nc = (t - CMP_BLOCK) // CMP_STRIDE + 1
    idx = np.arange(nc)[:, None] * CMP_STRIDE + np.arange(CMP_BLOCK)[None, :]
    blocks = rows[:, idx] + pe[None, None, :, None, :]
    hid = jax.nn.gelu(jnp.einsum('bnlkd,ldh->bnkh', blocks, w1.reshape(CMP_BLOCK, HEAD_DIM, CMP_HIDDEN)) + b1)
    return jnp.einsum('bnkh,hd->bnkd', hid, w2)

def sel_blocks(k):
    bsz, t = k.shape[:2]
    ns = -(-t // SEL_BLOCK)
    k = jnp.pad(k, ((0, 0), (0, ns * SEL_BLOCK - t), (0, 0), (0, 0)))
    return k.reshape(bsz, ns, SEL_BLOCK, N_KV_HEADS, HEAD_DIM).transpose(0, 3, 1, 2, 4)

def window_band(win_rows):
    seq = win_rows.shape[1]
    nqb = seq // WIN_QBLOCK
    pad = jnp.pad(win_rows, ((0, 0), (WINDOW, 0), (0, 0), (0, 0), (0, 0)))
    idx = np.arange(nqb)[:, None] * WIN_QBLOCK + np.arange(WINDOW + WIN_QBLOCK)[None, :]
    band = pad[:, idx]
    return band[:, :, :, 0], band[:, :, :, 1], jnp.asarray(idx - WINDOW)

def cmp_to_sel_matrix(nc, ns):
    r = SEL_BLOCK // CMP_STRIDE
    q = CMP_BLOCK // CMP_STRIDE
    offs = (np.arange(r)[:, None] - np.arange(q)[None, :]).reshape(-1)
    target = r * np.arange(ns)[None, :, None] + offs[None, None, :]
    m = (np.arange(nc)[:, None, None] == target).sum(-1)
    return jnp.asarray(m, jnp.float32)

def compressed_attention(qg, kc, vc, q_pos):
    nc = kc.shape[1]
    s = jnp.einsum('bqkgd,bckd->bkgqc', qg, kc).astype(jnp.float32)
    ends = jnp.arange(nc) * CMP_STRIDE + CMP_BLOCK - 1
    valid = ends[None, :] <= q_pos[:, None]
    p = jax.nn.softmax(jnp.where(valid, s, NEG), axis=-1) * valid
    o = jnp.einsum('bkgqc,bckd->bqkgd', p.astype(vc.dtype), vc)
    return o, p

def select_blocks(p_cmp, q_pos, ns):
    nc = p_cmp.shape[-1]
    score = jnp.einsum('bkgqc,cs->bkqs', p_cmp, cmp_to_sel_matrix(nc, ns))
    j = jnp.arange(ns)[None, :]
    cur = q_pos[:, None] // SEL_BLOCK
    valid = j * SEL_BLOCK <= q_pos[:, None]
    forced = (j == 0) | (j == cur) | (j == cur - 1)
    score = jnp.where(forced, jnp.inf, jnp.where(valid, score, -jnp.inf))
    return lax.top_k(score, min(N_SEL, ns))[1]

def selected_attention(qg, kb, vb, idx, q_pos):
    bsz, nkv = kb.shape[:2]
    bi = jnp.arange(bsz)[:, None, None, None]
    hi = jnp.arange(nkv)[None, :, None, None]
    kg = kb[bi, hi, idx]
    vg = vb[bi, hi, idx]
    s = jnp.einsum('bqkgd,bkqsld->bkgqsl', qg, kg).astype(jnp.float32)
    kpos = idx[..., None] * SEL_BLOCK + jnp.arange(SEL_BLOCK)
    mask = (kpos <= q_pos[None, None, :, None, None])[:, :, None]
    sh = s.shape
    p = jax.nn.softmax(jnp.where(mask, s, NEG).reshape(sh[:4] + (-1,)), axis=-1).reshape(sh)
    return jnp.einsum('bkgqsl,bkqsld->bqkgd', p.astype(vg.dtype), vg)

def selected_attention_blocked(qg, kb, vb, idx, q_pos, qblock):
    bsz, nq = qg.shape[:2]
    nb = nq // qblock
    qs = jnp.moveaxis(qg.reshape((bsz, nb, qblock) + qg.shape[2:]), 1, 0)
    ids = jnp.moveaxis(idx.reshape(idx.shape[:2] + (nb, qblock, idx.shape[-1])), 2, 0)
    ps = q_pos.reshape(nb, qblock)
    out = lax.map(lambda a: selected_attention(a[0], kb, vb, a[1], a[2]), (qs, ids, ps))
    return jnp.moveaxis(out, 0, 1).reshape((bsz, nq) + out.shape[3:])

def window_attention(qg, kb, vb, q_pos, k_pos):
    bsz, nq = qg.shape[:2]
    n = kb.shape[1]
    qb = qg.reshape((bsz, n, nq // n) + qg.shape[2:])
    qp = q_pos.reshape(n, nq // n)
    s = jnp.einsum('bnqkgd,bnskd->bnkgqs', qb, kb).astype(jnp.float32)
    diff = qp[:, :, None] - k_pos[:, None, :]
    mask = (diff >= 0) & (diff < WINDOW) & (k_pos[:, None, :] >= 0)
    p = jax.nn.softmax(jnp.where(mask[None, :, None, None], s, NEG), axis=-1)
    o = jnp.einsum('bnkgqs,bnskd->bnqkgd', p.astype(vb.dtype), vb)
    return o.reshape((bsz, nq) + o.shape[3:])

def nsa_mixer(h, pos, w_qg, w_o, ctx):
    bsz, nq, _ = h.shape
    proj = h @ w_qg
    q = proj[..., :N_HEADS * HEAD_DIM].reshape(bsz, nq, N_HEADS, HEAD_DIM)
    gates = jax.nn.sigmoid(proj[..., N_HEADS * HEAD_DIM:].astype(jnp.float32)).reshape(bsz, nq, 3, N_HEADS, 1)
    scale = HEAD_DIM ** -0.5
    grp = (bsz, nq, N_KV_HEADS, GQA_GROUP, HEAD_DIM)
    q_plain = (q * scale).reshape(grp)
    q_rot = (rope(q, pos) * scale).reshape(grp)
    o_cmp, p_cmp = compressed_attention(q_plain, ctx['kc'], ctx['vc'], pos)
    idx = select_blocks(p_cmp, pos, ctx['ks'].shape[2])
    qblk = SEL_QBLOCK if nq % SEL_QBLOCK == 0 else nq
    o_sel = selected_attention_blocked(q_rot, ctx['ks'], ctx['vs'], idx, pos, qblk)
    o_win = window_attention(q_rot, ctx['wk'], ctx['wv'], pos, ctx['wpos'])
    hs = (bsz, nq, N_HEADS, HEAD_DIM)
    o = (gates[:, :, 0] * o_cmp.reshape(hs) + gates[:, :, 1] * o_sel.reshape(hs)
         + gates[:, :, 2] * o_win.reshape(hs))
    return o.reshape(bsz, nq, N_HEADS * HEAD_DIM).astype(h.dtype) @ w_o

def build_context(rows, win_rows, past, p):
    seq = rows.shape[1]
    if past is None:
        full = rows
        wk, wv, wpos = window_band(win_rows)
        win_state = win_rows[:, -min(WINDOW, seq):]
    else:
        pool, table = past['pool'], past['page_table']
        past_rows = pool[table].reshape((table.shape[0], table.shape[1] * pool.shape[1]) + pool.shape[2:])
        past_len = past_rows.shape[1]
        full = jnp.concatenate([past_rows.astype(rows.dtype), rows], axis=1)
        w_buf = past['win'].shape[1]
        win_all = jnp.concatenate([past['win'].astype(win_rows.dtype), win_rows], axis=1)[:, None]
        wk, wv = win_all[:, :, :, 0], win_all[:, :, :, 1]
        wpos = (past_len - w_buf + jnp.arange(w_buf + seq))[None, :]
        win_state = win_rows
    kc = compress(full[:, :, 0], p['cmp_pe'][0], p['cmp_w1'][0], p['cmp_b1'][0], p['cmp_w2'][0])
    vc = compress(full[:, :, 1], p['cmp_pe'][1], p['cmp_w1'][1], p['cmp_b1'][1], p['cmp_w2'][1])
    ctx = {'kc': kc, 'vc': vc, 'ks': sel_blocks(full[:, :, 2]), 'vs': sel_blocks(full[:, :, 3]),
           'wk': wk, 'wv': wv, 'wpos': wpos}
    return ctx, win_state

def group_forward(x, c, pos, p, past):
    bsz = x.shape[0]
    ssm_re, ssm_im, convs = [], [], []
    ctx = None
    for layer in range(DEPTH):
        shift, scale, gate = adaln(c, p['w_mod'][layer, 0], p['b_mod'][layer, 0], 3)
        h = modulate(rms_norm(x, p['norm_pre'][layer, 0]), shift, scale)
        if layer < N_A_LAYERS:
            h0 = None if past is None else (past['ssm_re'][layer], past['ssm_im'][layer])
            out, s_re, s_im = s5_mixer(h, p['ssm_lam_re'][layer], p['ssm_lam_im'][layer], p['ssm_log_dt'][layer],
                                       p['ssm_b_re'][layer], p['ssm_b_im'][layer], p['ssm_c_re'][layer],
                                       p['ssm_c_im'][layer], p['ssm_d'][layer], p['w_glu'][layer],
                                       p['b_glu'][layer], h0)
            ssm_re.append(s_re)
            ssm_im.append(s_im)
        else:
            j = layer - N_A_LAYERS
            out = nsa_mixer(h, pos, p['w_qg'][j], p['w_o'][j], ctx)
        x = x + gate[:, None, :] * rms_norm(out, p['norm_post'][layer, 0])
        shift, scale, gate = adaln(c, p['w_mod'][layer, 1], p['b_mod'][layer, 1], 3)
        h = modulate(rms_norm(x, p['norm_pre'][layer, 1]), shift, scale)
        if past is None:
            prefix = jnp.zeros((bsz, CONV_WIDTH - 1, 2 * D_FF), h.dtype)
        else:
            prefix = past['conv'][layer]
        out, conv_state = conv_ffn(h, p['ffn_w_up'][layer], p['ffn_conv_w'][layer], p['ffn_conv_b'][layer],
                                   p['ffn_w_down'][layer], prefix)
        convs.append(conv_state)
        x = x + gate[:, None, :] * rms_norm(out, p['norm_post'][layer, 1])
        if layer == N_A_LAYERS - 1:
            rows, win_rows = shared_kv(x, c, pos, p)
            ctx, win_state = build_context(rows, win_rows, past, p)
    return x, rows, win_state, jnp.stack(ssm_re), jnp.stack(ssm_im), jnp.stack(convs)

def setup_inputs(seed: int = 0) -> dict:
    key = jax.random.key(seed)
    ks = iter(jax.random.split(key, 64))

    def nrm(shape, scale=1.0):
        return jax.random.normal(next(ks), shape, jnp.float32) * scale

    n_a, n_b = N_A_LAYERS, DEPTH - N_A_LAYERS
    n_pages = PAST_LEN // PAGE_SIZE
    n_used = DEC_BATCH * n_pages
    n_phys = n_used + max(1, n_used // 4)
    kvd = (N_KV_HEADS, HEAD_DIM)
    d2f = 2 * D_FF
    page_table = jax.random.permutation(next(ks), n_phys)[:n_used].reshape(DEC_BATCH, n_pages).astype(jnp.int32)
    lam_im = jnp.pi * jnp.arange(SSM_STATE, dtype=jnp.float32) + nrm((n_a, N_GROUPS, SSM_STATE), 0.01)
    log_dt = jax.random.uniform(next(ks), (n_a, N_GROUPS), jnp.float32, math.log(DT_MIN), math.log(DT_MAX))
    return {
        'x_prompt': nrm((BATCH, SEQ, D_MODEL)),
        'x_sample': nrm((DEC_BATCH, DEC_SEQ, D_MODEL)),
        'cache_nsa_paged': nrm((n_phys, PAGE_SIZE, 4) + kvd),
        'cache_nsa_window': nrm((DEC_BATCH, min(WINDOW, PAST_LEN), 2) + kvd),
        'state_ssm_re': nrm((n_a, DEC_BATCH, N_GROUPS, SSM_STATE), 0.1),
        'state_ssm_im': nrm((n_a, DEC_BATCH, N_GROUPS, SSM_STATE), 0.1),
        'state_ffn_conv': nrm((DEPTH, DEC_BATCH, CONV_WIDTH - 1, d2f)),
        'page_table': page_table,
        'c_prompt': nrm((BATCH, D_MODEL)),
        'c_sample': nrm((DEC_BATCH, D_MODEL)),
        'norm_pre': 1.0 + nrm((DEPTH, 2, D_MODEL), 0.01),
        'norm_post': 1.0 + nrm((DEPTH, 2, D_MODEL), 0.01),
        'w_mod': nrm((DEPTH, 2, D_MODEL, 3 * D_MODEL), 0.5 * D_MODEL ** -0.5),
        'b_mod': nrm((DEPTH, 2, 3 * D_MODEL), 0.2),
        'ssm_lam_re': -0.5 + nrm((n_a, N_GROUPS, SSM_STATE), 0.01),
        'ssm_lam_im': lam_im,
        'ssm_log_dt': log_dt,
        'ssm_b_re': nrm((n_a, N_GROUPS, SSM_STATE, SSM_GROUP), (2 * SSM_GROUP) ** -0.5),
        'ssm_b_im': nrm((n_a, N_GROUPS, SSM_STATE, SSM_GROUP), (2 * SSM_GROUP) ** -0.5),
        'ssm_c_re': nrm((n_a, N_GROUPS, SSM_GROUP, SSM_STATE), (2 * SSM_STATE) ** -0.5),
        'ssm_c_im': nrm((n_a, N_GROUPS, SSM_GROUP, SSM_STATE), (2 * SSM_STATE) ** -0.5),
        'ssm_d': nrm((n_a, D_MODEL), 0.5),
        'w_glu': nrm((n_a, D_MODEL, D_MODEL), D_MODEL ** -0.5),
        'b_glu': nrm((n_a, D_MODEL), 0.02),
        'ffn_w_up': nrm((DEPTH, D_MODEL, d2f), D_MODEL ** -0.5),
        'ffn_conv_w': nrm((DEPTH, CONV_WIDTH, d2f), CONV_WIDTH ** -0.5),
        'ffn_conv_b': nrm((DEPTH, d2f), 0.02),
        'ffn_w_down': nrm((DEPTH, D_FF, D_MODEL), D_FF ** -0.5),
        'norm_kv': 1.0 + nrm((D_MODEL,), 0.01),
        'w_mod_kv': nrm((D_MODEL, 2 * D_MODEL), 0.5 * D_MODEL ** -0.5),
        'b_mod_kv': nrm((2 * D_MODEL,), 0.2),
        'w_kv': nrm((D_MODEL, 6 * N_KV_HEADS * HEAD_DIM), D_MODEL ** -0.5),
        'cmp_pe': nrm((2, CMP_BLOCK, HEAD_DIM), 0.5),
        'cmp_w1': nrm((2, CMP_BLOCK * HEAD_DIM, CMP_HIDDEN), (CMP_BLOCK * HEAD_DIM) ** -0.5),
        'cmp_b1': nrm((2, CMP_HIDDEN), 0.02),
        'cmp_w2': nrm((2, CMP_HIDDEN, HEAD_DIM), CMP_HIDDEN ** -0.5),
        'w_qg': nrm((n_b, D_MODEL, N_HEADS * HEAD_DIM + 3 * N_HEADS), D_MODEL ** -0.5),
        'w_o': nrm((n_b, N_HEADS * HEAD_DIM, D_MODEL), (N_HEADS * HEAD_DIM) ** -0.5),
    }

def reference(x_prompt, x_sample, cache_nsa_paged, cache_nsa_window, state_ssm_re, state_ssm_im,
              state_ffn_conv, page_table, c_prompt, c_sample, norm_pre, norm_post, w_mod, b_mod,
              ssm_lam_re, ssm_lam_im, ssm_log_dt, ssm_b_re, ssm_b_im, ssm_c_re, ssm_c_im, ssm_d,
              w_glu, b_glu, ffn_w_up, ffn_conv_w, ffn_conv_b, ffn_w_down, norm_kv, w_mod_kv, b_mod_kv,
              w_kv, cmp_pe, cmp_w1, cmp_b1, cmp_w2, w_qg, w_o):
    p = {'norm_pre': norm_pre, 'norm_post': norm_post, 'w_mod': w_mod, 'b_mod': b_mod,
         'ssm_lam_re': ssm_lam_re, 'ssm_lam_im': ssm_lam_im, 'ssm_log_dt': ssm_log_dt,
         'ssm_b_re': ssm_b_re, 'ssm_b_im': ssm_b_im, 'ssm_c_re': ssm_c_re, 'ssm_c_im': ssm_c_im,
         'ssm_d': ssm_d, 'w_glu': w_glu, 'b_glu': b_glu, 'ffn_w_up': ffn_w_up, 'ffn_conv_w': ffn_conv_w,
         'ffn_conv_b': ffn_conv_b, 'ffn_w_down': ffn_w_down, 'norm_kv': norm_kv, 'w_mod_kv': w_mod_kv,
         'b_mod_kv': b_mod_kv, 'w_kv': w_kv, 'cmp_pe': cmp_pe, 'cmp_w1': cmp_w1, 'cmp_b1': cmp_b1,
         'cmp_w2': cmp_w2, 'w_qg': w_qg, 'w_o': w_o}
    past = {'pool': cache_nsa_paged, 'page_table': page_table, 'win': cache_nsa_window,
            'ssm_re': state_ssm_re, 'ssm_im': state_ssm_im, 'conv': state_ffn_conv}
    past_len = page_table.shape[1] * cache_nsa_paged.shape[1]
    pos_p = jnp.arange(x_prompt.shape[1])
    pos_s = past_len + jnp.arange(x_sample.shape[1])
    y_p, rows_p, win_p, sre_p, sim_p, conv_p = group_forward(x_prompt, c_prompt, pos_p, p, None)
    y_s, rows_s, win_s, sre_s, sim_s, conv_s = group_forward(x_sample, c_sample, pos_s, p, past)
    return (y_p, y_s, rows_p, rows_s, win_p, win_s, sre_p, sim_p, sre_s, sim_s, conv_p, conv_s)


_drawn_inputs = setup_inputs


def setup_inputs(seed=0):
    import zlib

    import numpy as np

    out = dict(_drawn_inputs(seed))
    spreads = {}
    factors = {'norm_pre': 5.379,
     'norm_post': 8.0,
     'ssm_lam_re': 15.616,
     'b_glu': 8.0,
     'ffn_conv_b': 5.033,
     'norm_kv': 5.699,
     'cmp_b1': 35.035}
    for name, (base, spread) in spreads.items():
        noise = np.random.default_rng([zlib.crc32(name.encode()), seed]).standard_normal(out[name].shape)
        drawn = base * np.exp(spread * noise) if base else spread * noise
        out[name] = jnp.asarray(drawn.astype(out[name].dtype))
    for name, factor in factors.items():
        out[name] = (out[name] * factor).astype(out[name].dtype)
    return out
```

```python
from contextlib import ExitStack

import concourse.bass as bass
from concourse import mybir

P = 128
D, SEQ, DB, DS, PAST, PAGE = 1024, 256, 8, 8, 1024, 128
NH, KVH, GQA, HD = 16, 4, 4, 64
T = SEQ + DB * DS
NB = 1 + DB
KT = D // P
ST = 32
FT = 22
NPG = PAST // PAGE
WIN = 512
NC, NCP = 63, 15
NFREE = 14
NEG = -1e30
EPS = 1e-6
EXT = 2 + SEQ + DB * (DS + 2)
CW = EXT - 2
NPJ = KVH * 2
RING = 3
SLOT = 4096
ROUND = 12582912.0
ROUND12 = 3072.0
INV_2PI = 0.15915494309189535
TWO_PI_HI, TWO_PI_LO = 6.28125, 0.0019353071795864769
TWO_PI_IN = 6.283185

CONST = [("ident", P), ("ones", P), ("rot", P), ("group_sum", P), ("gate_spread", 3 * P), ("cos", T), ("sin", T),
         ("causal", 2 * P), ("new_mask", DS), ("win_mask", DS), ("gate_pick", DS), ("cmp_valid", 2 * NCP),
         ("cmp_neg", 2 * NCP), ("blocks", NFREE), ("scan_run", T), ("steps", 32)]
VEC = [("norm_pre", 32), ("norm_post", 32), ("norm_kv", 8), ("b_mod", 112), ("ssm_d", 8), ("b_glu", 8),
       ("conv_w", 264), ("conv_b", 88), ("cmp_pe", 32), ("cmp_b1", 2), ("cmp_w2", 128)]


def build_step(nc, dram):
    F32 = mybir.dt.float32
    BF16 = mybir.dt.bfloat16
    I32 = mybir.dt.int32
    ALU = mybir.AluOpType
    ACT = mybir.ActivationFunctionType
    AX = mybir.AxisListType.X
    ctx = ExitStack()
    with ctx:
        sems = {}

        def S(name):
            if name not in sems:
                sems[name] = ctx.enter_context(nc.semaphore(name))
            return sems[name]

        def sb(name, cols, dt=F32, rows=P):
            return ctx.enter_context(nc.sbuf_tensor(name, [rows, cols], dt))

        consts = sb("consts_sb", sum(n for _, n in CONST))
        vec = sb("vec_sb", sum(n for _, n in VEC))
        x_sb, h_sb = sb("x_sb", KT * T), sb("h_sb", KT * T)
        x = x_sb[:, :].rearrange("p (k t) -> p k t", t=T)
        h = h_sb[:, :].rearrange("p (k t) -> p k t", t=T)

        def parts(v, n):
            return v.bitcast(BF16).rearrange("p (k e t) -> p k e t", k=n, e=2)

        hb = parts(h_sb[:, :], KT)
        wk = sb("wk_sb", KT * T)[:, :].rearrange("p (k t) -> p k t", t=T)
        ring = sb("ring", RING * SLOT)[:, :].rearrange("p (s n) -> p s n", n=SLOT)
        ring_hi = ring.rearrange("p s n -> p (s n)").bitcast(BF16).rearrange("p (s n e) -> p s n e", s=RING, e=2)[:, :, :, 1]
        lo = sb("lo", 2 * 1024)[:, :].bitcast(BF16).rearrange("p (s n) -> p s n", s=2)
        mod = sb("mod", 112 * NB)[:, :].rearrange("p (m b) -> p m b", b=NB)
        silc_sb = sb("silc", 2 * KT * NB)
        silc = silc_sb[:, 0:KT * NB].rearrange("p (k b) -> p k b", b=NB)
        silb = silc_sb[:, KT * NB:].bitcast(BF16).rearrange("p (e k b) -> p e k b", e=2, b=NB)
        rinv = sb("rinv", T)[:, :]
        rroot = sb("rroot", T)[:, :]
        kcT = sb("kcT", NB * 2 * NC)[:, :].rearrange("p (b e n) -> p b e n", b=NB, e=2)
        vc = sb("vc", NB * 256)[:, :].rearrange("p (b n) -> p b n", b=NB)
        cmp_bias = sb("cmp_bias", 2)[:, :]
        eps = sb("eps", 1)[:, :]
        conv_rows = sb("conv_rows", 2 * FT * 2 * NB)[:, :].rearrange("p (j a b r) -> p j a b r", a=2, b=NB, r=2)
        pages = sb("pages", DB * NPG, I32, rows=1)
        prefix = sb("prefix_sb", 2 * FT * 2 * DB)[:, :].rearrange("p (j a b r) -> p j a b r", a=2, b=DB, r=2)
        AR = 20850
        arena = sb("arena", AR)
        PS = ctx.enter_context(nc.psum_tensor("PS", [P, 8, 512], F32))

        def bank(i):
            return PS[:, i, :]

        def table(t, cols):
            out, at = {}, 0
            for n, c in cols:
                out[n] = t[:, at:at + c]
                at += c
            return out

        C = table(consts, CONST)
        V = table(vec, VEC)
        ident = C["ident"]
        b_mod = V["b_mod"]
        conv_w = V["conv_w"].rearrange("p (l m k) -> p l m k", l=2, k=3)
        conv_b = V["conv_b"].rearrange("p (l m) -> p l m", l=2)
        pe_ = V["cmp_pe"].rearrange("p (e l) -> p e l", e=2)
        w2 = V["cmp_w2"].rearrange("p (e d) -> p e d", e=2)

        def carver():
            at = [0]

            def carve(cols):
                v = arena[:, at[0]:at[0] + cols]
                at[0] += cols
                assert at[0] <= AR, at[0]
                return v
            return carve

        carve = carver()
        BT = carve(2 * 8 * P).rearrange("p (e f n) -> p e f n", e=2, f=8)
        CX = carve(2 * ST * 32).rearrange("p (e s n) -> p e s n", e=2, s=ST)
        w1 = carve(2048).rearrange("p (l n) -> p l n", n=P)
        XT = carve(2 * 2048).rearrange("p (s h n) -> p s h n", s=2, h=KVH)
        HG = carve(2 * KVH * NC).rearrange("p (s h n) -> p s h n", s=2, h=KVH)
        E = carve(2 * ST * 32).rearrange("p (e s n) -> p e s n", e=2, s=ST)
        AH = carve(2 * ST * DB).rearrange("p (e s b) -> p e s b", e=2, s=ST)
        FS = carve(ST * 2 * NB).rearrange("p (s e b) -> p s e b", s=ST, e=2)
        SP_ = carve(24 * ST).rearrange("p (i s) -> p i s", s=ST)
        TC = x_sb[:, 0:4 * T].rearrange("p (s i t) -> p s i t", s=2, i=2)
        TS = x_sb[:, 4 * T:8 * T].rearrange("p (s i t) -> p s i t", s=2, i=2)
        decay = carve(4 * T)
        t12 = carve(8 * T)
        gb = parts(t12, KT)
        t1f, t2f, zf = t12[:, 0:4 * T], t12[:, 4 * T:], wk[:, 4:8, :].rearrange("p k t -> p (k t)")
        VSf = [carve(4 * T), wk[:, 0:4, :].rearrange("p k t -> p (k t)")]

        def unit(v):
            return v.rearrange("p (i e t) -> p i e t", i=2, e=2)

        decay4, t1, t2, z = unit(decay), unit(t1f), unit(t2f), unit(zf)
        VS = [unit(v) for v in VSf]
        pt1, pt2 = carve(512), carve(512)
        braw = XT[:, 0].rearrange("p h n -> p (h n)")[:, 0:1024].rearrange("p (e s c) -> p e s c", e=2, s=ST)
        craw = XT[:, 0].rearrange("p h n -> p (h n)")[:, 1024:2048].rearrange("p (e s c) -> p e s c", e=2, s=ST)
        BX = XT[:, 1].rearrange("p h n -> p (h n)").rearrange("p (e s c) -> p e s c", e=2, s=ST)
        h0 = t2f[:, 0:512].rearrange("p (e s b) -> p e s b", e=2, s=ST)
        phase_sin = wk[:, 0:4, :].rearrange("p k t -> p (k t)")[:, 0:1024].rearrange("p (s n) -> p s n", n=32)
        phase_cos = wk[:, 4:8, :].rearrange("p k t -> p (k t)")[:, 0:1024].rearrange("p (s n) -> p s n", n=32)
        phase_tmp = t1f[:, 0:1024].rearrange("p (s n) -> p s n", n=32)
        sig = VSf[0][:, 0:2 * T].rearrange("p (s t) -> p s t", s=2)
        lam = SP_[:, 0:2, :]
        ldt = SP_[:, 2, :]
        NP_ = ["dt", "lrdt", "th", "k", "thr", "phi", "phi_hi", "phi_lo", "mag", "a_re", "a_im", "den", "u", "v", "w", "z_re", "z_im",
               "zl_re", "zl_im", "q"]
        pr = {n: SP_[:, 3 + i, :] for i, n in enumerate(NP_)}

        carve = carver()
        U = parts(carve(FT * T), FT)
        UF = carve(3 * T).rearrange("p (s t) -> p s t", s=3)
        XE = carve(3 * 2 * EXT).rearrange("p (s a t) -> p s a t", s=3, a=2)
        CV = carve(3 * 2 * CW).rearrange("p (s a t) -> p s a t", s=3, a=2)
        SG = carve(3 * CW).rearrange("p (s t) -> p s t", s=3)

        carve = carver()
        KV = carve(12 * T).rearrange("p (m t) -> p m t", t=T)
        qr_sb = carve(KT * T)
        ob = parts(qr_sb, KT)
        Qr = qr_sb.rearrange("p (m t) -> p m t", t=T)
        Qp = wk
        O = h
        QBr = carve(2 * DB * P).rearrange("p (e b n) -> p e b n", e=2, b=DB)
        SC1 = carve(2108)
        QBp = SC1[:, 0:2048].rearrange("p (e b n) -> p e b n", e=2, b=DB)
        VT = carve(2 * 512).rearrange("p (k n) -> p k n", k=2)
        SC0 = carve(2108)
        SC = [SC0, SC1]
        PT = carve(2560)
        VN = PT[:, 1920:2432]
        small = carve(1390)
        XP = SC0[:, 0:1024].rearrange("p (h n) -> p h n", h=8)
        HP = SC0[:, 1024:1144].rearrange("p (s n) -> p s n", s=2)
        rt1 = PT[:, 0:T]
        PC = small[:, 0:512].rearrange("p (b n) -> p b n", b=DB)
        imp = small[:, 512:624].rearrange("p (b n) -> p b n", b=DB)
        imp2 = small[:, 624:736].rearrange("p (b n) -> p b n", b=DB)
        drop = small[:, 736:864].rearrange("p (b n) -> p b n", b=DB)
        cm = small[:, 864:872]
        cs = small[:, 872:880]
        cr = small[:, 880:888]
        gs = small[:, 888:912].rearrange("p (c b) -> p c b", c=3)
        gp = small[:, 912:1008].rearrange("p (k n) -> p k n", k=2)
        gf = small[:, 1008:1072]
        gx = small[:, 1072:1264].rearrange("p (c t) -> p c t", c=3)
        nmax = small[:, 1264:1288].rearrange("p (s n) -> p s n", s=2)
        ssum = small[:, 1288:1312].rearrange("p (s n) -> p s n", s=2)
        fac = small[:, 1312:1336].rearrange("p (s n) -> p s n", s=2)
        imin = small[:, 1336:1344]
        imax = small[:, 1344:1352]
        cmax = small[:, 1352:1360]

        stream, place = [], {}

        def add_chunk(name, loads, used_by, used_at):
            place[name] = len(stream)
            stream.append((name, loads, used_by, used_at))

        def whole(src):
            n = src.shape[-1]
            return [(lambda s, n=n: s[:, 0:n], src, None)]

        units = 2 * 8
        for j in range(6):
            add_chunk(f"mod{j}", whole(dram["w_mod"][j]), "mod_mm", j + 1)
        mod_of_unit = []
        nxt = 6
        for u in range(units):
            n = 2 if u < 6 else 1
            mod_of_unit.append(list(range(nxt, nxt + n)))
            nxt += n
        assert nxt == 28
        mod_src = [dram["w_mod"][j] for j in range(12)] + [dram["w_mod_kv"][j] for j in range(4)] + [dram["w_mod"][12 + j] for j in range(12)]
        mod_bank = [5, 6, 5, 6, 5, 6] + [5] * 22
        mod_tile = [4 * j for j in range(12)] + [96 + 4 * j for j in range(4)] + [48 + 4 * j for j in range(12)]
        for u in range(units):
            for j in mod_of_unit[u]:
                add_chunk(f"mod{j}", whole(mod_src[j]), "mod_mm", j + 1)
        for j in range(2):
            add_chunk(f"glu{j}", whole(dram["w_glu"][j]), "glu_mm", 4 * j + 4)

        def ffn_chunks(l):
            for j in range(11):
                add_chunk(f"up{l}_{j}", whole(dram["w_up"][11 * l + j]), f"up{l}_mm", 2 * j + 2)
            for j in range(8):
                add_chunk(f"down{l}_{j}", whole(dram["w_down"][8 * l + j]), f"down{l}_mm", j + 1)

        ffn_chunks(0)
        for j in range(3):
            add_chunk(f"kv{j}", whole(dram["w_kv"][j]), "kv_mm", 4 * j + 4)
        add_chunk("w1", [(lambda s, e=e: s[:, 2048 * e:2048 * e + 2048], dram["cmp_w1"][e], None) for e in range(2)], "pcmp_mm", 2)
        add_chunk("gate", whole(dram["w_gate"]), "gate_mm", 3)
        for j in range(2):
            add_chunk(f"q{j}", whole(dram["w_q"][j]), "q_mm", 4 * j + 4)

        def k_chunk(b):
            loads = [(lambda s, j=j: s[:, 0:2048].rearrange("p (e n) -> p e n", e=2)[:, :, PAGE * j:PAGE * j + PAGE],
                      "pool_k", NPG * b + j) for j in range(NPG)]
            loads.append((lambda s: s[:, 2048:3072], dram["win_k"][b], None))
            add_chunk(f"k{b}", loads, "s_mm", NPJ + b + 1)

        def v_chunk(b):
            loads = [(lambda s, j=j: s[:, 256 * j:256 * j + 256], "pool_v", NPG * b + j) for j in range(NPG)]
            loads.append((lambda s: s[:, 2048:3072], dram["win_v"][b], None))
            add_chunk(f"v{b}", loads, "pv_mm", NPJ + b + 1)

        k_chunk(0)
        for b in range(DB):
            if b + 1 < DB:
                k_chunk(b + 1)
            v_chunk(b)
        for j in range(2):
            add_chunk(f"o{j}", whole(dram["w_o"][j]), "o_mm", 4 * j + 4)
        ffn_chunks(1)

        landed = []
        slot_count = [0] * RING
        for n, (_, loads, _, _) in enumerate(stream):
            slot_count[n % RING] += 16 * len(loads)
            landed.append(slot_count[n % RING])

        def arrived(eng, name):
            n = place[name]
            eng.wait_ge(S(f"ring{n % RING}"), landed[n])
            return ring[:, n % RING, :]

        jobs = [("prompt", hd, qt) for hd in range(KVH) for qt in range(2)] + [("sample", b, 0) for b in range(DB)]
        NG = [(5 if kind == "sample" else 3 + 2 * qt) for kind, _, qt in jobs]
        NE = [(6 if kind == "sample" else n) for (kind, _, _), n in zip(jobs, NG)]
        groups_before = [sum(NG[:j]) for j in range(len(jobs) + 1)]
        evacs_before = [sum(NE[:j]) for j in range(len(jobs) + 1)]
        NX = [(2 if kind == "sample" else 12) for kind, _, _ in jobs]
        NV = [(5 if kind == "sample" else 3) for kind, _, _ in jobs]
        NPR = [(2 if kind == "sample" else 9) for kind, _, _ in jobs]
        NOE = [(2 if kind == "sample" else 1) for kind, _, _ in jobs]

        def before(counts, j):
            return sum(counts[:j])

        pieces = {}
        for name, loads, _, _ in stream:
            if name[0:3] in ("mod", "glu") or name[0:2] in ("up", "kv") or name[0] in "qo" or name[0:4] == "down":
                for half in range(2):
                    pieces[name, half] = len(pieces)
        piece_list = list(pieces)

        def piece_tiles(name):
            return 11 if name[0:4] == "down" else 16

        nth_norm = {r: n + 1 for n, r in enumerate((0, 1, 2, 3, 4, 6, 7, 8))}
        nth_split = {r: n + 1 for n, r in enumerate((2, 4, 5, 7))}
        nth_mod = {r: n + 1 for n, r in enumerate((0, 2, 4, 5, 7))}
        down_banks = (6, 7, 0, 1)
        block = ctx.enter_context(nc.Block())

        @block.sync
        def _(sp):
            def page(i):
                return sp.value_load(pages[0:1, i:i + 1], min_val=0, max_val=dram["pool_v"].shape[0] - 1)

            def chunk(name):
                n = place[name]
                _, loads, _, _ = stream[n]
                if n >= RING:
                    _, _, used_by, used_at = stream[n - RING]
                    sp.wait_ge(S(used_by), used_at)
                for dst, src, pg in loads:
                    d = dst(ring[:, n % RING, :])
                    if pg is None:
                        sp.dma_start(d, src).then_inc(S(f"ring{n % RING}"), 16)
                    else:
                        s = dram[src][page(pg)]
                        if src == "pool_k":
                            s = s.rearrange("p (e n) -> p e n", e=2)
                        sp.dma_start(d, s).then_inc(S(f"ring{n % RING}"), 16)

            sp.dma_start(silc.rearrange("p k b -> p (k b)"), dram["c"].rearrange("p k b -> p (k b)")).then_inc(S("c_in"), 16)
            sp.dma_start(pages[:, :], dram["page_table"]).then_inc(S("pages_in"), 16)
            sp.dma_start(lam, dram["lam"].rearrange("p (i s) -> p i s", s=ST)).then_inc(S("params_in"), 16)
            for e in range(2):
                sp.dma_start(ldt[64 * e:64 * e + 64, :], dram["log_dt"][e].broadcast_to([64, ST])).then_inc(S("params_in"), 16)
            sp.dma_start(consts[:, :], dram["consts"]).then_inc(S("params_in"), 16)
            sp.dma_start(vec[:, :], dram["vec"]).then_inc(S("vec_in"), 16)
            for n in range(RING):
                chunk(stream[n][0])
            sp.dma_start(braw, dram["ssm_b"].rearrange("p (e s c) -> p e s c", e=2, s=ST)).then_inc(S("bc_in"), 16)
            sp.dma_start(craw, dram["ssm_c"].rearrange("p (e s c) -> p e s c", e=2, s=ST)).then_inc(S("bc_in"), 16)
            sp.dma_start(h0, dram["ssm_h0"].rearrange("p (e s b) -> p e s b", e=2, s=ST)).then_inc(S("bc_in"), 16)
            sp.dma_start(x, dram["x"]).then_inc(S("x_in"), 16)
            for n in range(RING, 6):
                chunk(stream[n][0])
            sp.dma_start(w1, dram["cmp_w1"][0].rearrange("p (l n) -> p l n", n=P)).then_inc(S("w1_in"), 16)
            sp.wait_ge(S("pages_in"), 16)
            for u in range(units):
                for j in mod_of_unit[u]:
                    chunk(f"mod{j}")
                e, b = u // DB, u % DB
                if u == DB:
                    sp.wait_ge(S("hid_mm"), DB)
                    sp.dma_start(w1, dram["cmp_w1"][1].rearrange("p (l n) -> p l n", n=P)).then_inc(S("w1_in"), 16)
                if u < 2:
                    sp.wait_ge(S("bt_mm"), 4)
                    sp.wait_ge(S("cx_done"), 1)
                else:
                    sp.wait_ge(S("hid_mm"), u - 1)
                for j in range(NPG):
                    sp.dma_start(XT[:, u % 2, :, 64 * j:64 * j + 64],
                                 dram["pool_cmp"][e][page(NPG * b + j)].rearrange("p (h n) -> p h n", h=KVH)
                                 ).then_inc(S(f"xt{u % 2}_in"), 16)
            for j in range(2):
                chunk(f"glu{j}")
            sp.dma_start(prefix, dram["prefix"][0].rearrange("p (j a b r) -> p j a b r", a=2, b=DB, r=2)).then_inc(S("prefix_in"), 16)
            sp.wait_ge(S("s_ready"), units)
            sp.dma_start(x, dram["x"]).then_inc(S("x_in"), 16)
            sp.wait_ge(S("last_states"), 2 * units)
            sp.dma_start(dram["out_ssm"], FS.rearrange("p s e b -> p (s e b)")).then_inc(S("out_ssm"), 16)
            first_after = place["up0_0"]
            for n in range(first_after, len(stream)):
                name = stream[n][0]
                chunk(name)
                if name == "kv0":
                    sp.wait_ge(S("conv_rows0"), 2 * FT)
                    sp.dma_start(dram["out_conv"][0], conv_rows.rearrange("p j a b r -> p (j a b r)")).then_inc(S("out_conv"), 16)
                    sp.wait_ge(S("prefixed0"), FT)
                    sp.dma_start(prefix, dram["prefix"][1].rearrange("p (j a b r) -> p j a b r", a=2, b=DB, r=2)).then_inc(S("prefix_in"), 16)
                if name == "gate":
                    sp.wait_ge(S("roped"), 4)
                    sp.wait_ge(S("kv_ev"), 12)
                    sp.dma_start(dram["out_kv"], KV).then_inc(S("out_kv"), 16)
            sp.wait_ge(S("conv_rows1"), 2 * FT)
            sp.dma_start(dram["out_conv"][1], conv_rows.rearrange("p j a b r -> p (j a b r)")).then_inc(S("out_conv"), 16)
            sp.wait_ge(S("x_done3"), KT + 1)
            sp.dma_start(dram["out_y"], x).then_inc(S("out_y"), 16)
            sp.wait_ge(S("out_ssm"), 16)
            sp.wait_ge(S("out_conv"), 32)
            sp.wait_ge(S("out_kv"), 16)
            sp.wait_ge(S("out_y"), 16)

        @block.tensor
        def _(pe):
            def product(out, name, tile, hi, low, start, stop):
                n, per = place[name], piece_tiles(name)
                p = pieces[name, tile // per]
                if tile % per == 0:
                    pe.wait_ge(S("lo_ready"), p + 1)
                w = ring_hi[:, n % RING, P * tile:P * tile + P]
                wl = lo[:, p % 2, P * (tile % per):P * (tile % per) + P]
                mm = pe.matmul(out, wl, hi, start=start, stop=False)
                if tile % per == per - 1:
                    mm.then_inc(S("lo_used"), 1)
                pe.matmul(out, w, hi, start=False, stop=False)
                return pe.matmul(out, w, low, start=False, stop=stop)

            def modulation(j):
                if j >= 2:
                    pe.wait_ge(S("mod_ev"), 4 * (j - 1) if j < 6 else 4 * j)
                for m in range(4):
                    for k in range(KT):
                        mm = product(PS[:, mod_bank[j], NB * m:NB * m + NB], f"mod{j}", KT * m + k, silb[:, 0, k, :], silb[:, 1, k, :],
                                     k == 0, k == KT - 1)
                mm.then_inc(S("mod_mm"), 1)

            def sums(r):
                for k in range(KT):
                    if k == 0:
                        pe.wait_ge(S("sqa"), nth_norm[r])
                    if k == 4:
                        pe.wait_ge(S("sqv"), nth_norm[r])
                    mm = pe.matmul(PS[:, 7, 0:T], C["ones"], h[:, k, :], start=(k == 0), stop=(k == KT - 1))
                mm.then_inc(S("sum"), 1)

            def h_ready(r):
                pe.wait_ge(S("hp"), KT * nth_mod[r])
                pe.wait_ge(S("hs"), nth_mod[r])

            def dense(tag, chunks, kt, src, per, banks, ev, ready):
                m = 0
                for name in chunks:
                    for i in range(per):
                        if m >= len(banks):
                            pe.wait_ge(S(ev), m - len(banks) + 1)
                        for k in range(kt):
                            if m == 0:
                                pe.wait_ge(S(ready[0]), ready[1] + k + 1)
                            mm = product(PS[:, banks[m % len(banks)], 0:T], name, kt * i + k, src[:, k, 0, :], src[:, k, 1, :],
                                         k == 0, k == kt - 1)
                        mm.then_inc(S(f"{tag}_mm"), 1)
                        m += 1

            def split_of(r):
                return "h_lo", KT * (nth_split[r] - 1)

            def ffn(l):
                ready = split_of((2, 7)[l])
                for j in range(FT):
                    if j >= 3:
                        pe.wait_ge(S(f"up_ev{l}"), 2 * (j - 2))
                    for a in range(2):
                        for k in range(KT):
                            if j == 0 and a == 0:
                                pe.wait_ge(S(ready[0]), ready[1] + k + 1)
                            mm = product(PS[:, 2 * (j % 3) + a, 0:T], f"up{l}_{j // 2}", 16 * (j % 2) + KT * a + k,
                                         hb[:, k, 0, :], hb[:, k, 1, :], k == 0, k == KT - 1)
                    mm.then_inc(S(f"up{l}_mm"), 1)
                dense(f"down{l}", [f"down{l}_{j}" for j in range(8)], FT, U, 1, down_banks, f"down{l}_ev", (f"u_lo{l}", 0))

            pe.wait_ge(S("silb"), 2)
            for j in range(6):
                modulation(j)
            pe.wait_ge(S("bx_done"), 4)
            for q in range(16):
                e, f = q // 8, q % 8
                mm = pe.transpose(PS[:, q // 4, P * (q % 4):P * (q % 4) + P],
                                  BX[:, e, 4 * f:4 * f + 4, :].rearrange("p s c -> p (s c)"), ident)
                if q % 4 == 3:
                    mm.then_inc(S("bt_mm"), 1)
            sums(0)
            h_ready(0)
            pe.wait_ge(S("bt_ev"), 4)

            def inputs_of(u):
                f = u // 2
                if u >= 1:
                    pe.wait_ge(S("u_read"), 2 * u)
                for i in range(2):
                    r = 32 * (2 * (u % 2) + i)
                    for e in range(2):
                        mm = pe.matmul(PS[:, 2 * i + e, 0:T], BT[r:r + 32, e, f, :], h[r:r + 32, f, :], start=True, stop=True)
                mm.then_inc(S("u_mm"), 1)

            def hidden(u):
                e = u // DB
                if u % DB == 0:
                    pe.wait_ge(S("w1_in"), 16 * (e + 1))
                    if e == 1:
                        pe.wait_ge(S("hid_ev"), u)
                    for l in range(16):
                        mm = pe.matmul(PS[:, 6, 500:501], w1[:, l, :], pe_[:, e, l:l + 1], start=(l == 0), stop=(l == 15))
                    mm.then_inc(S("pb_mm"), 1)
                    pe.wait_ge(S("pb_ev"), e + 1)
                pe.wait_ge(S(f"xt{u % 2}_in"), 16 * NPG * (u // 2 + 1))
                if u >= 1:
                    pe.wait_ge(S("hid_ev"), u)
                for l in range(16):
                    mm = pe.matmul(PS[:, 6, 0:KVH * NC], w1[:, l, :], XT[:, u % 2, :, l:l + 8 * (NC - 1) + 1:8],
                                   start=(l == 0), stop=(l == 15))
                mm.then_inc(S("hid_mm"), 1)

            def compressed(u):
                pe.wait_ge(S("hid_ev"), u + 1)
                if u >= 1:
                    pe.wait_ge(S("kc_ev"), u)
                hg = HG[:, u % 2]
                if u < DB:
                    for hp in range(2):
                        mm = pe.matmul(PS[64 * hp:64 * hp + 64, 7, 0:2 * NC], w2[:, 0, :], hg[:, hp:4:2, :], start=True, stop=True)
                else:
                    for hd in range(KVH):
                        mm = pe.matmul(PS[0:NC, 7, HD * hd:HD * hd + HD], hg[:, hd, :], w2[:, 1, :], start=True, stop=True)
                mm.then_inc(S("kc_mm"), 1)

            def outputs_of(u):
                f = u // 2
                pe.wait_ge(S("s_ready"), u + 1)
                if u % 2 == 0 and f >= 1:
                    pe.wait_ge(S("y_read"), f)
                for i in range(2):
                    r = 32 * (2 * (u % 2) + i)
                    for e in range(2):
                        mm = pe.matmul(PS[r:r + 32, 4, 0:T], CX[:, e, 2 * u + i, :], VS[u % 2][:, i, e, :], start=(e == 0), stop=(e == 1))
                mm.then_inc(S("y_mm"), 1)

            for u in range(units):
                inputs_of(u)
                hidden(u)
                modulation(mod_of_unit[u][0])
                if u >= 1:
                    compressed(u - 1)
                    outputs_of(u - 1)
                for j in mod_of_unit[u][1:]:
                    modulation(j)
            compressed(units - 1)
            outputs_of(units - 1)

            dense("glu", ["glu0", "glu1"], KT, gb, 4, (0, 1, 2, 3), "glu_ev", ("g_lo", 0))
            sums(1)
            sums(2)
            ffn(0)
            sums(3)

            sums(4)
            dense("kv", ["kv0", "kv1", "kv2"], KT, hb, 4, (0, 1, 2, 3), "kv_ev", split_of(4))

            def rotated(i, src):
                if i >= 2:
                    pe.wait_ge(S("rope_read"), i - 1)
                pe.matmul(PS[:, 4 + i % 2, 0:T], C["rot"], src, start=True, stop=True).then_inc(S("rope_mm"), 1)

            pe.wait_ge(S("kv_ev"), 12)
            for i, m in enumerate((4, 5, 8, 9)):
                rotated(i, KV[:, m, :])
            pw = arrived(pe, "w1").rearrange("p (e l n) -> p e l n", e=2, l=16)
            for e in range(2):
                for hd in range(KVH):
                    for par in range(2):
                        hp = hd % 2
                        mm = pe.matmul(PS[64 * par:64 * par + 64, e, P * hd:P * hd + P], ident[:, 64 * hp:64 * hp + 64],
                                       KV[:, 2 * e + hd // 2, par:SEQ:2], start=True, stop=True)
                mm.then_inc(S("pair_mm"), 1)
            for e in range(2):
                pe.wait_ge(S("pair_ev"), e + 1)
                for l in range(16):
                    mm = pe.matmul(PS[:, 2 + e, 0:KVH * NCP], pw[:, e, l, :], XP[:, KVH * e:KVH * e + KVH, l:l + 8 * (NCP - 1) + 1:8],
                                   start=(l == 0), stop=(l == 15))
                mm.then_inc(S("pcmp_mm"), 1)
            pe.wait_ge(S("hp_ev"), 2)
            hp_ = HP.rearrange("p e (h n) -> p e h n", n=NCP)
            for hp in range(2):
                mm = pe.matmul(PS[64 * hp:64 * hp + 64, 6, 0:2 * NCP], w2[:, 0, :], hp_[:, 0, hp:4:2, :], start=True, stop=True)
            mm.then_inc(S("pkc_mm"), 1)
            for hd in range(KVH):
                mm = pe.matmul(PS[0:NCP, 7, HD * hd:HD * hd + HD], hp_[:, 1, hd, :], w2[:, 1, :], start=True, stop=True)
            mm.then_inc(S("pkc_mm"), 1)

            pe.wait_ge(S("hp_ev"), 2)
            for n in range(2):
                for sl in range(2):
                    for hh in range(2):
                        at = 256 * sl + P * hh
                        mm = pe.transpose(PS[:, n, at:at + P], KV[:, (6, 10)[sl] + hh, P * n:P * n + P], ident)
                mm.then_inc(S("vt_mm"), 1)

            h_ready(5)
            wg = arrived(pe, "gate")[:, 0:KT * 3 * NH].rearrange("p (k n) -> p k n", k=KT)
            pe.wait_ge(S("pkc_ev"), 2)
            for k in range(KT):
                mm = pe.matmul(PS[0:3 * NH, 7, 0:DB * DS], wg[:, k, :], wk[:, k, SEQ:T], start=(k == 0), stop=(k == KT - 1))
            mm.then_inc(S("gate_mm"), 1)
            for qt in range(2):
                at = 64 + 3 * NH * qt
                for k in range(KT):
                    mm = pe.matmul(PS[:, 7, at:at + 3 * NH], wk[:, k, P * qt:P * qt + P], wg[:, k, :], start=(k == 0), stop=(k == KT - 1))
                mm.then_inc(S("gate_mm"), 1)
            pe.wait_ge(S("vt_ev"), 2)
            dense("q", ["q0", "q1"], KT, hb, 4, (0, 1, 2, 3), "q_ev", split_of(5))
            for i in range(4, 12):
                pe.wait_ge(S("q_ev"), i - 3)
                rotated(i, Qp[:, i - 4, :])
            pe.wait_ge(S("gate_ev"), 1)
            for br in range(3):
                mm = pe.matmul(PS[:, 6, 64 * br:64 * br + 64], C["gate_spread"][0:3 * NH, P * br:P * br + P], gf[0:3 * NH, :],
                               start=True, stop=True)
            mm.then_inc(S("spread_mm"), 1)

            pe.wait_ge(S("qbp_done"), 4)
            pe.wait_ge(S("q_ev"), KT)
            for b in range(DB):
                for hh in range(2):
                    mm = pe.matmul(PS[:, 0, NC * b:NC * b + NC], QBp[:, hh, b, :], kcT[:, b, hh, :], start=(hh == 0), stop=(hh == 1))
            mm.then_inc(S("c_mm"), 1)
            pe.wait_ge(S("imp_ready"), 1)
            pe.matmul(PS[:, 1, 0:DB * NFREE], C["group_sum"], imp.rearrange("p b n -> p (b n)"), start=True, stop=True).then_inc(S("imp_mm"), 1)

            def scores(j):
                kind, a, qt = jobs[j]
                if j == 0:
                    pe.wait_ge(S("drop_done"), 1)
                    pe.wait_ge(S("roped"), 12)
                else:
                    pe.wait_ge(S("s_evd"), before(NV, j))
                if kind == "prompt":
                    hh, hp, K = a // 2, a % 2, P * (qt + 1)
                    r = slice(64 * hp, 64 * hp + 64)
                    q = slice(P * qt, P * qt + P)
                    for g in range(GQA):
                        for br, m in ((0, 4), (2, 8)):
                            at = g * K
                            pe.matmul(PS[:, br + at // 512, at % 512:at % 512 + K], Qr[r, 4 * hh + g, q], KV[r, m + hh, 0:K],
                                      start=True, stop=True)
                        mm = pe.matmul(PS[:, 4, NCP * g:NCP * g + NCP], Qp[r, 4 * hh + g, q], kcT[r, DB, hh, 0:NCP], start=True, stop=True)
                else:
                    ks = arrived(pe, f"k{a}")
                    if a == 0:
                        pe.wait_ge(S("qbr_done"), 4)
                    new = slice(SEQ + DS * a, SEQ + DS * a + DS)
                    sel = ks[:, 0:2048].rearrange("p (e n) -> p e n", e=2)
                    win = ks[:, 2048:3072].rearrange("p (e n) -> p e n", e=2)
                    for out, rhs in ((PS[:, 0, :], sel[:, :, 0:512]), (PS[:, 1, :], sel[:, :, 512:1024]), (PS[:, 2, :], win),
                                     (PS[:, 3, 0:DS], KV[:, 4:6, new]), (PS[:, 3, DS:2 * DS], KV[:, 8:10, new])):
                        for hh in range(2):
                            mm = pe.matmul(out, QBr[:, hh, a, :], rhs[:, hh, :], start=(hh == 0), stop=(hh == 1))
                mm.then_inc(S("s_mm"), 1)

            def turned(j):
                kind, a, qt = jobs[j]
                sc = SC[j % 2]
                pe.wait_ge(S("p_ready"), before(NPR, j + 1))
                if kind == "prompt":
                    K = P * (qt + 1)
                    cols = [[(base + g * K + P * kt, P) for g in range(GQA)] for base in (0, 1024) for kt in range(qt + 1)]
                    cols.append([(2048 + NCP * g, NCP) for g in range(GQA)])
                    groups = [[(sc[:, c:c + n], n) for c, n in grp] for grp in cols]
                else:
                    groups = [[(sc[:, c + P * i:c + P * i + P], P) for i in range(4)] for c in (0, 512, 1032)]
                    groups.append([(sc[:, 1024:1032], DS), (sc[:, 1544:1552], DS), (PC[:, a, 0:NC], NC)])
                    new = slice(SEQ + DS * a, SEQ + DS * a + DS)
                    groups.append([(KV[:, m, new], DS) for m in (6, 7, 10, 11)])
                for n, grp in enumerate(groups):
                    G = groups_before[j] + n
                    if G >= 2:
                        jj = max(i for i in range(len(jobs)) if groups_before[i] <= G - 2)
                        k = G - 2 - groups_before[jj]
                        done = evacs_before[jj] + k + 1 + (1 if k >= 3 and jobs[jj][0] == "sample" else 0)
                        pe.wait_ge(S("tr_ev"), done)
                    for i, (src, rows) in enumerate(grp):
                        mm = pe.transpose(PS[0:rows, 5 + G % 2, P * i:P * i + P], src, ident)
                    mm.then_inc(S("tr_mm"), 1)

            def values(j):
                kind, a, qt = jobs[j]
                if j >= 1:
                    pe.wait_ge(S("o_ev"), before(NOE, j))
                pe.wait_ge(S("tr_ev"), evacs_before[j + 1])
                if kind == "prompt":
                    hp = a % 2
                    out = PS[64 * hp:64 * hp + 64, 7, :]
                    ops = [(VT[:, kt, 256 * sl + HD * a:256 * sl + HD * a + HD], P) for sl in range(2) for kt in range(qt + 1)]
                    ops.append((vc[0:NCP, DB, HD * a:HD * a + HD], NCP))
                    for n, (lhs, rows) in enumerate(ops):
                        mm = pe.matmul(out, lhs, PT[0:rows, 512 * n:512 * n + 512], start=(n == 0), stop=(n == len(ops) - 1))
                else:
                    vs = arrived(pe, f"v{a}")
                    for hh in range(2):
                        hc = P * hh
                        ops = [(vs[:, 256 * c + hc:256 * c + hc + P], P) for c in range(12)]
                        ops += [(VN[0:DS, 256 * sl + hc:256 * sl + hc + P], DS) for sl in range(2)]
                        ops.append((vc[0:NC, a, hc:hc + P], NC))
                        for n, (lhs, rows) in enumerate(ops):
                            mm = pe.matmul(PS[:, 7, 64 * hh:64 * hh + 64], lhs, PT[0:rows, P * n + 64 * hh:P * n + 64 * hh + 64],
                                           start=(n == 0), stop=(n == len(ops) - 1))
                mm.then_inc(S("pv_mm"), 1)

            scores(0)
            for j in range(len(jobs)):
                if j + 1 < len(jobs):
                    scores(j + 1)
                turned(j)
                values(j)
            dense("o", ["o0", "o1"], KT, ob, 4, (0, 1, 2, 3), "o_ev2", ("o_lo", 0))
            sums(6)
            sums(7)
            ffn(1)
            sums(8)

        @block.scalar
        def _(act):
            def squares(r, src, ready, count):
                act.wait_ge(S(ready), count)
                act.activation(h[:, 0:4, :], src[:, 0:4, :], ACT.Square).then_inc(S("sqa"), 1)

            def root(r):
                act.wait_ge(S("sum"), nth_norm[r])
                act.activation(rroot, PS[:, 7, 0:T], ACT.Sqrt, scale=1.0 / D, bias=eps).then_inc(S("root"), 1)

            def modulated(r, tile):
                dst = h if r == 0 else wk
                for k in range(KT):
                    act.wait_ge(S("scaled"), KT * (nth_mod[r] - 1) + k + 1)
                    act.activation(dst[:, k, 0:SEQ], dst[:, k, 0:SEQ], ACT.Identity, bias=mod[:, tile + k, 0:1],
                                   scale=mod[:, tile + 8 + k, 0:1]).then_inc(S("hp"), 1)

            def modulation(j):
                act.wait_ge(S("mod_mm"), j + 1)
                for m in range(4):
                    tile = mod_tile[j] + m
                    act.activation(mod[:, tile, :], PS[:, mod_bank[j], NB * m:NB * m + NB], ACT.Identity,
                                   bias=b_mod[:, tile:tile + 1]).then_inc(S("mod_ev"), 1)

            def tiles_out(tag, dst, n, ev, scale=1.0, banks=(0, 1, 2, 3)):
                for m in range(n):
                    act.wait_ge(S(f"{tag}_mm"), m + 1)
                    act.activation(dst[:, m, :], PS[:, banks[m % len(banks)], 0:T], ACT.Copy, scale=scale).then_inc(S(ev), 1)

            def ffn(l):
                act.wait_ge(S(f"ext_zero{l}"), 3)
                for j in range(FT):
                    s = j % 3
                    e = XE[:, s]
                    act.wait_ge(S(f"up{l}_mm"), j + 1)
                    if j >= 3:
                        act.wait_ge(S(f"conv2_{l}"), 2 * (j - 2))
                        act.wait_ge(S(f"conv_rows{l}"), 2 * (j - 2))
                    pair = PS[:, 2 * (j % 3):2 * (j % 3) + 2, :]
                    act.activation(e[:, :, 2:2 + SEQ], pair[:, :, 0:SEQ], ACT.Copy).then_inc(S(f"up_ev{l}"), 1)
                    act.activation(e[:, :, 2 + SEQ:].rearrange("p a (b r) -> p a b r", b=DB)[:, :, :, 2:],
                                   pair[:, :, SEQ:T].rearrange("p a (b r) -> p a b r", b=DB), ACT.Copy).then_inc(S(f"up_ev{l}"), 1)
                    act.wait_ge(S(f"up_ev{l}"), 2 * j + 2)
                    act.wait_ge(S(f"prefixed{l}"), j + 1)
                    if j >= 3:
                        act.wait_ge(S(f"u_mul{l}"), 2 * (j - 2))
                    for a in range(2):
                        m = 2 * j + a
                        act.activation(CV[:, s, a, :], e[:, a, 0:CW], ACT.Identity, bias=conv_b[:, l, m:m + 1],
                                       scale=conv_w[:, l, m, 0:1]).then_inc(S(f"conv0_{l}"), 1)
                    if j >= 1:
                        gate_of(l, j - 1)
                    if j >= 2:
                        high_of(l, j - 2)
                gate_of(l, FT - 1)
                high_of(l, FT - 2)
                high_of(l, FT - 1)
                tiles_out(f"down{l}", wk, KT, f"down{l}_ev", banks=down_banks)

            def high_of(l, j):
                act.wait_ge(S(f"u_mul{l}"), 2 * j + 2)
                act.activation(U[:, j, 0, :], UF[:, j % 3, :], ACT.Copy).then_inc(S(f"u_hi{l}"), 1)

            def gate_of(l, j):
                act.wait_ge(S(f"conv2_{l}"), 2 * j + 2)
                act.activation(SG[:, j % 3, :], CV[:, j % 3, 1, :], ACT.Silu).then_inc(S(f"sg{l}"), 1)

            act.wait_ge(S("eps"), 1)
            act.wait_ge(S("c_in"), 16)
            act.activation(silc, silc, ACT.Silu).then_inc(S("silc"), 1)
            act.wait_ge(S("silc"), 1)
            act.activation(silb[:, 0], silc, ACT.Copy).then_inc(S("silb"), 1)
            act.wait_ge(S("params_in"), 64)
            act.activation(pr["dt"], ldt, ACT.Exp).then_inc(S("dt"), 1)
            act.wait_ge(S("lrdt"), 1)
            act.activation(pr["mag"], pr["lrdt"], ACT.Exp).then_inc(S("mag"), 1)
            act.wait_ge(S("phases"), 2)
            act.activation(E[:, 1], phase_sin, ACT.Sin, scale=TWO_PI_IN).then_inc(S("trig"), 1)
            act.activation(E[:, 0], phase_cos, ACT.Sin, scale=TWO_PI_IN).then_inc(S("trig"), 1)
            act.wait_ge(S("vec_in"), 16)
            for j in range(6):
                modulation(j)
            squares(0, x, "x_in", 16)
            for i in range(4):
                act.wait_ge(S("bt_mm"), i + 1)
                act.activation(BT.rearrange("p e f n -> p (e f n)")[:, 512 * i:512 * i + 512], bank(i), ACT.Copy).then_inc(S("bt_ev"), 1)
            root(0)
            modulated(0, 0)

            def hidden(u):
                e = u // DB
                if u % DB == 0:
                    act.wait_ge(S("pb_mm"), e + 1)
                    act.activation(cmp_bias[:, e:e + 1], PS[:, 6, 500:501], ACT.Identity, bias=V["cmp_b1"][:, e:e + 1]).then_inc(S("pb_ev"), 1)
                    act.wait_ge(S("pb_ev"), e + 1)
                act.wait_ge(S("hid_mm"), u + 1)
                if u >= 2:
                    act.wait_ge(S("kc_mm"), u - 1)
                act.activation(HG[:, u % 2].rearrange("p h n -> p (h n)"), PS[:, 6, 0:KVH * NC], ACT.Gelu_apprx_tanh,
                               bias=cmp_bias[:, e:e + 1]).then_inc(S("hid_ev"), 1)

            def compressed(u):
                act.wait_ge(S("kc_mm"), u + 1)
                b = u % DB
                if u < DB:
                    act.activation(kcT[:, b], PS[:, 7, 0:2 * NC].rearrange("p (e n) -> p e n", e=2), ACT.Copy).then_inc(S("kc_ev"), 1)
                else:
                    act.activation(vc[0:NC, b, :], PS[0:NC, 7, 0:KVH * HD], ACT.Copy).then_inc(S("kc_ev"), 1)

            def last_states(u):
                act.wait_ge(S("s_ready"), u + 1)
                v = VS[u % 2]
                act.activation(FS[:, 2 * u:2 * u + 2, :, 0], v[:, :, :, SEQ - 1], ACT.Copy).then_inc(S("last_states"), 1)
                act.activation(FS[:, 2 * u:2 * u + 2, :, 1:], v[:, :, :, SEQ + DS - 1::DS], ACT.Copy).then_inc(S("last_states"), 1)

            def gelu(f):
                act.wait_ge(S("y_read"), f + 1)
                act.activation(h[:, f, :], h[:, f, :], ACT.Gelu_apprx_tanh).then_inc(S("g_ready"), 1)

            for u in range(units):
                hidden(u)
                modulation(mod_of_unit[u][0])
                if u >= 1:
                    compressed(u - 1)
                    last_states(u - 1)
                for j in mod_of_unit[u][1:]:
                    modulation(j)
                if u >= 3 and u % 2 == 1:
                    gelu((u - 3) // 2)
            compressed(units - 1)
            last_states(units - 1)
            gelu(7)
            for m in range(KT):
                act.wait_ge(S("glu_mm"), m + 1)
                if m >= 2:
                    act.wait_ge(S("wk_done"), m - 1)
                act.activation(sig[:, m % 2, :], PS[:, m % 4, 0:T], ACT.Sigmoid, bias=V["b_glu"][:, m:m + 1]).then_inc(S("glu_ev"), 1)
            squares(1, wk, "wk_done", KT)
            root(1)
            squares(2, x, "x_done0", KT + 1)
            root(2)
            modulated(2, 24)
            ffn(0)
            squares(3, wk, "down0_ev", KT)
            root(3)
            squares(4, x, "x_done1", KT + 1)
            root(4)
            modulated(4, 96)

            tiles_out("kv", KV, 12, "kv_ev")
            for e in range(2):
                act.wait_ge(S("pair_mm"), e + 1)
                act.activation(XP[:, KVH * e:KVH * e + KVH, :].rearrange("p h n -> p (h n)"), bank(e), ACT.Copy).then_inc(S("pair_ev"), 1)
            for e in range(2):
                act.wait_ge(S("pcmp_mm"), e + 1)
                act.activation(HP[:, e, :], PS[:, 2 + e, 0:KVH * NCP], ACT.Gelu_apprx_tanh, bias=cmp_bias[:, e:e + 1]).then_inc(S("hp_ev"), 1)
            act.wait_ge(S("pkc_mm"), 2)
            act.activation(kcT[:, DB, :, 0:NCP], PS[:, 6, 0:2 * NCP].rearrange("p (e n) -> p e n", e=2), ACT.Copy).then_inc(S("pkc_ev"), 1)
            act.activation(vc[0:NCP, DB, :], PS[0:NCP, 7, 0:KVH * HD], ACT.Copy).then_inc(S("pkc_ev"), 1)
            for n in range(2):
                act.wait_ge(S("vt_mm"), n + 1)
                act.activation(VT[:, n, :], bank(n), ACT.Copy).then_inc(S("vt_ev"), 1)
            modulated(5, 48)
            act.wait_ge(S("gate_mm"), 3)
            act.activation(gf[0:3 * NH, :], PS[0:3 * NH, 7, 0:DB * DS], ACT.Sigmoid).then_inc(S("gate_ev"), 1)
            act.activation(gp, PS[:, 7, 64:64 + 6 * NH].rearrange("p (k n) -> p k n", k=2), ACT.Sigmoid).then_inc(S("gate_ev"), 1)
            tiles_out("q", Qp, KT, "q_ev", scale=HD ** -0.5)
            act.wait_ge(S("c_shift"), 1)
            act.activation(PC[:, :, 0:NC], PC[:, :, 0:NC], ACT.Exp).then_inc(S("c_exp"), 1)

            for j, (kind, a, qt) in enumerate(jobs):
                sc, s = SC[j % 2], j % 2
                act.wait_ge(S("nmax"), j + 1)
                if j >= 2:
                    act.wait_ge(S("fac"), j - 1)
                if kind == "prompt":
                    K = P * (qt + 1)
                    for br, base, n in ((0, 2048, NCP), (1, 0, K), (2, 1024, K)):
                        for g in range(GQA):
                            i = 4 * br + g
                            v = sc[:, base + g * n:base + g * n + n]
                            act.activation(v, v, ACT.Exp, bias=nmax[:, s, i:i + 1], accum_out=ssum[:, s, i:i + 1]).then_inc(S("exp"), 1)
                else:
                    for i, v in enumerate((sc[:, 0:1032], sc[:, 1032:1552])):
                        act.activation(v, v, ACT.Exp, bias=nmax[:, s, i:i + 1], accum_out=ssum[:, s, i:i + 1]).then_inc(S("exp"), 1)
                for n in range(NG[j]):
                    G = groups_before[j] + n
                    act.wait_ge(S("tr_mm"), G + 1)
                    if n == 0 and j >= 1:
                        act.wait_ge(S("pv_mm"), j)
                    bk = 5 + G % 2
                    if kind == "sample" and n == 4:
                        act.activation(VN[0:DS, :], PS[0:DS, bk, :], ACT.Copy).then_inc(S("tr_ev"), 1)
                    elif kind == "sample" and n == 3:
                        act.activation(PT[0:DS, 1536:1792], PS[0:DS, bk, 0:256], ACT.Copy).then_inc(S("tr_ev"), 1)
                        act.activation(PT[0:NC, 1792:1920], PS[0:NC, bk, 256:384], ACT.Copy).then_inc(S("tr_ev"), 1)
                    else:
                        rows = NCP if kind == "prompt" and n == NG[j] - 1 else P
                        act.activation(PT[0:rows, 512 * n:512 * n + 512], PS[0:rows, bk, :], ACT.Copy).then_inc(S("tr_ev"), 1)
                act.wait_ge(S("pv_mm"), j + 1)
                if kind == "prompt":
                    hh, hp = a // 2, a % 2
                    r = slice(64 * hp, 64 * hp + 64)
                    act.activation(O[r, 4 * hh:4 * hh + 4, P * qt:P * qt + P], PS[r, 7, :].rearrange("p (g q) -> p g q", g=GQA),
                                   ACT.Copy).then_inc(S("o_ev"), 1)
                else:
                    for hp in range(2):
                        r = slice(64 * hp, 64 * hp + 64)
                        o = O[r, :, SEQ + DS * a:SEQ + DS * a + DS].rearrange("p (e g) q -> p e g q", e=2)
                        i = PS[r, 7, 0:P].rearrange("p (e f g q) -> p e f g q", e=2, f=2, g=GQA)[:, :, hp]
                        act.activation(o, i, ACT.Copy).then_inc(S("o_ev"), 1)
            tiles_out("o", wk, KT, "o_ev2")
            squares(6, wk, "o_ev2", KT)
            root(6)
            squares(7, x, "x_done2", KT + 1)
            root(7)
            modulated(7, 72)
            ffn(1)
            squares(8, wk, "down1_ev", KT)
            root(8)

        @block.gpsimd
        def _(pool):
            pool.memset(eps, EPS).then_inc(S("eps"), 1)
            pool.memset(BX, 0.0).then_inc(S("zeroed"), 1)
            pool.memset(CX, 0.0).then_inc(S("zeroed"), 1)
            pool.wait_ge(S("trig"), 2)
            pool.wait_ge(S("mag"), 1)
            pool.wait_ge(S("hs"), 1)
            pool.wait_ge(S("scaled"), KT)
            run = C["scan_run"]
            n_tab = [0]

            def tab(ins):
                n_tab[0] += 1
                ins.then_inc(S("pool_chain"), 1)
                pool.wait_ge(S("pool_chain"), n_tab[0])

            for u in range(units):
                s = u % 2
                if u >= 2:
                    pool.wait_ge(S("s_ready"), u - 1)

                def fine(e):
                    return E[:, e, 2 * u:2 * u + 2, 0:16].unsqueeze(2).broadcast_to([P, 2, 16, 16])

                def coarse(e):
                    return E[:, e, 2 * u:2 * u + 2, 16:32].unsqueeze(3).broadcast_to([P, 2, 16, 16])

                def grid(v):
                    return v.rearrange("p (i a b) -> p i a b", i=2, a=16)

                for tabl, (x1, x2), (y1, y2), op in ((TC, (0, 0), (1, 1), ALU.subtract), (TS, (1, 0), (0, 1), ALU.add)):
                    pool.tensor_tensor(grid(pt1), fine(x1), coarse(x2), ALU.mult).then_inc(S("pool_chain"), 1)
                    pool.tensor_tensor(grid(pt2), fine(y1), coarse(y2), ALU.mult).then_inc(S("pool_chain"), 1)
                    n_tab[0] += 2
                    pool.wait_ge(S("pool_chain"), n_tab[0])
                    tab(pool.tensor_tensor(tabl[:, s, :, 0:SEQ], pt1.rearrange("p (i t) -> p i t", i=2),
                                           pt2.rearrange("p (i t) -> p i t", i=2), op))
                    pool.tensor_copy(tabl[:, s, :, SEQ:T].rearrange("p i (b t) -> p i b t", b=DB),
                                     tabl[:, s, :, 0:DS].unsqueeze(2).broadcast_to([P, 2, DB, DS])).then_inc(S("tables"), 1)
                if u >= 1:
                    pool.wait_ge(S("scanned"), u)
                pool.tensor_tensor(decay4, run.unsqueeze(1).unsqueeze(1).broadcast_to([P, 2, 2, T]),
                                   pr["mag"][:, 2 * u:2 * u + 2].unsqueeze(2).unsqueeze(3).broadcast_to([P, 2, 2, T]),
                                   ALU.mult).then_inc(S("decay"), 1)

            def ffn(l):
                for s in range(3):
                    pool.memset(XE[:, s, :, 0:2], 0.0).then_inc(S(f"ext_zero{l}"), 1)
                pool.wait_ge(S("prefix_in"), 16 * (l + 1))
                if l == 1:
                    pool.wait_ge(S("out_conv"), 16)
                for j in range(FT):
                    e = XE[:, j % 3]
                    rows = e[:, :, 2 + SEQ:].rearrange("p a (b r) -> p a b r", b=DB)
                    if j >= 3:
                        pool.wait_ge(S(f"conv2_{l}"), 2 * (j - 2))
                    pool.tensor_copy(rows[:, :, :, 0:2], prefix[:, j]).then_inc(S(f"prefixed{l}"), 1)
                    pool.wait_ge(S(f"up_ev{l}"), 2 * j + 2)
                    pool.tensor_copy(conv_rows[:, j, :, 0, :], e[:, :, SEQ:SEQ + 2]).then_inc(S(f"conv_rows{l}"), 1)
                    pool.tensor_copy(conv_rows[:, j, :, 1:, :], rows[:, :, :, DS:]).then_inc(S(f"conv_rows{l}"), 1)

            pool.wait_ge(S("x_done0"), KT + 1)
            ffn(0)
            pool.wait_ge(S("x_done1"), KT + 1)
            pool.wait_ge(S("conv_rows0"), 2 * FT)
            pool.memset(QBp.rearrange("p e b n -> p (e b n)"), 0.0).then_inc(S("qb_zero"), 1)
            pool.memset(QBr.rearrange("p e b n -> p (e b n)"), 0.0).then_inc(S("qb_zero"), 1)
            pool.memset(PC, 0.0).then_inc(S("small_zero"), 1)
            pool.memset(drop, 0.0).then_inc(S("small_zero"), 1)
            pool.wait_ge(S("qb_zero"), 2)
            pool.wait_ge(S("small_zero"), 2)

            def spread(dst, src, done):
                for hp in range(2):
                    for hh in range(2):
                        r = slice(64 * hp, 64 * hp + 64)
                        c = 32 * (2 * hh + hp)
                        pool.tensor_copy(dst[r, hh, :, c:c + 32].rearrange("p b (g q) -> p b g q", g=GQA),
                                         src[r, 4 * hh:4 * hh + 4, SEQ:T].rearrange("p g (b q) -> p b g q", b=DB)).then_inc(S(done), 1)
                        pool.wait_ge(S(done), 2 * hp + hh + 1)

            pool.wait_ge(S("q_ev"), KT)
            spread(QBp, Qp, "qbp_done")
            pool.wait_ge(S("roped"), 12)
            spread(QBr, Qr, "qbr_done")
            pool.wait_ge(S("x_done2"), KT + 1)
            ffn(1)

        @block.vector
        def _(dve):
            chain, posted = [0], {}

            def link(ins):
                chain[0] += 1
                ins.then_inc(S("dve_chain"), 1)
                dve.wait_ge(S("dve_chain"), chain[0])

            def post(ins, name, own=True):
                posted[name] = posted.get(name, 0) + 1
                ins.then_inc(S(name), 1)
                if own:
                    dve.wait_ge(S(name), posted[name])

            def tt(out, a, b, op):
                return dve.tensor_tensor(out, a, b, op)

            def squares(r, src):
                post(tt(h[:, 4:8, :], src[:, 4:8, :], src[:, 4:8, :], ALU.mult), "sqv")

            def inverse(r):
                dve.wait_ge(S("root"), nth_norm[r])
                link(dve.reciprocal(rinv, rroot))

            def samples(v):
                return v[:, :, SEQ:T].rearrange("p k (b t) -> p k b t", b=DB)

            def per_sample(tile):
                return mod[:, tile:tile + KT, 1:NB].unsqueeze(3).broadcast_to([P, KT, DB, DS])

            def modulated(r, tile):
                dst = h if r == 0 else wk
                link(tt(dst[:, :, SEQ:T], x[:, :, SEQ:T], rinv[:, SEQ:T].unsqueeze(1).broadcast_to([P, KT, DB * DS]), ALU.mult))
                link(tt(samples(dst), samples(dst), per_sample(tile + 8), ALU.mult))
                post(tt(samples(dst), samples(dst), per_sample(tile), ALU.add), "hs")
                for k in range(KT):
                    post(tt(dst[:, k, 0:SEQ], x[:, k, 0:SEQ], rinv[:, 0:SEQ], ALU.mult), "scaled", own=(k == KT - 1))

            def split(dst, src, k, name):
                link(dve.tensor_copy(dst[:, k, 0, :], src[:, k, :]))
                post(tt(dst[:, k, 1, :], src[:, k, :], dst[:, k, 0, :], ALU.subtract), name, own=False)

            def split_modulated(r):
                for k in range(KT):
                    dve.wait_ge(S("hp"), KT * (nth_mod[r] - 1) + k + 1)
                    split(hb, wk, k, "h_lo")

            made = [0]

            def low_parts(count=1):
                for _ in range(count):
                    p = made[0]
                    made[0] += 1
                    name, half = piece_list[p]
                    n, cols = place[name], P * piece_tiles(name)
                    dve.wait_ge(S(f"ring{n % RING}"), landed[n])
                    if p >= 2:
                        dve.wait_ge(S("lo_used"), p - 1)
                    c = cols * half
                    post(tt(lo[:, p % 2, 0:cols], ring[:, n % RING, c:c + cols], ring_hi[:, n % RING, c:c + cols], ALU.subtract),
                         "lo_ready", own=False)

            def added(r, tile, i):
                for k in range(KT):
                    ins = tt(wk[:, k, :], wk[:, k, :], rinv, ALU.mult)
                    chain[0] += 1
                    ins.then_inc(S("dve_chain"), 1)
                dve.wait_ge(S("dve_chain"), chain[0])
                for k in range(KT):
                    post(dve.scalar_tensor_tensor(out=x[:, k, 0:SEQ], in0=wk[:, k, 0:SEQ], scalar=mod[:, tile + k, 0:1],
                                                  in1=x[:, k, 0:SEQ], op0=ALU.mult, op1=ALU.add), f"x_done{i}", own=False)
                link(tt(samples(wk), samples(wk), per_sample(tile), ALU.mult))
                post(tt(samples(x), samples(x), samples(wk), ALU.add), f"x_done{i}")

            def norm_weights(tile, pre, post_):
                sc_ = mod[:, tile + 8:tile + 16, :]
                link(dve.scalar_tensor_tensor(out=sc_, in0=sc_, scalar=1.0, in1=pre.unsqueeze(2).broadcast_to([P, KT, NB]),
                                              op0=ALU.add, op1=ALU.mult))
                if post_ is not None:
                    g_ = mod[:, tile + 16:tile + 24, :]
                    link(tt(g_, g_, post_.unsqueeze(2).broadcast_to([P, KT, NB]), ALU.mult))

            def ts(out, a, s1, s2, op0, op1=None):
                return dve.tensor_scalar(out, a, s1, s2, op0, op1) if op1 is not None else dve.tensor_scalar(out, a, s1, s2, op0)

            def ffn(l):
                for j in range(FT):
                    low_parts()
                    s = j % 3
                    for k in (1, 2):
                        for a in range(2):
                            m = 2 * j + a
                            dve.wait_ge(S(f"conv{k - 1}_{l}"), 2 * j + a + 1)
                            post(dve.scalar_tensor_tensor(out=CV[:, s, a, :], in0=XE[:, s, a, k:k + CW], scalar=conv_w[:, l, m, k:k + 1],
                                                          in1=CV[:, s, a, :], op0=ALU.mult, op1=ALU.add), f"conv{k}_{l}", own=False)
                    if j >= 1:
                        gated(l, j - 1)
                    if j >= 2:
                        low_of(l, j - 2)
                gated(l, FT - 1)
                low_of(l, FT - 2)
                low_of(l, FT - 1)
                low_parts(16 if l == 0 else 14)

            def gated(l, j):
                s = j % 3
                dve.wait_ge(S(f"sg{l}"), j + 1)
                if j >= 3:
                    dve.wait_ge(S(f"u_lo{l}"), j - 2)
                post(tt(UF[:, s, 0:SEQ], CV[:, s, 0, 0:SEQ], SG[:, s, 0:SEQ], ALU.mult), f"u_mul{l}", own=False)
                post(tt(UF[:, s, SEQ:T].rearrange("p (b t) -> p b t", b=DB), every_ten(CV[:, s, 0, :]), every_ten(SG[:, s, :]), ALU.mult),
                     f"u_mul{l}")

            def low_of(l, j):
                dve.wait_ge(S(f"u_hi{l}"), j + 1)
                post(tt(U[:, j, 1, :], UF[:, j % 3, :], U[:, j, 0, :], ALU.subtract), f"u_lo{l}")

            def every_ten(v):
                return v[:, CW - 10 * DB:CW].rearrange("p (b t) -> p b t", t=DS + 2)[:, :, 2:]

            dve.wait_ge(S("silb"), 1)
            post(tt(silb[:, 1], silc, silb[:, 0], ALU.subtract), "silb", own=False)
            low_parts(2)
            dve.wait_ge(S("params_in"), 64)
            lr, li = lam[:, 0, :], lam[:, 1, :]
            dve.wait_ge(S("dt"), 1)
            post(tt(pr["lrdt"], lr, pr["dt"], ALU.mult), "lrdt")
            link(tt(pr["th"], li, pr["dt"], ALU.mult))
            link(ts(pr["k"], pr["th"], INV_2PI, ROUND, ALU.mult, ALU.add))
            link(ts(pr["k"], pr["k"], ROUND, None, ALU.subtract))
            link(dve.scalar_tensor_tensor(out=pr["thr"], in0=pr["k"], scalar=-TWO_PI_HI, in1=pr["th"], op0=ALU.mult, op1=ALU.add))
            link(dve.scalar_tensor_tensor(out=pr["thr"], in0=pr["k"], scalar=-TWO_PI_LO, in1=pr["thr"], op0=ALU.mult, op1=ALU.add))
            link(ts(pr["phi"], pr["thr"], INV_2PI, None, ALU.mult))
            link(ts(pr["phi_hi"], pr["phi"], ROUND12, ROUND12, ALU.add, ALU.subtract))
            link(tt(pr["phi_lo"], pr["phi"], pr["phi_hi"], ALU.subtract))
            steps = C["steps"].unsqueeze(1).broadcast_to([P, ST, 32])

            def spread(v, n):
                return v.unsqueeze(2).broadcast_to([P, ST, n])

            link(tt(phase_sin, steps, spread(pr["phi_hi"], 32), ALU.mult))
            link(ts(phase_tmp, phase_sin, ROUND, ROUND, ALU.add, ALU.subtract))
            link(tt(phase_sin, phase_sin, phase_tmp, ALU.subtract))
            link(tt(phase_tmp, steps, spread(pr["phi_lo"], 32), ALU.mult))
            link(tt(phase_sin, phase_sin, phase_tmp, ALU.add))
            link(ts(phase_cos, phase_sin, 0.25, None, ALU.add))
            link(ts(phase_tmp, phase_sin, ROUND, ROUND, ALU.add, ALU.subtract))
            post(tt(phase_sin, phase_sin, phase_tmp, ALU.subtract), "phases")
            link(ts(phase_tmp, phase_cos, ROUND, ROUND, ALU.add, ALU.subtract))
            post(tt(phase_cos, phase_cos, phase_tmp, ALU.subtract), "phases")
            dve.wait_ge(S("mag"), 1)
            dve.wait_ge(S("trig"), 2)
            link(tt(pr["a_re"], pr["mag"], E[:, 0, :, 1], ALU.mult))
            link(tt(pr["a_im"], pr["mag"], E[:, 1, :, 1], ALU.mult))
            link(tt(pr["u"], lr, lr, ALU.mult))
            link(tt(pr["v"], li, li, ALU.mult))
            link(tt(pr["den"], pr["u"], pr["v"], ALU.add))
            link(dve.reciprocal(pr["w"], pr["den"]))
            link(tt(pr["zl_re"], lr, pr["w"], ALU.mult))
            link(tt(pr["zl_im"], li, pr["w"], ALU.mult))
            link(ts(pr["q"], pr["a_re"], -1.0, None, ALU.add))
            link(tt(pr["u"], pr["q"], pr["zl_re"], ALU.mult))
            link(tt(pr["v"], pr["a_im"], pr["zl_im"], ALU.mult))
            link(tt(pr["z_re"], pr["u"], pr["v"], ALU.add))
            link(tt(pr["u"], pr["a_im"], pr["zl_re"], ALU.mult))
            link(tt(pr["v"], pr["q"], pr["zl_im"], ALU.mult))
            link(tt(pr["z_im"], pr["u"], pr["v"], ALU.subtract))
            low_parts(10)
            dve.wait_ge(S("bc_in"), 48)
            dve.wait_ge(S("zeroed"), 2)
            m1 = phase_sin.rearrange("p s n -> p (s n)")[:, 0:512].rearrange("p (s c) -> p s c", s=ST)
            m2 = phase_sin.rearrange("p s n -> p (s n)")[:, 512:1024].rearrange("p (s c) -> p s c", s=ST)
            zr, zi = spread(pr["z_re"], 16), spread(pr["z_im"], 16)
            for e in range(2):
                link(tt(m1, braw[:, e], zr, ALU.mult))
                link(tt(m2, braw[:, 1 - e], zi, ALU.mult))
                for gl in range(2):
                    r = slice(64 * gl, 64 * gl + 64)
                    ins = tt(BX[r, e, :, 16 * gl:16 * gl + 16], m1[r], m2[r], ALU.subtract if e == 0 else ALU.add)
                    post(ins, "bx_done")
            for e in range(2):
                for gl in range(2):
                    r = slice(64 * gl, 64 * gl + 64)
                    ins = ts(CX[r, e, :, 16 * gl:16 * gl + 16], craw[r, e], -1.0 if e else 1.0, None, ALU.mult)
                    link(ins)
            p1 = phase_cos.rearrange("p s n -> p (s n)")[:, 0:256].rearrange("p (s b) -> p s b", s=ST)
            p2 = phase_cos.rearrange("p s n -> p (s n)")[:, 256:512].rearrange("p (s b) -> p s b", s=ST)
            ar, ai = spread(pr["a_re"], DB), spread(pr["a_im"], DB)
            for e in range(2):
                link(tt(p1, h0[:, e], ar, ALU.mult))
                link(tt(p2, h0[:, 1 - e], ai, ALU.mult))
                link(tt(AH[:, e], p1, p2, ALU.subtract if e == 0 else ALU.add))
            post(dve.tensor_copy(rinv[:, 0:1], AH[:, 0, 0, 0:1]), "cx_done")

            dve.wait_ge(S("x_in"), 16)
            squares(0, x)
            dve.wait_ge(S("vec_in"), 16)
            dve.wait_ge(S("mod_ev"), 24)
            g_pre = V["norm_pre"].rearrange("p (s k) -> p s k", s=4)
            g_post = V["norm_post"].rearrange("p (s k) -> p s k", s=4)
            norm_weights(0, g_pre[:, 0], g_post[:, 0])
            inverse(0)
            low_parts(2)
            modulated(0, 0)

            def cosine(s):
                return TC[:, s].unsqueeze(2).broadcast_to([P, 2, 2, T])

            def sine(s):
                return TS[:, s].unsqueeze(2).broadcast_to([P, 2, 2, T])

            def y_read(f):
                dve.wait_ge(S("y_mm"), 2 * f + 2)
                post(dve.scalar_tensor_tensor(out=h[:, f, :], in0=h[:, f, :], scalar=V["ssm_d"][:, f:f + 1], in1=PS[:, 4, 0:T],
                                              op0=ALU.mult, op1=ALU.add), "y_read")

            for u in range(units):
                s = u % 2
                v = VS[s]
                dve.wait_ge(S("u_mm"), u + 1)
                dve.wait_ge(S("tables"), 2 * u + 2)
                raw = PS[:, 0:4, 0:T].rearrange("p (i e) t -> p i e t", i=2)
                post(tt(t1, raw, cosine(s), ALU.mult), "u_read", own=False)
                post(tt(t2, raw, sine(s), ALU.mult), "u_read")
                if u >= 2:
                    dve.wait_ge(S("y_mm"), u - 1)
                    dve.wait_ge(S("last_states"), 2 * (u - 1))
                link(tt(v[:, :, 0, :], t1[:, :, 0, :], t2[:, :, 1, :], ALU.add))
                link(tt(v[:, :, 1, :], t1[:, :, 1, :], t2[:, :, 0, :], ALU.subtract))
                first = v[:, :, :, SEQ::DS]
                link(tt(first, first, AH[:, :, 2 * u:2 * u + 2, :].rearrange("p e i b -> p i e b"), ALU.add))
                dve.wait_ge(S("decay"), u + 1)
                post(dve.tensor_tensor_scan(zf, decay, VSf[s], 0.0, ALU.mult, ALU.add), "scanned")
                link(tt(t1, z, cosine(s), ALU.mult))
                link(tt(t2, z, sine(s), ALU.mult))
                link(tt(v[:, :, 0, :], t1[:, :, 0, :], t2[:, :, 1, :], ALU.subtract))
                post(tt(v[:, :, 1, :], t1[:, :, 1, :], t2[:, :, 0, :], ALU.add), "s_ready")
                if u >= 2 and u % 2 == 0:
                    y_read((u - 2) // 2)
                low_parts(2 * len(mod_of_unit[u][1:]))
                if u + 1 < units:
                    low_parts(2)
            low_parts(2)
            y_read(7)
            dve.wait_ge(S("mod_ev"), 112)
            for i, tile in ((1, 24), (2, 48), (3, 72)):
                norm_weights(tile, g_pre[:, i], g_post[:, i])
            norm_weights(96, V["norm_kv"], None)

            for k in range(KT):
                dve.wait_ge(S("g_ready"), k + 1)
                split(gb, h, k, "g_lo")
            for m in range(KT):
                if m in (2, 4, 6, 7):
                    low_parts()
                dve.wait_ge(S("glu_ev"), m + 1)
                post(tt(wk[:, m, :], h[:, m, :], sig[:, m % 2, :], ALU.mult), "wk_done", own=(m == KT - 1))
            squares(1, wk)
            inverse(1)
            dve.wait_ge(S("x_in"), 32)
            added(1, 16, 0)
            squares(2, x)
            inverse(2)
            modulated(2, 24)
            split_modulated(2)
            ffn(0)
            dve.wait_ge(S("down0_ev"), KT)
            squares(3, wk)
            inverse(3)
            added(3, 40, 1)
            squares(4, x)
            inverse(4)
            modulated(4, 96)
            split_modulated(4)
            low_parts(4)

            def rope(i, src, dst):
                dve.wait_ge(S("rope_mm"), i + 1)
                post(tt(rt1, PS[:, 4 + i % 2, 0:T], C["sin"], ALU.mult), "rope_read")
                link(tt(dst, src, C["cos"], ALU.mult))
                post(tt(dst, dst, rt1, ALU.add), "roped")

            for i, m in enumerate((4, 5, 8, 9)):
                rope(i, KV[:, m, :], KV[:, m, :])
            dve.wait_ge(S("kv_mm"), 12)
            modulated(5, 48)
            split_modulated(5)
            low_parts(4)
            for m in range(KT):
                dve.wait_ge(S("q_ev"), m + 1)
                rope(4 + m, Qp[:, m, :], Qr[:, m, :])
            dve.wait_ge(S("spread_mm"), 1)
            pick = C["gate_pick"].unsqueeze(1).broadcast_to([P, 3 * DB, DS])
            link(tt(gx.rearrange("p c (b t) -> p (c b) t", b=DB), PS[:, 6, 0:192].rearrange("p (n t) -> p n t", t=DS), pick, ALU.mult))
            link(dve.tensor_reduce(gs.rearrange("p c b -> p (c b)"), gx.rearrange("p c (b t) -> p (c b) t", b=DB), AX, ALU.add))

            def by(v, n):
                return v.unsqueeze(2).broadcast_to([P, DB, n])

            pcv = PC[:, :, 0:NC]
            dve.wait_ge(S("c_mm"), 1)
            dve.wait_ge(S("small_zero"), 2)
            cpsum = PS[:, 0, 0:DB * NC].rearrange("p (b n) -> p b n", b=DB)
            link(dve.tensor_reduce(cmax, cpsum, AX, ALU.max))
            post(tt(pcv, cpsum, by(cmax, NC), ALU.subtract), "c_shift")
            dve.wait_ge(S("c_exp"), 1)
            link(dve.tensor_reduce(cs, pcv, AX, ALU.add))
            link(dve.reciprocal(cr, cs))
            link(tt(pcv, pcv, by(cr, NC), ALU.mult))
            link(tt(imp, PC[:, :, 4:57:4], PC[:, :, 5:58:4], ALU.add))
            link(tt(imp, imp, PC[:, :, 6:59:4], ALU.add))
            link(tt(imp2, PC[:, :, 3:56:4], PC[:, :, 7:60:4], ALU.add))
            post(dve.scalar_tensor_tensor(out=imp, in0=imp, scalar=2.0, in1=imp2, op0=ALU.mult, op1=ALU.add), "imp_ready")
            dve.wait_ge(S("imp_mm"), 1)
            total = PS[:, 1, 0:DB * NFREE].rearrange("p (b n) -> p b n", b=DB)
            blocks = C["blocks"].unsqueeze(1).broadcast_to([P, DB, NFREE])
            link(dve.tensor_reduce(imin, total, AX, ALU.min))
            link(tt(imp2, total, by(imin, NFREE), ALU.is_le))
            link(tt(imp2, imp2, blocks, ALU.mult))
            link(dve.tensor_reduce(imax, imp2, AX, ALU.max))
            link(tt(imp2, blocks, by(imax, NFREE), ALU.is_equal))
            post(ts(drop[:, :, 1:1 + NFREE], imp2, NEG, None, ALU.mult), "drop_done")
            link(tt(pcv, pcv, by(gs[:, 0, :], NC), ALU.mult))

            for j, (kind, a, qt) in enumerate(jobs):
                sc, s = SC[j % 2], j % 2
                dve.wait_ge(S("s_mm"), j + 1)
                if j >= 1:
                    dve.wait_ge(S("tr_mm"), groups_before[j - 1])
                if j >= 2:
                    dve.wait_ge(S("exp"), before(NX, j - 1))
                if kind == "prompt":
                    K = P * (qt + 1)
                    views = [sc[:, base:base + GQA * n].rearrange("p (g k) -> p g k", g=GQA) for base, n in ((2048, NCP), (0, K), (1024, K))]
                    mask = C["causal"][:, 2 * P - K:2 * P].unsqueeze(1).broadcast_to([P, GQA, K])
                    for br in (1, 2):
                        src = PS[:, 2 * br - 2:2 * br, :].rearrange("p c n -> p (c n)")[:, 0:GQA * K].rearrange("p (g k) -> p g k", g=GQA)
                        post(tt(views[br], src, mask, ALU.add), "s_evd")
                    neg = C["cmp_neg"][:, NCP * qt:NCP * qt + NCP].unsqueeze(1).broadcast_to([P, GQA, NCP])
                    post(tt(views[0], PS[:, 4, 0:GQA * NCP].rearrange("p (g k) -> p g k", g=GQA), neg, ALU.add), "s_evd")
                    for br in (0, 1):
                        link(dve.tensor_reduce(nmax[:, s, 4 * br:4 * br + 4], views[br], AX, ALU.max, negate=True))
                    post(dve.tensor_reduce(nmax[:, s, 8:12], views[2], AX, ALU.max, negate=True), "nmax")
                    n = 12
                    gate = gp[:, qt, :].rearrange("p (c m) -> p c m", c=3)[:, :, 4 * a:4 * a + 4]
                    fv = fac[:, s, :].rearrange("p (c g) -> p c g", c=3)
                else:
                    post(tt(sc[:, 0:1024].rearrange("p (n k) -> p n k", n=16), PS[:, 0:2, :].rearrange("p c n -> p (c n)").rearrange("p (n k) -> p n k", n=16),
                            drop[:, a, :].unsqueeze(2).broadcast_to([P, 16, 64]), ALU.add), "s_evd", own=False)
                    post(tt(sc[:, 1024:1032], PS[:, 3, 0:DS], C["new_mask"], ALU.add), "s_evd", own=False)
                    post(tt(sc[:, 1032:1040], PS[:, 2, 0:DS], C["win_mask"], ALU.add), "s_evd")
                    post(dve.tensor_copy(sc[:, 1040:1544], PS[:, 2, DS:512]), "s_evd", own=False)
                    post(tt(sc[:, 1544:1552], PS[:, 3, DS:2 * DS], C["new_mask"], ALU.add), "s_evd")
                    link(dve.tensor_reduce(nmax[:, s, 0:1], sc[:, 0:1032], AX, ALU.max, negate=True))
                    post(dve.tensor_reduce(nmax[:, s, 1:2], sc[:, 1032:1552], AX, ALU.max, negate=True), "nmax")
                    n = 2
                    gate = gs[:, 1:3, a]
                    fv = fac[:, s, 0:2]
                dve.wait_ge(S("exp"), before(NX, j + 1))
                link(dve.reciprocal(fac[:, s, 0:n], ssum[:, s, 0:n]))
                post(tt(fv, fv, gate, ALU.mult), "fac")
                if kind == "prompt":
                    f0 = fac[:, s, 0:4].unsqueeze(2).broadcast_to([P, GQA, NCP])
                    link(tt(views[0], views[0], f0, ALU.mult))
                    valid = C["cmp_valid"][:, NCP * qt:NCP * qt + NCP].unsqueeze(1).broadcast_to([P, GQA, NCP])
                    post(tt(views[0], views[0], valid, ALU.mult), "p_ready")
                    for br in (1, 2):
                        for g in range(GQA):
                            i = 4 * br + g
                            post(ts(views[br][:, g, :], views[br][:, g, :], fac[:, s, i:i + 1], None, ALU.mult), "p_ready", own=False)
                else:
                    post(ts(sc[:, 0:1032], sc[:, 0:1032], fac[:, s, 0:1], None, ALU.mult), "p_ready", own=False)
                    post(ts(sc[:, 1032:1552], sc[:, 1032:1552], fac[:, s, 1:2], None, ALU.mult), "p_ready", own=False)
            low_parts(2)
            dve.wait_ge(S("o_ev"), before(NOE, len(jobs)))
            dve.wait_ge(S("pv_mm"), len(jobs))
            for k in range(KT):
                split(ob, O, k, "o_lo")
            low_parts(4)
            dve.wait_ge(S("o_ev2"), KT)
            squares(6, wk)
            inverse(6)
            added(6, 64, 2)
            squares(7, x)
            inverse(7)
            modulated(7, 72)
            split_modulated(7)
            ffn(1)
            dve.wait_ge(S("down1_ev"), KT)
            squares(8, wk)
            inverse(8)
            added(8, 88, 3)

def _weight_chunks(w, group):
    K, M = w.shape
    kt, mt = K // P, M // P
    return w.reshape(kt, P, mt // group, group, P).transpose(2, 1, 3, 0, 4).reshape(mt // group, P, group * kt * P)


def _features(v):
    t = v.reshape(*v.shape[:-1], v.shape[-1] // P, P)
    return t.transpose(t.ndim - 1, *range(t.ndim - 1)).reshape(P, -1)


def _constants():
    import numpy as np

    f = np.float32
    tab = {}
    tab["ident"] = np.eye(P, dtype=f)
    tab["ones"] = np.ones((P, P), f)
    half = HD // 2
    rot = np.zeros((P, P), f)
    for base in (0, HD):
        for m in range(half):
            rot[base + m + half, base + m] = -1.0
            rot[base + m, base + m + half] = 1.0
    tab["rot"] = rot
    r = np.arange(P)
    same_head = r[:, None] // (GQA * DS) == r[None, :] // (GQA * DS)
    tab["group_sum"] = (same_head & (r[:, None] % DS == r[None, :] % DS)).astype(f)
    spread = np.zeros((P, 3, P), f)
    for br in range(3):
        for h in range(NH):
            spread[br * NH + h, br, h * DS:(h + 1) * DS] = 1.0
    tab["gate_spread"] = spread.reshape(P, -1)
    pos = np.concatenate([np.arange(SEQ)] + [PAST + np.arange(DS)] * DB).astype(f)
    freqs = (f(10000.0) ** (-np.arange(half, dtype=f) / f(half))).astype(f)
    ang = (pos[None, :] * freqs[np.arange(P) % half][:, None]).astype(f)
    tab["cos"] = np.cos(ang).astype(f)
    tab["sin"] = np.sin(ang).astype(f)
    k = np.arange(P)
    tab["causal"] = np.concatenate([np.zeros((P, P), f), np.where(k[None, :] <= r[:, None], 0.0, NEG).astype(f)], 1)
    j = np.arange(DS)
    q = (r % DS)[:, None]
    tab["new_mask"] = np.where(j[None, :] <= q, 0.0, NEG).astype(f)
    tab["win_mask"] = np.where(j[None, :] > q, 0.0, NEG).astype(f)
    tab["gate_pick"] = (j[None, :] == q).astype(f)
    ends = np.arange(NCP) * 16 + 31
    valid = np.stack([ends[None, :] <= (r[:, None] + qt * P) for qt in range(2)], 1)
    tab["cmp_valid"] = valid.astype(f).reshape(P, -1)
    tab["cmp_neg"] = np.where(valid, 0.0, NEG).astype(f).reshape(P, -1)
    tab["blocks"] = np.broadcast_to(np.arange(1, NFREE + 1, dtype=f), (P, NFREE))
    run = np.ones(T, f)
    run[0] = 0.0
    run[SEQ::DS] = 0.0
    tab["scan_run"] = np.broadcast_to(run, (P, T))
    tab["steps"] = np.broadcast_to(np.concatenate([np.arange(16), 16 * np.arange(16)]).astype(f), (P, 32))
    assert {n: t.shape[1] for n, t in tab.items()} == dict(CONST)
    return np.concatenate([tab[n] for n, _ in CONST], 1).astype(f)


def _lay_out(i):
    import numpy as np

    i = {n: np.asarray(a) for n, a in i.items()}
    d = {"consts": _constants()}
    tokens = np.concatenate([i["x_prompt"].reshape(SEQ, D), i["x_sample"].reshape(DB * DS, D)], 0)
    d["x"] = _features(tokens).reshape(P, T, KT).transpose(0, 2, 1)
    d["c"] = _features(np.concatenate([i["c_prompt"], i["c_sample"]], 0)).reshape(P, NB, KT).transpose(0, 2, 1)
    d["page_table"] = i["page_table"].reshape(1, DB * NPG)
    pool = i["cache_nsa_paged"]
    n_phys = pool.shape[0]
    d["pool_cmp"] = pool[:, :, 0:2].reshape(n_phys, 64, 2, 2, KVH, HD).transpose(3, 0, 2, 5, 4, 1).reshape(2, n_phys, P, KVH * 64)
    d["pool_k"] = pool[:, :, 2].reshape(n_phys, PAGE, 2, 2, HD).transpose(0, 3, 4, 2, 1).reshape(n_phys, P, 2 * PAGE)
    d["pool_v"] = pool[:, :, 3].reshape(n_phys, PAGE, KVH * HD)
    win = i["cache_nsa_window"]
    d["win_k"] = win[:, :, 0].reshape(DB, WIN, 2, 2, HD).transpose(0, 3, 4, 2, 1).reshape(DB, P, 2 * WIN)
    d["win_v"] = win[:, :, 1].reshape(DB, WIN // P, P, KVH * HD).transpose(0, 2, 1, 3).reshape(DB, P, -1)
    def states(a):
        return a.reshape(ST, P).T

    d["lam"] = np.stack([states(i["ssm_lam_re"]), states(i["ssm_lam_im"])], 1).reshape(P, 2 * ST)
    d["log_dt"] = i["ssm_log_dt"].reshape(ST, 2).T.reshape(2, 1, ST)
    h0 = np.stack([i["state_ssm_re"], i["state_ssm_im"]], 0).reshape(2, DB, ST, P)
    d["ssm_h0"] = h0.transpose(3, 0, 2, 1).reshape(P, -1)
    b = np.stack([i["ssm_b_re"], i["ssm_b_im"]], 0).reshape(2, ST, P, 16)
    d["ssm_b"] = b.transpose(2, 0, 1, 3).reshape(P, -1)
    c = np.stack([i["ssm_c_re"], i["ssm_c_im"]], 0).reshape(2, ST, 2, 16, HD)
    d["ssm_c"] = c.transpose(2, 4, 0, 1, 3).reshape(P, -1)
    def pairs(a):
        return a.reshape(*a.shape[:-1], 2, FT, P).swapaxes(-2, -3).reshape(a.shape)

    conv_w = _features(pairs(i["ffn_conv_w"])).reshape(P, 2, 3, 2 * FT).transpose(0, 1, 3, 2)
    conv_b = _features(pairs(i["ffn_conv_b"]))
    pre = _features(pairs(i["state_ffn_conv"])).reshape(P, 2, 16, 2 * FT).transpose(0, 1, 3, 2)
    d["prefix"] = pre.reshape(P, 2, -1).transpose(1, 0, 2)
    pe = i["cmp_pe"].reshape(2, 16, 2, HD).transpose(2, 3, 0, 1).reshape(P, 32)
    vec = {
        "norm_pre": _features(i["norm_pre"]), "norm_post": _features(i["norm_post"]), "norm_kv": _features(i["norm_kv"]),
        "b_mod": np.concatenate([_features(i["b_mod"]), _features(i["b_mod_kv"])], 1), "ssm_d": _features(i["ssm_d"]),
        "b_glu": _features(i["b_glu"]), "conv_w": conv_w.reshape(P, -1), "conv_b": conv_b, "cmp_pe": pe,
        "cmp_b1": i["cmp_b1"].T, "cmp_w2": i["cmp_w2"].transpose(1, 0, 2).reshape(P, -1),
    }
    assert {n: t.shape[1] for n, t in vec.items()} == dict(VEC), {n: t.shape[1] for n, t in vec.items()}
    d["vec"] = np.concatenate([vec[n] for n, _ in VEC], 1)
    wm = i["w_mod"].reshape(4, D, 3 * D)
    d["w_mod"] = np.concatenate([_weight_chunks(wm[s], 4) for s in range(4)], 0)
    d["w_mod_kv"] = _weight_chunks(i["w_mod_kv"], 4)
    d["w_glu"] = _weight_chunks(i["w_glu"][0], 4)
    d["w_kv"] = _weight_chunks(i["w_kv"], 4)
    wq = i["w_qg"][0][:, :D].reshape(D, 2, 2, GQA, HD).transpose(0, 1, 3, 2, 4).reshape(D, D)
    d["w_q"] = _weight_chunks(wq, 4)
    d["w_gate"] = i["w_qg"][0][:, D:].reshape(KT, P, 3 * NH).transpose(1, 0, 2).reshape(P, -1)
    wo = i["w_o"][0].reshape(2, 2, GQA, HD, D).transpose(0, 2, 1, 3, 4).reshape(D, D)
    d["w_o"] = _weight_chunks(wo, 4)
    d["cmp_w1"] = i["cmp_w1"].reshape(2, 16, P, P).transpose(0, 2, 1, 3).reshape(2, P, 16 * P)
    up = pairs(i["ffn_w_up"])
    d["w_up"] = np.concatenate([_weight_chunks(up[l], 4) for l in range(2)], 0)
    d["w_down"] = np.concatenate([_weight_chunks(i["ffn_w_down"][l], 1) for l in range(2)], 0)
    return {n: np.ascontiguousarray(a) for n, a in d.items()}


def _rows(o):
    r = o.transpose(2, 1, 0).reshape(T, -1)
    return r[:SEQ], r[SEQ:]


def _returned(o):
    import numpy as np

    y_p, y_s = _rows(o["out_y"])
    kv_p, kv_s = (r.reshape(-1, 6, KVH, HD) for r in _rows(o["out_kv"]))
    ssm = o["out_ssm"].reshape(P, ST, 2, NB).transpose(2, 3, 1, 0).reshape(2, NB, 64, 64)
    conv = o["out_conv"].reshape(2, P, FT, 2, NB, 2).transpose(0, 4, 5, 3, 2, 1).reshape(2, NB, 2, 2 * FT * P)
    out = (
        y_p.reshape(1, SEQ, D), y_s.reshape(DB, DS, D),
        kv_p[:, :4].reshape(1, SEQ, 4, KVH, HD), kv_s[:, :4].reshape(DB, DS, 4, KVH, HD),
        kv_p[:, 4:].reshape(1, SEQ, 2, KVH, HD), kv_s[:, 4:].reshape(DB, DS, 2, KVH, HD),
        ssm[0, :1][None], ssm[1, :1][None], ssm[0, 1:][None], ssm[1, 1:][None],
        conv[:, :1], conv[:, 1:],
    )
    return tuple(np.ascontiguousarray(a) for a in out)


_OUTS = {"out_y": (P, KT, T), "out_kv": (P, 12, T), "out_ssm": (P, ST * 2 * NB), "out_conv": (2, P, 2 * FT * 2 * NB)}


def kernel(**inputs):
    import concourse.bacc as _bacc
    from concourse import mybir as _mybir
    from concourse.bass_utils import run_bass_kernel_spmd as _run

    nc = _bacc.Bacc("TRN2", target_bir_lowering=False, num_devices=1)
    arrays = _lay_out(inputs)
    dram = {n: nc.dram_tensor(n, a.shape, _mybir.dt.from_np(a.dtype), kind="ExternalInput").ap() for n, a in arrays.items()}
    for n, shape in _OUTS.items():
        dram[n] = nc.dram_tensor(n, shape, _mybir.dt.float32, kind="ExternalOutput").ap()
    build_step(nc, dram)
    r = _run(nc, [arrays], core_ids=[0])
    return _returned(r.results[0])
```

```python
from contextlib import ExitStack

import concourse.bass as bass
from concourse import mybir

P = 128
D, SEQ, DB, DS, PAST, PAGE = 1024, 256, 8, 8, 1024, 128
NH, KVH, GQA, HD = 16, 4, 4, 64
T = SEQ + DB * DS
NB = 1 + DB
KT = D // P
ST = 32
FT = 22
NPG = PAST // PAGE
WIN = 512
NC, NCP = 63, 15
NFREE = 14
NEG = -1e30
EPS = 1e-6
EXT = 2 + SEQ + DB * (DS + 2)
CW = EXT - 2
NPJ = KVH * 2
NMOD0 = 4
SPLIT, PIECE = 3, 8
RING = 3
SLOT = 4096
ROUND = 12582912.0
ROUND12 = 3072.0
INV_2PI = 0.15915494309189535
TWO_PI_HI, TWO_PI_LO = 6.28125, 0.0019353071795864769
TWO_PI_IN = 6.283185

CONST = [("ident", P), ("ones", P), ("rot", P), ("group_sum", P), ("gate_spread", 3 * P), ("cos", T), ("sin", T),
         ("causal", 2 * P), ("new_mask", DS), ("win_mask", DS), ("gate_pick", DS), ("cmp_valid", 2 * NCP),
         ("cmp_neg", 2 * NCP), ("blocks", NFREE), ("scan_run", T), ("steps", 32)]
VEC = [("norm_pre", 32), ("norm_post", 32), ("norm_kv", 8), ("b_mod", 112), ("ssm_d", 8), ("b_glu", 8),
       ("conv_w", 264), ("conv_b", 88), ("cmp_pe", 32), ("cmp_b1", 2), ("cmp_w2", 128)]


def build_step(nc, dram):
    F32 = mybir.dt.float32
    BF16 = mybir.dt.bfloat16
    F32R = mybir.dt.float32r
    I32 = mybir.dt.int32
    ALU = mybir.AluOpType
    ACT = mybir.ActivationFunctionType
    AX = mybir.AxisListType.X
    ctx = ExitStack()
    with ctx:
        sems = {}

        def S(name):
            if name not in sems:
                sems[name] = ctx.enter_context(nc.semaphore(name))
            return sems[name]

        def sb(name, cols, dt=F32, rows=P):
            return ctx.enter_context(nc.sbuf_tensor(name, [rows, cols], dt))

        consts = sb("consts_sb", sum(n for _, n in CONST))
        vec = sb("vec_sb", sum(n for _, n in VEC))
        x_sb = sb("x_sb", KT * T)
        N_H, N_WR, AR = KT * T, SPLIT * PIECE * P, 17852
        with nc.sbuf_tensor("space", [P, AR + N_H + N_WR], F32) as space:
            pass
        rounded = ctx.enter_context(nc.sbuf_tensor("space_rounded", [P, AR + N_H + N_WR], F32R))
        h_sb, wr_sb = space[:, AR:AR + N_H], space[:, AR + N_H:]
        x = x_sb[:, :].rearrange("p (k t) -> p k t", t=T)
        h = h_sb.rearrange("p (k t) -> p k t", t=T)

        def low(v, n):
            return v.bitcast(BF16).rearrange("p (k t) -> p k t", k=n)

        def halves(v, n):
            return v.bitcast(BF16).rearrange("p (k t e) -> p k t e", k=n, e=2)[:, :, :, 1]

        def parts(v, v_low, n):
            return v.rearrange("p (k t) -> p k t", k=n), halves(v, n), low(v_low, n)
        wk = sb("wk_sb", KT * T)[:, :].rearrange("p (k t) -> p k t", t=T)
        ring = sb("ring", RING * SLOT)[:, :].rearrange("p (s n) -> p s n", n=SLOT)
        ring_hi = ring.rearrange("p s n -> p (s n)").bitcast(BF16).rearrange("p (s n e) -> p s n e", s=RING, e=2)[:, :, :, 1]
        wr = rounded[:, AR + N_H:].rearrange("p (s n) -> p s n", s=SPLIT)
        lo = sb("lo", SPLIT * PIECE * P // 2)[:, :].bitcast(BF16).rearrange("p (s n) -> p s n", s=SPLIT)
        mod = sb("mod", 112 * NB)[:, :].rearrange("p (m b) -> p m b", b=NB)
        silc_sb = sb("silc", 2 * KT * NB)
        silc = silc_sb[:, 0:KT * NB].rearrange("p (k b) -> p k b", b=NB)
        silb = silc_sb[:, KT * NB:].bitcast(BF16).rearrange("p (e k b) -> p e k b", e=2, b=NB)
        rinv = sb("rinv", T)[:, :]
        rroot = sb("rroot", T)[:, :]
        kcT = sb("kcT", NB * 2 * NC)[:, :].rearrange("p (b e n) -> p b e n", b=NB, e=2)
        vc = sb("vc", NB * 256)[:, :].rearrange("p (b n) -> p b n", b=NB)
        cmp_bias = sb("cmp_bias", 2)[:, :]
        eps = sb("eps", 1)[:, :]
        conv_rows = sb("conv_rows", 2 * FT * 2 * NB)[:, :].rearrange("p (j a b r) -> p j a b r", a=2, b=NB, r=2)
        pages = sb("pages", DB * NPG, I32, rows=1)
        prefix = sb("prefix_sb", 2 * FT * 2 * DB)[:, :].rearrange("p (j a b r) -> p j a b r", a=2, b=DB, r=2)
        arena = space[:, 0:AR]
        PS = ctx.enter_context(nc.psum_tensor("PS", [P, 8, 512], F32))

        def bank(i):
            return PS[:, i, :]

        def table(t, cols):
            out, at = {}, 0
            for n, c in cols:
                out[n] = t[:, at:at + c]
                at += c
            return out

        C = table(consts, CONST)
        V = table(vec, VEC)
        ident = C["ident"]
        b_mod = V["b_mod"]
        conv_w = V["conv_w"].rearrange("p (l m k) -> p l m k", l=2, k=3)
        conv_b = V["conv_b"].rearrange("p (l m) -> p l m", l=2)
        pe_ = V["cmp_pe"].rearrange("p (e l) -> p e l", e=2)
        w2 = V["cmp_w2"].rearrange("p (e d) -> p e d", e=2)

        def carver():
            at = [0]

            def carve(cols):
                v = arena[:, at[0]:at[0] + cols]
                at[0] += cols
                assert at[0] <= AR, at[0]
                return v
            carve.at = at
            return carve

        def in_rounded(at, cols):
            return rounded[:, at:at + cols]

        carve = carver()
        BT = carve(2 * 8 * P).rearrange("p (e f n) -> p e f n", e=2, f=8)
        CX = carve(2 * ST * 32).rearrange("p (e s n) -> p e s n", e=2, s=ST)
        w1 = carve(2048).rearrange("p (l n) -> p l n", n=P)
        XT = carve(2 * 2048).rearrange("p (s h n) -> p s h n", s=2, h=KVH)
        HG = carve(2 * KVH * NC).rearrange("p (s h n) -> p s h n", s=2, h=KVH)
        E = wr_sb[:, 0:2 * ST * 32].rearrange("p (e s n) -> p e s n", e=2, s=ST)
        AH = carve(2 * ST * DB).rearrange("p (e s b) -> p e s b", e=2, s=ST)
        FS = carve(ST * 2 * NB).rearrange("p (s e b) -> p s e b", s=ST, e=2)
        SP_ = carve(24 * ST).rearrange("p (i s) -> p i s", s=ST)
        TC = x_sb[:, 0:4 * T].rearrange("p (s i t) -> p s i t", s=2, i=2)
        TS = x_sb[:, 4 * T:8 * T].rearrange("p (s i t) -> p s i t", s=2, i=2)
        decay = carve(4 * T)
        t12_at = carve.at[0]
        t12 = carve(8 * T)
        gb = parts(in_rounded(t12_at, 8 * T), decay, KT)
        t1f, t2f, zf = t12[:, 0:4 * T], t12[:, 4 * T:], wk[:, 4:8, :].rearrange("p k t -> p (k t)")
        VSf = [carve(4 * T), wk[:, 0:4, :].rearrange("p k t -> p (k t)")]

        def unit(v):
            return v.rearrange("p (i e t) -> p i e t", i=2, e=2)

        decay4, t1, t2, z = unit(decay), unit(t1f), unit(t2f), unit(zf)
        VS = [unit(v) for v in VSf]
        pt1, pt2 = wr_sb[:, 2048:2560], wr_sb[:, 2560:3072]
        braw = XT[:, 0].rearrange("p h n -> p (h n)")[:, 0:1024].rearrange("p (e s c) -> p e s c", e=2, s=ST)
        craw = XT[:, 0].rearrange("p h n -> p (h n)")[:, 1024:2048].rearrange("p (e s c) -> p e s c", e=2, s=ST)
        BX = XT[:, 1].rearrange("p h n -> p (h n)").rearrange("p (e s c) -> p e s c", e=2, s=ST)
        h0 = t2f[:, 0:512].rearrange("p (e s b) -> p e s b", e=2, s=ST)
        phase_sin = wk[:, 0:4, :].rearrange("p k t -> p (k t)")[:, 0:1024].rearrange("p (s n) -> p s n", n=32)
        phase_cos = wk[:, 4:8, :].rearrange("p k t -> p (k t)")[:, 0:1024].rearrange("p (s n) -> p s n", n=32)
        phase_tmp = t1f[:, 0:1024].rearrange("p (s n) -> p s n", n=32)
        sig = VSf[0][:, 0:2 * T].rearrange("p (s t) -> p s t", s=2)
        lam = SP_[:, 0:2, :]
        ldt = SP_[:, 2, :]
        pr = {n: SP_[:, 3 + i, :] for i, n in enumerate((
            "dt", "lrdt", "th", "k", "thr", "phi", "phi_hi", "phi_lo", "mag", "a_re", "a_im", "den", "u", "v", "w", "z_re", "z_im",
            "zl_re", "zl_im", "q"))}

        carve = carver()
        carve(FT * T)
        UF = carve(3 * T).rearrange("p (s t) -> p s t", s=3)
        XE = carve(3 * 2 * EXT).rearrange("p (s a t) -> p s a t", s=3, a=2)
        CV = carve(3 * 2 * CW).rearrange("p (s a t) -> p s a t", s=3, a=2)
        SG = carve(3 * CW).rearrange("p (s t) -> p s t", s=3)
        U = parts(in_rounded(0, FT * T), carve(FT * T // 2), FT)
        hr = rounded[:, AR:AR + N_H]
        hb = parts(hr, carve(KT * T // 2), KT)

        carve = carver()
        KV = carve(12 * T).rearrange("p (m t) -> p m t", t=T)
        qr_at = carve.at[0]
        qr_sb = carve(KT * T)
        Qr = qr_sb.rearrange("p (m t) -> p m t", t=T)
        Qp = wk
        O = h
        QBr = carve(2 * DB * P).rearrange("p (e b n) -> p e b n", e=2, b=DB)
        SC1 = carve(2108)
        QBp = SC1[:, 0:2048].rearrange("p (e b n) -> p e b n", e=2, b=DB)
        VT = carve(2 * 512).rearrange("p (k n) -> p k n", k=2)
        SC0 = carve(2108)
        SC = [SC0, SC1]
        PT = carve(2560)
        hb_kv = parts(hr, PT[:, 640:640 + KT * T // 2], KT)
        ob = parts(in_rounded(qr_at, KT * T), PT[:, 640:640 + KT * T // 2], KT)
        VN = PT[:, 1920:2432]
        small = carve(1390)
        XP = SC0[:, 0:1024].rearrange("p (h n) -> p h n", h=8)
        HP = SC0[:, 1024:1144].rearrange("p (s n) -> p s n", s=2)
        rt1 = PT[:, 0:T]
        PC = small[:, 0:512].rearrange("p (b n) -> p b n", b=DB)
        imp = small[:, 512:624].rearrange("p (b n) -> p b n", b=DB)
        imp2 = small[:, 624:736].rearrange("p (b n) -> p b n", b=DB)
        drop = small[:, 736:864].rearrange("p (b n) -> p b n", b=DB)
        cs = small[:, 872:880]
        cr = small[:, 880:888]
        gs = small[:, 888:912].rearrange("p (c b) -> p c b", c=3)
        gp = small[:, 912:1008].rearrange("p (k n) -> p k n", k=2)
        gf = small[:, 1008:1072]
        gx = small[:, 1072:1264].rearrange("p (c t) -> p c t", c=3)
        nmax = small[:, 1264:1288].rearrange("p (s n) -> p s n", s=2)
        ssum = small[:, 1288:1312].rearrange("p (s n) -> p s n", s=2)
        fac = small[:, 1312:1336].rearrange("p (s n) -> p s n", s=2)
        imin = small[:, 1336:1344]
        imax = small[:, 1344:1352]
        cmax = small[:, 1352:1360]

        stream, place = [], {}

        def add_chunk(name, loads, used_by, used_at):
            place[name] = len(stream)
            stream.append((name, loads, used_by, used_at))

        def whole(src):
            n = src.shape[-1]
            return [(lambda s, n=n: s[:, 0:n], src, None)]

        units = 2 * 8
        for j in range(NMOD0):
            add_chunk(f"mod{j}", whole(dram["w_mod"][j]), "mod_mm", j + 1)
        mod_of_unit = []
        nxt = NMOD0
        for u in range(units):
            n = 2 if u < 28 - NMOD0 - units else 1
            mod_of_unit.append(list(range(nxt, nxt + n)))
            nxt += n
        assert nxt == 28
        mod_src = [dram["w_mod"][j] for j in range(12)] + [dram["w_mod_kv"][j] for j in range(4)] + [dram["w_mod"][12 + j] for j in range(12)]
        mod_bank = [5, 6, 5, 6] + [5] * 24
        mod_tile = [4 * j for j in range(12)] + [96 + 4 * j for j in range(4)] + [48 + 4 * j for j in range(12)]
        for u in range(units):
            for j in mod_of_unit[u]:
                add_chunk(f"mod{j}", whole(mod_src[j]), "mod_mm", j + 1)
        for j in range(2):
            add_chunk(f"glu{j}", whole(dram["w_glu"][j]), "glu_mm", 4 * j + 4)

        def ffn_chunks(l):
            for j in range(11):
                add_chunk(f"up{l}_{j}", whole(dram["w_up"][11 * l + j]), f"up{l}_mm", 2 * j + 2)
            for j in range(8):
                add_chunk(f"down{l}_{j}", whole(dram["w_down"][8 * l + j]), f"down{l}_mm", j + 1)

        ffn_chunks(0)
        for j in range(3):
            add_chunk(f"kv{j}", whole(dram["w_kv"][j]), "kv_mm", 4 * j + 4)
        add_chunk("w1", [(lambda s, e=e: s[:, 2048 * e:2048 * e + 2048], dram["cmp_w1"][e], None) for e in range(2)], "pcmp_mm", 2)
        add_chunk("gate", whole(dram["w_gate"]), "gate_mm", 3)
        for j in range(2):
            add_chunk(f"q{j}", whole(dram["w_q"][j]), "q_mm", 4 * j + 4)

        def k_chunk(b):
            loads = [(lambda s, j=j: s[:, 0:2048].rearrange("p (e n) -> p e n", e=2)[:, :, PAGE * j:PAGE * j + PAGE],
                      "pool_k", NPG * b + j) for j in range(NPG)]
            loads.append((lambda s: s[:, 2048:3072], dram["win_k"][b], None))
            add_chunk(f"k{b}", loads, "s_mm", NPJ + b + 1)

        def v_chunk(b):
            loads = [(lambda s, j=j: s[:, 256 * j:256 * j + 256], "pool_v", NPG * b + j) for j in range(NPG)]
            loads.append((lambda s: s[:, 2048:3072], dram["win_v"][b], None))
            add_chunk(f"v{b}", loads, "pv_mm", NPJ + b + 1)

        k_chunk(0)
        for b in range(DB):
            if b + 1 < DB:
                k_chunk(b + 1)
            v_chunk(b)
        for j in range(2):
            add_chunk(f"o{j}", whole(dram["w_o"][j]), "o_mm", 4 * j + 4)
        ffn_chunks(1)

        landed = []
        slot_count = [0] * RING
        for n, (_, loads, _, _) in enumerate(stream):
            slot_count[n % RING] += 16 * len(loads)
            landed.append(slot_count[n % RING])

        def arrived(eng, name):
            n = place[name]
            eng.wait_ge(S(f"ring{n % RING}"), landed[n])
            return ring[:, n % RING, :]

        jobs = [("prompt", hd, qt) for hd in range(KVH) for qt in range(2)] + [("sample", b, 0) for b in range(DB)]
        NG = [(5 if kind == "sample" else 3 + 2 * qt) for kind, _, qt in jobs]
        NE = [(6 if kind == "sample" else n) for (kind, _, _), n in zip(jobs, NG)]
        groups_before = [sum(NG[:j]) for j in range(len(jobs) + 1)]
        evacs_before = [sum(NE[:j]) for j in range(len(jobs) + 1)]
        NX = [(2 if kind == "sample" else 12) for kind, _, _ in jobs]
        NV = [(5 if kind == "sample" else 3) for kind, _, _ in jobs]
        NPR = [(2 if kind == "sample" else 9) for kind, _, _ in jobs]
        NOE = [(2 if kind == "sample" else 1) for kind, _, _ in jobs]

        def before(counts, j):
            return sum(counts[:j])

        pieces, piece_list = {}, []
        for name, loads, _, _ in stream:
            if name[0:3] in ("mod", "glu") or name[0:2] in ("up", "kv") or name[0] in "qo" or name[0:4] == "down":
                tiles = FT if name[0:4] == "down" else 32
                for first in range(0, tiles, PIECE):
                    pieces[name, first] = len(piece_list)
                    piece_list.append((name, first, min(PIECE, tiles - first)))
        n_mod_pieces = sum(name[0:3] == "mod" for name, _, _ in piece_list)

        nth_norm = {r: n + 1 for n, r in enumerate((0, 1, 2, 3, 4, 6, 7, 8))}
        nth_split = {r: n + 1 for n, r in enumerate((2, 4, 5, 7))}
        nth_mod = {r: n + 1 for n, r in enumerate((0, 2, 4, 5, 7))}
        down_banks = (6, 2, 3, 4)
        block = ctx.enter_context(nc.Block())

        @block.sync
        def _(sp):
            def page(i):
                return sp.value_load(pages[0:1, i:i + 1], min_val=0, max_val=dram["pool_v"].shape[0] - 1)

            def chunk(name):
                n = place[name]
                _, loads, _, _ = stream[n]
                if n >= RING:
                    _, _, used_by, used_at = stream[n - RING]
                    sp.wait_ge(S(used_by), used_at)
                for dst, src, pg in loads:
                    d = dst(ring[:, n % RING, :])
                    if pg is None:
                        sp.dma_start(d, src).then_inc(S(f"ring{n % RING}"), 16)
                    else:
                        s = dram[src][page(pg)]
                        if src == "pool_k":
                            s = s.rearrange("p (e n) -> p e n", e=2)
                        sp.dma_start(d, s).then_inc(S(f"ring{n % RING}"), 16)

            sp.dma_start(silc.rearrange("p k b -> p (k b)"), dram["c"].rearrange("p k b -> p (k b)")).then_inc(S("c_in"), 16)
            chunk(stream[0][0])
            sp.dma_start(pages[:, :], dram["page_table"]).then_inc(S("pages_in"), 16)
            sp.dma_start(lam, dram["lam"].rearrange("p (i s) -> p i s", s=ST)).then_inc(S("params_in"), 16)
            for e in range(2):
                sp.dma_start(ldt[64 * e:64 * e + 64, :], dram["log_dt"][e].broadcast_to([64, ST])).then_inc(S("params_in"), 16)
            sp.dma_start(consts[:, :], dram["consts"]).then_inc(S("params_in"), 16)
            sp.dma_start(vec[:, :], dram["vec"]).then_inc(S("vec_in"), 16)
            for n in range(1, RING):
                chunk(stream[n][0])
            sp.dma_start(braw, dram["ssm_b"].rearrange("p (e s c) -> p e s c", e=2, s=ST)).then_inc(S("bc_in"), 16)
            sp.dma_start(craw, dram["ssm_c"].rearrange("p (e s c) -> p e s c", e=2, s=ST)).then_inc(S("bc_in"), 16)
            sp.dma_start(h0, dram["ssm_h0"].rearrange("p (e s b) -> p e s b", e=2, s=ST)).then_inc(S("bc_in"), 16)
            sp.dma_start(x, dram["x"]).then_inc(S("x_in"), 16)
            for n in range(RING, NMOD0):
                chunk(stream[n][0])
            sp.dma_start(w1, dram["cmp_w1"][0].rearrange("p (l n) -> p l n", n=P)).then_inc(S("w1_in"), 16)
            sp.wait_ge(S("pages_in"), 16)
            for u in range(units):
                e, b = u // DB, u % DB
                if not 2 <= u < DB:
                    for j in mod_of_unit[u]:
                        chunk(f"mod{j}")
                if u == DB:
                    sp.wait_ge(S("hid_mm"), DB)
                    sp.dma_start(w1, dram["cmp_w1"][1].rearrange("p (l n) -> p l n", n=P)).then_inc(S("w1_in"), 16)
                if u < 2:
                    sp.wait_ge(S("bt_mm"), 4)
                    sp.wait_ge(S("cx_done"), 1)
                else:
                    sp.wait_ge(S("hid_mm"), u - 1)
                for j in range(NPG):
                    sp.dma_start(XT[:, u % 2, :, 64 * j:64 * j + 64],
                                 dram["pool_cmp"][e][page(NPG * b + j)].rearrange("p (h n) -> p h n", h=KVH)
                                 ).then_inc(S(f"xt{u % 2}_in"), 16)
                if 2 <= u < DB:
                    for j in mod_of_unit[u]:
                        chunk(f"mod{j}")
            for j in range(2):
                chunk(f"glu{j}")
            sp.dma_start(prefix, dram["prefix"][0].rearrange("p (j a b r) -> p j a b r", a=2, b=DB, r=2)).then_inc(S("prefix_in"), 16)
            sp.wait_ge(S("s_ready"), units)
            sp.dma_start(x, dram["x"]).then_inc(S("x_in"), 16)
            sp.wait_ge(S("last_states"), 2 * units)
            sp.dma_start(dram["out_ssm"], FS.rearrange("p s e b -> p (s e b)")).then_inc(S("out_ssm"), 16)
            first_after = place["up0_0"]
            for n in range(first_after, len(stream)):
                name = stream[n][0]
                chunk(name)
                if name == "kv0":
                    sp.wait_ge(S("conv_rows0"), 2 * FT)
                    sp.dma_start(dram["out_conv"][0], conv_rows.rearrange("p j a b r -> p (j a b r)")).then_inc(S("out_conv"), 16)
                    sp.wait_ge(S("prefixed0"), FT)
                    sp.dma_start(prefix, dram["prefix"][1].rearrange("p (j a b r) -> p j a b r", a=2, b=DB, r=2)).then_inc(S("prefix_in"), 16)
                if name == "gate":
                    sp.wait_ge(S("roped"), 4)
                    sp.wait_ge(S("kv_ev"), 12)
                    sp.dma_start(dram["out_kv"], KV).then_inc(S("out_kv"), 16)
            sp.wait_ge(S("conv_rows1"), 2 * FT)
            sp.dma_start(dram["out_conv"][1], conv_rows.rearrange("p j a b r -> p (j a b r)")).then_inc(S("out_conv"), 16)
            for k in range(2, KT + 1, 2):
                sp.wait_ge(S("x_done3"), 2 * k)
                sp.dma_start(dram["out_y"][:, k - 2:k], x[:, k - 2:k]).then_inc(S("out_y"), 16)
            sp.wait_ge(S("out_ssm"), 16)
            sp.wait_ge(S("out_conv"), 32)
            sp.wait_ge(S("out_kv"), 16)
            sp.wait_ge(S("out_y"), 16 * KT // 2)

        @block.tensor
        def _(pe):
            def product(out, name, tile, src, k, start, stop):
                n, first = place[name], tile - tile % PIECE
                p = pieces[name, first]
                if tile == first:
                    pe.wait_ge(S("lo_ready"), p + 1)
                at = P * (tile - first)
                xr, xh, xl = src
                w = ring_hi[:, n % RING, P * tile:P * tile + P]
                if name[0:3] == "mod":
                    pe.matmul(out, w, xh[:, k, :], start=start, stop=False)
                    pe.matmul(out, lo[:, p % SPLIT, at:at + P], xl[:, k, :], start=False, stop=False)
                else:
                    pe.matmul(out, wr[:, p % SPLIT, at:at + P], xr[:, k, :], start=start, stop=False)
                mm = pe.matmul(out, lo[:, p % SPLIT, at:at + P], xh[:, k, :], start=False, stop=False)
                if tile - first == piece_list[p][2] - 1:
                    mm.then_inc(S("lo_used"), 1)
                return pe.matmul(out, w, xl[:, k, :], start=False, stop=stop)

            def modulation(j, between=None):
                if j >= 2:
                    pe.wait_ge(S("mod_ev"), 4 * (j - 1) if j < NMOD0 else 4 * j)
                for m in range(4):
                    for k in range(KT):
                        mm = product(PS[:, mod_bank[j], NB * m:NB * m + NB], f"mod{j}", KT * m + k, (None, silb[:, 0], silb[:, 1]), k,
                                     k == 0, k == KT - 1)
                    if m == 3:
                        mm.then_inc(S("mod_mm"), 1)
                    if between:
                        between()

            def sums(r):
                for k in range(KT):
                    sum_of(r, k)

            def sum_of(r, k):
                pe.wait_ge(S("sq"), KT * (nth_norm[r] - 1) + k + 1)
                mm = pe.matmul(PS[:, 7, 0:T], C["ones"], h[:, k, :], start=(k == 0), stop=(k == KT - 1))
                if k == KT - 1:
                    mm.then_inc(S("sum"), 1)

            def h_ready(r):
                pe.wait_ge(S("hp"), KT * nth_mod[r])
                pe.wait_ge(S("hs"), nth_mod[r])

            def dense(tag, chunks, kt, src, per, banks, ev, ready, norm=None):
                m = 0
                for name in chunks:
                    for i in range(per):
                        if norm is not None and m >= 3:
                            sum_of(norm, m - 3)
                        if m >= len(banks):
                            pe.wait_ge(S(ev), m - len(banks) + 1)
                        for k in range(kt):
                            if m == 0:
                                pe.wait_ge(S(ready[0]), ready[1] + k + 1)
                            mm = product(PS[:, banks[m % len(banks)], 0:T], name, kt * i + k, src, k, k == 0, k == kt - 1)
                        mm.then_inc(S(f"{tag}_mm"), 1)
                        m += 1
                for k in range(m - 3 if norm is not None else m, m):
                    if norm is not None:
                        sum_of(norm, k)

            def split_of(r):
                return "h_lo", KT * (nth_split[r] - 1)

            def ffn(l):
                ready = split_of((2, 7)[l])
                for j in range(FT):
                    if j >= 3:
                        pe.wait_ge(S(f"up_ev{l}"), 2 * (j - 2))
                    for a in range(2):
                        for k in range(KT):
                            if j == 0 and a == 0:
                                pe.wait_ge(S(ready[0]), ready[1] + k + 1)
                            mm = product(PS[:, 2 * (j % 3) + a, 0:T], f"up{l}_{j // 2}", 16 * (j % 2) + KT * a + k, hb, k, k == 0, k == KT - 1)
                    mm.then_inc(S(f"up{l}_mm"), 1)
                dense(f"down{l}", [f"down{l}_{j}" for j in range(8)], FT, U, 1, down_banks, f"down{l}_ev", (f"u_lo{l}", 0), norm=(3, 8)[l])

            pe.wait_ge(S("silb"), 2)
            for j in range(NMOD0 - 1):
                modulation(j)
            pe.wait_ge(S("bx_done"), 4)
            for q in range(16):
                e, f = q // 8, q % 8
                mm = pe.transpose(PS[:, q // 4, P * (q % 4):P * (q % 4) + P],
                                  BX[:, e, 4 * f:4 * f + 4, :].rearrange("p s c -> p (s c)"), ident)
                if q % 4 == 3:
                    mm.then_inc(S("bt_mm"), 1)
            sums(0)
            modulation(NMOD0 - 1)
            pe.wait_ge(S("bt_ev"), 4)

            def inputs_of(u):
                f = u // 2
                if u == 0:
                    pe.wait_ge(S("hs"), 1)
                if u % 2 == 0:
                    pe.wait_ge(S("hp"), f + 1)
                if u >= 1:
                    pe.wait_ge(S("u_read"), 2 * u)
                for i in range(2):
                    r = 32 * (2 * (u % 2) + i)
                    for e in range(2):
                        mm = pe.matmul(PS[:, 2 * i + e, 0:T], BT[r:r + 32, e, f, :], h[r:r + 32, f, :], start=True, stop=True)
                mm.then_inc(S("u_mm"), 1)

            def hidden(u):
                e = u // DB
                if u % DB == 0:
                    pe.wait_ge(S("w1_in"), 16 * (e + 1))
                    if e == 1:
                        pe.wait_ge(S("hid_ev"), u)
                    for l in range(16):
                        mm = pe.matmul(PS[:, 6, 500:501], w1[:, l, :], pe_[:, e, l:l + 1], start=(l == 0), stop=(l == 15))
                    mm.then_inc(S("pb_mm"), 1)
                    pe.wait_ge(S("pb_ev"), e + 1)
                pe.wait_ge(S(f"xt{u % 2}_in"), 16 * NPG * (u // 2 + 1))
                if u >= 1:
                    pe.wait_ge(S("hid_ev"), u)

            def hidden_part(u, ls):
                for l in ls:
                    mm = pe.matmul(PS[:, 6, 0:KVH * NC], w1[:, l, :], XT[:, u % 2, :, l:l + 8 * (NC - 1) + 1:8],
                                   start=(l == 0), stop=(l == 15))
                    if l == 15:
                        mm.then_inc(S("hid_mm"), 1)

            def compressed(u):
                pe.wait_ge(S("hid_ev"), u + 1)
                if u >= 1:
                    pe.wait_ge(S("kc_ev"), u)
                hg = HG[:, u % 2]
                if u < DB:
                    for hp in range(2):
                        mm = pe.matmul(PS[64 * hp:64 * hp + 64, 7, 0:2 * NC], w2[:, 0, :], hg[:, hp:4:2, :], start=True, stop=True)
                else:
                    for hd in range(KVH):
                        mm = pe.matmul(PS[0:NC, 7, HD * hd:HD * hd + HD], hg[:, hd, :], w2[:, 1, :], start=True, stop=True)
                mm.then_inc(S("kc_mm"), 1)

            def outputs_of(u):
                f = u // 2
                pe.wait_ge(S("s_ready"), u + 1)
                if u % 2 == 0 and f >= 1:
                    pe.wait_ge(S("y_read"), f)
                for i in range(2):
                    r = 32 * (2 * (u % 2) + i)
                    for e in range(2):
                        mm = pe.matmul(PS[r:r + 32, 4, 0:T], CX[:, e, 2 * u + i, :], VS[u % 2][:, i, e, :], start=(e == 0), stop=(e == 1))
                mm.then_inc(S("y_mm"), 1)

            for u in range(units):
                inputs_of(u)
                hidden(u)
                per, done = 4 // len(mod_of_unit[u]), [0]

                def between():
                    hidden_part(u, range(done[0], done[0] + per))
                    done[0] += per

                modulation(mod_of_unit[u][0], between)
                if u >= 1:
                    compressed(u - 1)
                    outputs_of(u - 1)
                for j in mod_of_unit[u][1:]:
                    modulation(j, between)
            compressed(units - 1)
            outputs_of(units - 1)

            dense("glu", ["glu0", "glu1"], KT, gb, 4, (0, 1, 2, 3), "glu_ev", ("g_lo", 0), norm=1)
            sums(2)
            ffn(0)

            sums(4)
            dense("kv", ["kv0", "kv1", "kv2"], KT, hb_kv, 4, (0, 1, 2, 3), "kv_ev", split_of(4))

            def rotated(i, src):
                if i >= 2:
                    pe.wait_ge(S("rope_read"), i - 1)
                pe.matmul(PS[:, 4 + i % 2, 0:T], C["rot"], src, start=True, stop=True).then_inc(S("rope_mm"), 1)

            pe.wait_ge(S("kv_ev"), 12)
            for i, m in enumerate((4, 5, 8, 9)):
                rotated(i, KV[:, m, :])
            pw = arrived(pe, "w1").rearrange("p (e l n) -> p e l n", e=2, l=16)
            for e in range(2):
                for hd in range(KVH):
                    for par in range(2):
                        hp = hd % 2
                        mm = pe.matmul(PS[64 * par:64 * par + 64, e, P * hd:P * hd + P], ident[:, 64 * hp:64 * hp + 64],
                                       KV[:, 2 * e + hd // 2, par:SEQ:2], start=True, stop=True)
                mm.then_inc(S("pair_mm"), 1)
            for e in range(2):
                pe.wait_ge(S("pair_ev"), e + 1)
                for l in range(16):
                    mm = pe.matmul(PS[:, 2 + e, 0:KVH * NCP], pw[:, e, l, :], XP[:, KVH * e:KVH * e + KVH, l:l + 8 * (NCP - 1) + 1:8],
                                   start=(l == 0), stop=(l == 15))
                mm.then_inc(S("pcmp_mm"), 1)
            pe.wait_ge(S("hp_ev"), 2)
            hp_ = HP.rearrange("p e (h n) -> p e h n", n=NCP)
            for hp in range(2):
                mm = pe.matmul(PS[64 * hp:64 * hp + 64, 6, 0:2 * NCP], w2[:, 0, :], hp_[:, 0, hp:4:2, :], start=True, stop=True)
            mm.then_inc(S("pkc_mm"), 1)
            for hd in range(KVH):
                mm = pe.matmul(PS[0:NCP, 7, HD * hd:HD * hd + HD], hp_[:, 1, hd, :], w2[:, 1, :], start=True, stop=True)
            mm.then_inc(S("pkc_mm"), 1)

            pe.wait_ge(S("hp_ev"), 2)
            for n in range(2):
                for sl in range(2):
                    for hh in range(2):
                        at = 256 * sl + P * hh
                        mm = pe.transpose(PS[:, n, at:at + P], KV[:, (6, 10)[sl] + hh, P * n:P * n + P], ident)
                mm.then_inc(S("vt_mm"), 1)

            h_ready(5)
            wg = arrived(pe, "gate")[:, 0:KT * 3 * NH].rearrange("p (k n) -> p k n", k=KT)
            pe.wait_ge(S("pkc_ev"), 2)
            for k in range(KT):
                mm = pe.matmul(PS[0:3 * NH, 7, 0:DB * DS], wg[:, k, :], wk[:, k, SEQ:T], start=(k == 0), stop=(k == KT - 1))
            mm.then_inc(S("gate_mm"), 1)
            for qt in range(2):
                at = 64 + 3 * NH * qt
                for k in range(KT):
                    mm = pe.matmul(PS[:, 7, at:at + 3 * NH], wk[:, k, P * qt:P * qt + P], wg[:, k, :], start=(k == 0), stop=(k == KT - 1))
                mm.then_inc(S("gate_mm"), 1)
            pe.wait_ge(S("vt_ev"), 2)
            dense("q", ["q0", "q1"], KT, hb_kv, 4, (0, 1, 2, 3), "q_ev", split_of(5))
            for i in range(4, 12):
                pe.wait_ge(S("q_ev"), i - 3)
                rotated(i, Qp[:, i - 4, :])
            pe.wait_ge(S("gate_ev"), 1)
            for br in range(3):
                mm = pe.matmul(PS[:, 6, 64 * br:64 * br + 64], C["gate_spread"][0:3 * NH, P * br:P * br + P], gf[0:3 * NH, :],
                               start=True, stop=True)
            mm.then_inc(S("spread_mm"), 1)

            pe.wait_ge(S("qbp_done"), 4)
            pe.wait_ge(S("q_ev"), KT)
            pe.wait_ge(S("gate_ev"), 2)
            for b in range(DB):
                for hh in range(2):
                    mm = pe.matmul(PS[:, 7, NC * b:NC * b + NC], QBp[:, hh, b, :], kcT[:, b, hh, :], start=(hh == 0), stop=(hh == 1))
            mm.then_inc(S("c_mm"), 1)

            def scores(j):
                kind, a, qt = jobs[j]
                if j == 0:
                    pe.wait_ge(S("roped"), 12)
                else:
                    pe.wait_ge(S("s_evd"), before(NV, j))
                if kind == "prompt":
                    hh, hp, K = a // 2, a % 2, P * (qt + 1)
                    r = slice(64 * hp, 64 * hp + 64)
                    q = slice(P * qt, P * qt + P)
                    for g in range(GQA):
                        for br, m in ((0, 4), (2, 8)):
                            at = g * K
                            pe.matmul(PS[:, br + at // 512, at % 512:at % 512 + K], Qr[r, 4 * hh + g, q], KV[r, m + hh, 0:K],
                                      start=True, stop=True)
                        mm = pe.matmul(PS[:, 4, NCP * g:NCP * g + NCP], Qp[r, 4 * hh + g, q], kcT[r, DB, hh, 0:NCP], start=True, stop=True)
                else:
                    ks = arrived(pe, f"k{a}")
                    if a == 0:
                        pe.wait_ge(S("qbr_done"), 4)
                    new = slice(SEQ + DS * a, SEQ + DS * a + DS)
                    sel = ks[:, 0:2048].rearrange("p (e n) -> p e n", e=2)
                    win = ks[:, 2048:3072].rearrange("p (e n) -> p e n", e=2)
                    for out, rhs in ((PS[:, 0, :], sel[:, :, 0:512]), (PS[:, 1, :], sel[:, :, 512:1024]), (PS[:, 2, :], win),
                                     (PS[:, 3, 0:DS], KV[:, 4:6, new]), (PS[:, 3, DS:2 * DS], KV[:, 8:10, new])):
                        for hh in range(2):
                            mm = pe.matmul(out, QBr[:, hh, a, :], rhs[:, hh, :], start=(hh == 0), stop=(hh == 1))
                mm.then_inc(S("s_mm"), 1)

            def turned(j):
                kind, a, qt = jobs[j]
                sc = SC[j % 2]
                if kind == "prompt":
                    K = P * (qt + 1)
                    cols = [[(base + g * K + P * kt, P) for g in range(GQA)] for base in (0, 1024) for kt in range(qt + 1)]
                    cols.append([(2048 + NCP * g, NCP) for g in range(GQA)])
                    groups = [[(sc[:, c:c + n], n) for c, n in grp] for grp in cols]
                    needed = [5] * (qt + 1) + [9] * (qt + 2)
                else:
                    groups = [[(sc[:, c + P * i:c + P * i + P], P) for i in range(4)] for c in (0, 512, 1032)]
                    groups.append([(sc[:, 1024:1032], DS), (sc[:, 1544:1552], DS), (PC[:, a, 0:NC], NC)])
                    new = slice(SEQ + DS * a, SEQ + DS * a + DS)
                    groups.append([(KV[:, m, new], DS) for m in (6, 7, 10, 11)])
                    needed = [1, 1, 2, 2, 2]
                for n, grp in enumerate(groups):
                    pe.wait_ge(S("p_ready"), before(NPR, j) + needed[n])
                    G = groups_before[j] + n
                    if G >= 2:
                        jj = max(i for i in range(len(jobs)) if groups_before[i] <= G - 2)
                        k = G - 2 - groups_before[jj]
                        done = evacs_before[jj] + k + 1 + (1 if k >= 3 and jobs[jj][0] == "sample" else 0)
                        pe.wait_ge(S("tr_ev"), done)
                    for i, (src, rows) in enumerate(grp):
                        mm = pe.transpose(PS[0:rows, 5 + G % 2, P * i:P * i + P], src, ident)
                    mm.then_inc(S("tr_mm"), 1)

            def values(j):
                kind, a, qt = jobs[j]
                if j >= 1:
                    pe.wait_ge(S("o_ev"), before(NOE, j))
                pe.wait_ge(S("tr_ev"), evacs_before[j + 1])
                if kind == "prompt":
                    hp = a % 2
                    out = PS[64 * hp:64 * hp + 64, 7, :]
                    ops = [(VT[:, kt, 256 * sl + HD * a:256 * sl + HD * a + HD], P) for sl in range(2) for kt in range(qt + 1)]
                    ops.append((vc[0:NCP, DB, HD * a:HD * a + HD], NCP))
                    for n, (lhs, rows) in enumerate(ops):
                        mm = pe.matmul(out, lhs, PT[0:rows, 512 * n:512 * n + 512], start=(n == 0), stop=(n == len(ops) - 1))
                else:
                    vs = arrived(pe, f"v{a}")
                    for hh in range(2):
                        hc = P * hh
                        ops = [(vs[:, 256 * c + hc:256 * c + hc + P], P) for c in range(12)]
                        ops += [(VN[0:DS, 256 * sl + hc:256 * sl + hc + P], DS) for sl in range(2)]
                        ops.append((vc[0:NC, a, hc:hc + P], NC))
                        for n, (lhs, rows) in enumerate(ops):
                            mm = pe.matmul(PS[:, 7, 64 * hh:64 * hh + 64], lhs, PT[0:rows, P * n + 64 * hh:P * n + 64 * hh + 64],
                                           start=(n == 0), stop=(n == len(ops) - 1))
                mm.then_inc(S("pv_mm"), 1)

            scores(0)
            pe.wait_ge(S("imp_ready"), 1)
            pe.matmul(PS[:, 6, 0:DB * NFREE], C["group_sum"], imp.rearrange("p b n -> p (b n)"), start=True, stop=True).then_inc(S("imp_mm"), 1)
            for j in range(len(jobs)):
                if j + 1 < len(jobs):
                    scores(j + 1)
                turned(j)
                values(j)
            dense("o", ["o0", "o1"], KT, ob, 4, (0, 1, 2, 3), "o_ev2", ("o_lo", 0), norm=6)
            sums(7)
            ffn(1)


        @block.scalar
        def _(act):
            def square(src, k):
                act.activation(h[:, k, :], src[:, k, :], ACT.Square).then_inc(S("sq"), 1)

            def squares(src, ready, first, step):
                for k in range(KT):
                    act.wait_ge(S(ready), first + step * k)
                    square(src, k)

            def root(r):
                act.wait_ge(S("sum"), nth_norm[r])
                act.activation(rroot, PS[:, 7, 0:T], ACT.Sqrt, scale=1.0 / D, bias=eps).then_inc(S("root"), 1)

            def modulated(r, tile):
                dst = h if r == 0 else wk
                for k in range(KT):
                    act.wait_ge(S("scaled"), KT * (nth_mod[r] - 1) + k + 1)
                    act.activation(dst[:, k, 0:SEQ], dst[:, k, 0:SEQ], ACT.Identity, bias=mod[:, tile + k, 0:1],
                                   scale=mod[:, tile + 8 + k, 0:1]).then_inc(S("hp"), 1)

            def modulation(j):
                act.wait_ge(S("mod_mm"), j + 1)
                for m in range(4):
                    tile = mod_tile[j] + m
                    act.activation(mod[:, tile, :], PS[:, mod_bank[j], NB * m:NB * m + NB], ACT.Identity,
                                   bias=b_mod[:, tile:tile + 1]).then_inc(S("mod_ev"), 1)

            made = [n_mod_pieces]

            def high_parts(count=1):
                for _ in range(count):
                    p = made[0]
                    made[0] += 1
                    name, first, tiles = piece_list[p]
                    n, c = place[name], P * first
                    act.wait_ge(S(f"ring{n % RING}"), landed[n])
                    if p >= n_mod_pieces + SPLIT:
                        act.wait_ge(S("lo_used"), p - SPLIT + 1)
                    act.activation(wr[:, p % SPLIT, 0:P * tiles], ring[:, n % RING, c:c + P * tiles],
                                   ACT.Copy).then_inc(S("hi_ready"), 1)

            def tiles_out(tag, dst, n, ev, scale=1.0, banks=(0, 1, 2, 3), ahead=(), norm=False):
                for m in range(n):
                    if m < len(ahead):
                        high_parts(ahead[m])
                    act.wait_ge(S(f"{tag}_mm"), m + 1)
                    act.activation(dst[:, m, :], PS[:, banks[m % len(banks)], 0:T], ACT.Copy, scale=scale).then_inc(S(ev), 1)
                    if norm:
                        act.wait_ge(S(ev), m + 1)
                        square(dst, m)

            def ffn(l):
                act.wait_ge(S(f"ext_zero{l}"), 3)
                for j in range(FT):
                    high_parts(2)
                    s = j % 3
                    e = XE[:, s]
                    act.wait_ge(S(f"up{l}_mm"), j + 1)
                    if j >= 3:
                        act.wait_ge(S(f"conv2_{l}"), 2 * (j - 2))
                        act.wait_ge(S(f"conv_rows{l}"), 2 * (j - 2))
                    pair = PS[:, 2 * (j % 3):2 * (j % 3) + 2, :]
                    act.activation(e[:, :, 2:2 + SEQ], pair[:, :, 0:SEQ], ACT.Copy).then_inc(S(f"up_ev{l}"), 1)
                    act.activation(e[:, :, 2 + SEQ:].rearrange("p a (b r) -> p a b r", b=DB)[:, :, :, 2:],
                                   pair[:, :, SEQ:T].rearrange("p a (b r) -> p a b r", b=DB), ACT.Copy).then_inc(S(f"up_ev{l}"), 1)
                    act.wait_ge(S(f"up_ev{l}"), 2 * j + 2)
                    act.wait_ge(S(f"prefixed{l}"), j + 1)
                    if j >= 3:
                        act.wait_ge(S(f"u_mul{l}"), 2 * (j - 2))
                    for a in range(2):
                        m = 2 * j + a
                        act.activation(CV[:, s, a, :], e[:, a, 0:CW], ACT.Identity, bias=conv_b[:, l, m:m + 1],
                                       scale=conv_w[:, l, m, 0:1]).then_inc(S(f"conv0_{l}"), 1)
                    if j >= 1:
                        gate_of(l, j - 1)
                    if j >= 2:
                        high_of(l, j - 2)
                gate_of(l, FT - 1)
                high_of(l, FT - 2)
                high_of(l, FT - 1)
                tiles_out(f"down{l}", wk, KT, f"down{l}_ev", banks=down_banks, ahead=[3] * (KT - l), norm=True)

            def high_of(l, j):
                act.wait_ge(S(f"u_mul{l}"), 2 * j + 2)
                act.activation(U[0][:, j, :], UF[:, j % 3, :], ACT.Copy).then_inc(S(f"u_hi{l}"), 1)

            def gate_of(l, j):
                act.wait_ge(S(f"conv2_{l}"), 2 * j + 2)
                act.activation(SG[:, j % 3, :], CV[:, j % 3, 1, :], ACT.Silu).then_inc(S(f"sg{l}"), 1)

            act.wait_ge(S("eps"), 1)
            act.wait_ge(S("c_in"), 16)
            act.activation(silc, silc, ACT.Silu).then_inc(S("silc"), 1)
            act.wait_ge(S("silc"), 1)
            act.activation(silb[:, 0], silc, ACT.Copy).then_inc(S("silb"), 1)
            act.wait_ge(S("params_in"), 64)
            act.activation(pr["dt"], ldt, ACT.Exp).then_inc(S("dt"), 1)
            act.wait_ge(S("lrdt"), 1)
            act.activation(pr["mag"], pr["lrdt"], ACT.Exp).then_inc(S("mag"), 1)
            act.wait_ge(S("phases"), 2)
            act.activation(E[:, 1], phase_sin, ACT.Sin, scale=TWO_PI_IN).then_inc(S("trig"), 1)
            act.activation(E[:, 0], phase_cos, ACT.Sin, scale=TWO_PI_IN).then_inc(S("trig"), 1)
            act.wait_ge(S("vec_in"), 16)
            for j in range(NMOD0 - 1):
                modulation(j)
            squares(x, "x_in", 16, 0)
            for i in range(4):
                act.wait_ge(S("bt_mm"), i + 1)
                act.activation(BT.rearrange("p e f n -> p (e f n)")[:, 512 * i:512 * i + 512], bank(i), ACT.Copy).then_inc(S("bt_ev"), 1)
            root(0)
            modulation(NMOD0 - 1)
            modulated(0, 0)

            def hidden(u):
                e = u // DB
                if u % DB == 0:
                    act.wait_ge(S("pb_mm"), e + 1)
                    act.activation(cmp_bias[:, e:e + 1], PS[:, 6, 500:501], ACT.Identity, bias=V["cmp_b1"][:, e:e + 1]).then_inc(S("pb_ev"), 1)
                    act.wait_ge(S("pb_ev"), e + 1)

            def hidden_out(u):
                e = u // DB
                act.wait_ge(S("hid_mm"), u + 1)
                if u >= 2:
                    act.wait_ge(S("kc_mm"), u - 1)
                act.activation(HG[:, u % 2].rearrange("p h n -> p (h n)"), PS[:, 6, 0:KVH * NC], ACT.Gelu_apprx_tanh,
                               bias=cmp_bias[:, e:e + 1]).then_inc(S("hid_ev"), 1)

            def compressed(u):
                act.wait_ge(S("kc_mm"), u + 1)
                b = u % DB
                if u < DB:
                    act.activation(kcT[:, b], PS[:, 7, 0:2 * NC].rearrange("p (e n) -> p e n", e=2), ACT.Copy).then_inc(S("kc_ev"), 1)
                else:
                    act.activation(vc[0:NC, b, :], PS[0:NC, 7, 0:KVH * HD], ACT.Copy).then_inc(S("kc_ev"), 1)

            def last_states(u):
                act.wait_ge(S("s_ready"), u + 1)
                v = VS[u % 2]
                act.activation(FS[:, 2 * u:2 * u + 2, :, 0], v[:, :, :, SEQ - 1], ACT.Copy).then_inc(S("last_states"), 1)
                act.activation(FS[:, 2 * u:2 * u + 2, :, 1:], v[:, :, :, SEQ + DS - 1::DS], ACT.Copy).then_inc(S("last_states"), 1)

            def gelu(f):
                act.wait_ge(S("y_read"), f + 1)
                act.activation(h[:, f, :], h[:, f, :], ACT.Gelu_apprx_tanh).then_inc(S("g_ready"), 1)

            for u in range(units):
                hidden(u)
                modulation(mod_of_unit[u][0])
                if u >= 1:
                    compressed(u - 1)
                    last_states(u - 1)
                for j in mod_of_unit[u][1:]:
                    modulation(j)
                hidden_out(u)
                if u >= 3 and u % 2 == 1:
                    gelu((u - 3) // 2)
            compressed(units - 1)
            last_states(units - 1)
            act.wait_ge(S("tables"), 2 * units)
            high_parts(2)
            gelu(7)
            high_parts(1)
            for m in range(KT):
                high_parts()
                act.wait_ge(S("glu_mm"), m + 1)
                if m >= 2:
                    act.wait_ge(S("wk_done"), m - 1)
                act.activation(sig[:, m % 2, :], PS[:, m % 4, 0:T], ACT.Sigmoid, bias=V["b_glu"][:, m:m + 1]).then_inc(S("glu_ev"), 1)
                if m >= 1:
                    act.wait_ge(S("wk_done"), m)
                    square(wk, m - 1)
            act.wait_ge(S("wk_done"), KT)
            square(wk, KT - 1)
            root(1)
            squares(x, "x_done0", 2, 2)
            root(2)
            modulated(2, 24)
            ffn(0)
            root(3)
            squares(x, "x_done1", 2, 2)
            root(4)
            modulated(4, 96)
            modulated(5, 48)

            tiles_out("kv", KV, 12, "kv_ev", ahead=[1] * 9)
            for e in range(2):
                act.wait_ge(S("pair_mm"), e + 1)
                act.activation(XP[:, KVH * e:KVH * e + KVH, :].rearrange("p h n -> p (h n)"), bank(e), ACT.Copy).then_inc(S("pair_ev"), 1)
            for e in range(2):
                act.wait_ge(S("pcmp_mm"), e + 1)
                act.activation(HP[:, e, :], PS[:, 2 + e, 0:KVH * NCP], ACT.Gelu_apprx_tanh, bias=cmp_bias[:, e:e + 1]).then_inc(S("hp_ev"), 1)
            act.wait_ge(S("pkc_mm"), 2)
            act.activation(kcT[:, DB, :, 0:NCP], PS[:, 6, 0:2 * NCP].rearrange("p (e n) -> p e n", e=2), ACT.Copy).then_inc(S("pkc_ev"), 1)
            act.activation(vc[0:NCP, DB, :], PS[0:NCP, 7, 0:KVH * HD], ACT.Copy).then_inc(S("pkc_ev"), 1)
            for n in range(2):
                act.wait_ge(S("vt_mm"), n + 1)
                act.activation(VT[:, n, :], bank(n), ACT.Copy).then_inc(S("vt_ev"), 1)
            high_parts(3)
            act.wait_ge(S("gate_mm"), 3)
            act.activation(gf[0:3 * NH, :], PS[0:3 * NH, 7, 0:DB * DS], ACT.Sigmoid).then_inc(S("gate_ev"), 1)
            act.activation(gp, PS[:, 7, 64:64 + 6 * NH].rearrange("p (k n) -> p k n", k=2), ACT.Sigmoid).then_inc(S("gate_ev"), 1)
            tiles_out("q", Qp, KT, "q_ev", scale=HD ** -0.5, ahead=[1] * 5)
            act.wait_ge(S("c_shift"), 1)
            act.activation(PC[:, :, 0:NC], PC[:, :, 0:NC], ACT.Exp).then_inc(S("c_exp"), 1)

            def exponentials(j):
                kind, a, qt = jobs[j]
                sc, s = SC[j % 2], j % 2
                act.wait_ge(S("nmax"), 2 * j + 1)
                if j >= 2:
                    act.wait_ge(S("fac"), 2 * (j - 1))
                if kind == "prompt":
                    K = P * (qt + 1)
                    for br, base, n in ((0, 2048, NCP), (1, 0, K), (2, 1024, K)):
                        if br == 2:
                            act.wait_ge(S("nmax"), 2 * j + 2)
                        for g in range(GQA):
                            i = 4 * br + g
                            v = sc[:, base + g * n:base + g * n + n]
                            act.activation(v, v, ACT.Exp, bias=nmax[:, s, i:i + 1], accum_out=ssum[:, s, i:i + 1]).then_inc(S("exp"), 1)
                else:
                    for i, v in enumerate((sc[:, 0:1032], sc[:, 1032:1552])):
                        act.wait_ge(S("nmax"), 2 * j + 1 + i)
                        act.activation(v, v, ACT.Exp, bias=nmax[:, s, i:i + 1], accum_out=ssum[:, s, i:i + 1]).then_inc(S("exp"), 1)

            def turned_out(j):
                kind, a, qt = jobs[j]
                for n in range(NG[j]):
                    G = groups_before[j] + n
                    act.wait_ge(S("tr_mm"), G + 1)
                    if n == 0 and j >= 1:
                        act.wait_ge(S("pv_mm"), j)
                    bk = 5 + G % 2
                    if kind == "sample" and n == 4:
                        act.activation(VN[0:DS, :], PS[0:DS, bk, :], ACT.Copy).then_inc(S("tr_ev"), 1)
                    elif kind == "sample" and n == 3:
                        act.activation(PT[0:DS, 1536:1792], PS[0:DS, bk, 0:256], ACT.Copy).then_inc(S("tr_ev"), 1)
                        act.activation(PT[0:NC, 1792:1920], PS[0:NC, bk, 256:384], ACT.Copy).then_inc(S("tr_ev"), 1)
                    else:
                        rows = NCP if kind == "prompt" and n == NG[j] - 1 else P
                        act.activation(PT[0:rows, 512 * n:512 * n + 512], PS[0:rows, bk, :], ACT.Copy).then_inc(S("tr_ev"), 1)

            def output(j):
                kind, a, qt = jobs[j]
                act.wait_ge(S("pv_mm"), j + 1)
                if kind == "prompt":
                    hh, hp = a // 2, a % 2
                    r = slice(64 * hp, 64 * hp + 64)
                    act.activation(O[r, 4 * hh:4 * hh + 4, P * qt:P * qt + P], PS[r, 7, :].rearrange("p (g q) -> p g q", g=GQA),
                                   ACT.Copy).then_inc(S("o_ev"), 1)
                else:
                    for hp in range(2):
                        r = slice(64 * hp, 64 * hp + 64)
                        o = O[r, :, SEQ + DS * a:SEQ + DS * a + DS].rearrange("p (e g) q -> p e g q", e=2)
                        i = PS[r, 7, 0:P].rearrange("p (e f g q) -> p e f g q", e=2, f=2, g=GQA)[:, :, hp]
                        act.activation(o, i, ACT.Copy).then_inc(S("o_ev"), 1)

            exponentials(0)
            for j in range(len(jobs)):
                turned_out(j)
                if j + 1 < len(jobs):
                    exponentials(j + 1)
                else:
                    high_parts(3)
                output(j)
            tiles_out("o", wk, KT, "o_ev2", ahead=[1] * KT, norm=True)
            root(6)
            squares(x, "x_done2", 2, 2)
            root(7)
            modulated(7, 72)
            ffn(1)
            root(8)

        @block.gpsimd
        def _(pool):
            pool.memset(eps, EPS).then_inc(S("eps"), 1)
            pool.memset(BX, 0.0).then_inc(S("zeroed"), 1)
            pool.memset(CX, 0.0).then_inc(S("zeroed"), 1)
            pool.wait_ge(S("trig"), 2)
            pool.wait_ge(S("mag"), 1)
            pool.wait_ge(S("hs"), 1)
            pool.wait_ge(S("scaled"), KT)
            run = C["scan_run"]
            n_tab = [0]

            def tab(ins):
                n_tab[0] += 1
                ins.then_inc(S("pool_chain"), 1)
                pool.wait_ge(S("pool_chain"), n_tab[0])

            for u in range(units):
                s = u % 2
                if u >= 2:
                    pool.wait_ge(S("s_ready"), u - 1)

                def fine(e):
                    return E[:, e, 2 * u:2 * u + 2, 0:16].unsqueeze(2).broadcast_to([P, 2, 16, 16])

                def coarse(e):
                    return E[:, e, 2 * u:2 * u + 2, 16:32].unsqueeze(3).broadcast_to([P, 2, 16, 16])

                def grid(v):
                    return v.rearrange("p (i a b) -> p i a b", i=2, a=16)

                for tabl, (x1, x2), (y1, y2), op in ((TC, (0, 0), (1, 1), ALU.subtract), (TS, (1, 0), (0, 1), ALU.add)):
                    pool.tensor_tensor(grid(pt1), fine(x1), coarse(x2), ALU.mult).then_inc(S("pool_chain"), 1)
                    pool.tensor_tensor(grid(pt2), fine(y1), coarse(y2), ALU.mult).then_inc(S("pool_chain"), 1)
                    n_tab[0] += 2
                    pool.wait_ge(S("pool_chain"), n_tab[0])
                    tab(pool.tensor_tensor(tabl[:, s, :, 0:SEQ], pt1.rearrange("p (i t) -> p i t", i=2),
                                           pt2.rearrange("p (i t) -> p i t", i=2), op))
                    pool.tensor_copy(tabl[:, s, :, SEQ:T].rearrange("p i (b t) -> p i b t", b=DB),
                                     tabl[:, s, :, 0:DS].unsqueeze(2).broadcast_to([P, 2, DB, DS])).then_inc(S("tables"), 1)
                if u >= 1:
                    pool.wait_ge(S("scanned"), u)
                pool.tensor_tensor(decay4, run.unsqueeze(1).unsqueeze(1).broadcast_to([P, 2, 2, T]),
                                   pr["mag"][:, 2 * u:2 * u + 2].unsqueeze(2).unsqueeze(3).broadcast_to([P, 2, 2, T]),
                                   ALU.mult).then_inc(S("decay"), 1)

            def ffn(l):
                for s in range(3):
                    pool.memset(XE[:, s, :, 0:2], 0.0).then_inc(S(f"ext_zero{l}"), 1)
                pool.wait_ge(S("prefix_in"), 16 * (l + 1))
                if l == 1:
                    pool.wait_ge(S("out_conv"), 16)
                for j in range(FT):
                    e = XE[:, j % 3]
                    rows = e[:, :, 2 + SEQ:].rearrange("p a (b r) -> p a b r", b=DB)
                    if j >= 3:
                        pool.wait_ge(S(f"conv2_{l}"), 2 * (j - 2))
                    pool.tensor_copy(rows[:, :, :, 0:2], prefix[:, j]).then_inc(S(f"prefixed{l}"), 1)
                    pool.wait_ge(S(f"up_ev{l}"), 2 * j + 2)
                    pool.tensor_copy(conv_rows[:, j, :, 0, :], e[:, :, SEQ:SEQ + 2]).then_inc(S(f"conv_rows{l}"), 1)
                    pool.tensor_copy(conv_rows[:, j, :, 1:, :], rows[:, :, :, DS:]).then_inc(S(f"conv_rows{l}"), 1)

            pool.wait_ge(S("x_done0"), 2 * KT)
            ffn(0)
            pool.wait_ge(S("x_done1"), 2 * KT)
            pool.wait_ge(S("conv_rows0"), 2 * FT)
            pool.memset(QBp.rearrange("p e b n -> p (e b n)"), 0.0).then_inc(S("qb_zero"), 1)
            pool.memset(QBr.rearrange("p e b n -> p (e b n)"), 0.0).then_inc(S("qb_zero"), 1)
            pool.memset(PC, 0.0).then_inc(S("small_zero"), 1)
            pool.memset(drop, 0.0).then_inc(S("small_zero"), 1)
            pool.wait_ge(S("qb_zero"), 2)
            pool.wait_ge(S("small_zero"), 2)

            def spread(dst, src, done):
                for hp in range(2):
                    for hh in range(2):
                        r = slice(64 * hp, 64 * hp + 64)
                        c = 32 * (2 * hh + hp)
                        pool.tensor_copy(dst[r, hh, :, c:c + 32].rearrange("p b (g q) -> p b g q", g=GQA),
                                         src[r, 4 * hh:4 * hh + 4, SEQ:T].rearrange("p g (b q) -> p b g q", b=DB)).then_inc(S(done), 1)
                        pool.wait_ge(S(done), 2 * hp + hh + 1)

            pool.wait_ge(S("q_ev"), KT)
            spread(QBp, Qp, "qbp_done")
            pool.wait_ge(S("roped"), 12)
            spread(QBr, Qr, "qbr_done")
            pool.wait_ge(S("x_done2"), 2 * KT)
            ffn(1)

        @block.vector
        def _(dve):
            chain, posted = [0], {}

            def link(ins):
                chain[0] += 1
                ins.then_inc(S("dve_chain"), 1)
                dve.wait_ge(S("dve_chain"), chain[0])

            def post(ins, name, own=True):
                posted[name] = posted.get(name, 0) + 1
                ins.then_inc(S(name), 1)
                if own:
                    dve.wait_ge(S(name), posted[name])

            def tt(out, a, b, op):
                return dve.tensor_tensor(out, a, b, op)

            def inverse(r):
                dve.wait_ge(S("root"), nth_norm[r])
                link(dve.reciprocal(rinv, rroot))

            def samples(v):
                return v[:, :, SEQ:T].rearrange("p k (b t) -> p k b t", b=DB)

            def per_sample(tile):
                return mod[:, tile:tile + KT, 1:NB].unsqueeze(3).broadcast_to([P, KT, DB, DS])

            def modulated(r, tile, dst):
                out = h if r == 0 else wk
                of_samples = [
                    lambda: link(tt(out[:, :, SEQ:T], x[:, :, SEQ:T], rinv[:, SEQ:T].unsqueeze(1).broadcast_to([P, KT, DB * DS]), ALU.mult)),
                    lambda: link(tt(samples(out), samples(out), per_sample(tile + 8), ALU.mult)),
                    lambda: post(tt(samples(out), samples(out), per_sample(tile), ALU.add), "hs"),
                ]
                for k in range(KT + 3):
                    if k < KT:
                        post(tt(out[:, k, 0:SEQ], x[:, k, 0:SEQ], rinv[:, 0:SEQ], ALU.mult), "scaled", own=(k == KT - 1))
                    if k < 3:
                        of_samples[k]()
                    elif dst is not None:
                        dve.wait_ge(S("hp"), KT * (nth_mod[r] - 1) + k - 2)
                        split(dst, wk, k - 3, "h_lo")

            def split(dst, src, k, name):
                link(dve.tensor_copy(dst[0][:, k, :], src[:, k, :]))
                post(tt(dst[2][:, k, :], src[:, k, :], dst[0][:, k, :].bitcast(F32), ALU.subtract), name, own=False)

            made = [0]

            def low_parts(count=1):
                for _ in range(count):
                    p = made[0]
                    made[0] += 1
                    name, first, tiles = piece_list[p]
                    n, c, cols = place[name], P * first, P * tiles
                    dve.wait_ge(S(f"ring{n % RING}"), landed[n])
                    if p >= SPLIT:
                        dve.wait_ge(S("lo_used"), p - SPLIT + 1)
                    high = ring_hi[:, n % RING, c:c + cols]
                    if p >= n_mod_pieces:
                        dve.wait_ge(S("hi_ready"), p - n_mod_pieces + 1)
                        high = wr[:, p % SPLIT, 0:cols].bitcast(F32)
                    post(tt(lo[:, p % SPLIT, 0:cols], ring[:, n % RING, c:c + cols], high, ALU.subtract), "lo_ready", own=False)

            def added(r, tile, i):
                def normed(k):
                    chain[0] += 1
                    tt(wk[:, k, :], wk[:, k, :], rinv, ALU.mult).then_inc(S("dve_chain"), 1)
                    return chain[0]

                ready = normed(0)
                for k in range(KT):
                    following = normed(k + 1) if k + 1 < KT else None
                    dve.wait_ge(S("dve_chain"), ready)
                    mine, x_ = (v[:, k, SEQ:T].rearrange("p (b t) -> p b t", b=DB) for v in (wk, x))
                    gated_samples = tt(mine, mine, mod[:, tile + k, 1:NB].unsqueeze(2).broadcast_to([P, DB, DS]), ALU.mult)
                    chain[0] += 1
                    gated_samples.then_inc(S("dve_chain"), 1)
                    done = chain[0]
                    post(dve.scalar_tensor_tensor(out=x[:, k, 0:SEQ], in0=wk[:, k, 0:SEQ], scalar=mod[:, tile + k, 0:1],
                                                  in1=x[:, k, 0:SEQ], op0=ALU.mult, op1=ALU.add), f"x_done{i}", own=False)
                    dve.wait_ge(S("dve_chain"), done)
                    post(tt(x_, x_, mine, ALU.add), f"x_done{i}", own=(k == KT - 1))
                    ready = following

            def norm_weights(tile, pre, post_):
                sc_ = mod[:, tile + 8:tile + 16, :]
                link(dve.scalar_tensor_tensor(out=sc_, in0=sc_, scalar=1.0, in1=pre.unsqueeze(2).broadcast_to([P, KT, NB]),
                                              op0=ALU.add, op1=ALU.mult))
                if post_ is not None:
                    gate_weights(tile, post_)

            def gate_weights(tile, post_):
                g_ = mod[:, tile + 16:tile + 24, :]
                link(tt(g_, g_, post_.unsqueeze(2).broadcast_to([P, KT, NB]), ALU.mult))

            def ts(out, a, s1, s2, op0, op1=None):
                return dve.tensor_scalar(out, a, s1, s2, op0, op1) if op1 is not None else dve.tensor_scalar(out, a, s1, s2, op0)

            def ffn(l):
                for j in range(FT):
                    low_parts(2)
                    s = j % 3
                    for k in (1, 2):
                        for a in range(2):
                            m = 2 * j + a
                            dve.wait_ge(S(f"conv{k - 1}_{l}"), 2 * j + a + 1)
                            post(dve.scalar_tensor_tensor(out=CV[:, s, a, :], in0=XE[:, s, a, k:k + CW], scalar=conv_w[:, l, m, k:k + 1],
                                                          in1=CV[:, s, a, :], op0=ALU.mult, op1=ALU.add), f"conv{k}_{l}", own=False)
                    if j >= 1:
                        gated(l, j - 1)
                    if j >= 2:
                        low_of(l, j - 2)
                gated(l, FT - 1)
                low_of(l, FT - 2)
                low_of(l, FT - 1)
                low_parts(3 * (KT - l))

            def gated(l, j):
                s = j % 3
                dve.wait_ge(S(f"sg{l}"), j + 1)
                if j >= 3:
                    dve.wait_ge(S(f"u_lo{l}"), j - 2)
                post(tt(UF[:, s, 0:SEQ], CV[:, s, 0, 0:SEQ], SG[:, s, 0:SEQ], ALU.mult), f"u_mul{l}", own=False)
                post(tt(UF[:, s, SEQ:T].rearrange("p (b t) -> p b t", b=DB), every_ten(CV[:, s, 0, :]), every_ten(SG[:, s, :]), ALU.mult),
                     f"u_mul{l}")

            def low_of(l, j):
                dve.wait_ge(S(f"u_hi{l}"), j + 1)
                post(tt(U[2][:, j, :], UF[:, j % 3, :], U[0][:, j, :].bitcast(F32), ALU.subtract), f"u_lo{l}")

            def every_ten(v):
                return v[:, CW - 10 * DB:CW].rearrange("p (b t) -> p b t", t=DS + 2)[:, :, 2:]

            dve.wait_ge(S("silb"), 1)
            post(tt(silb[:, 1], silc, silb[:, 0], ALU.subtract), "silb", own=False)
            dve.wait_ge(S("params_in"), 64)
            lr, li = lam[:, 0, :], lam[:, 1, :]
            dve.wait_ge(S("dt"), 1)
            post(tt(pr["lrdt"], lr, pr["dt"], ALU.mult), "lrdt")
            link(tt(pr["th"], li, pr["dt"], ALU.mult))
            link(ts(pr["k"], pr["th"], INV_2PI, ROUND, ALU.mult, ALU.add))
            link(ts(pr["k"], pr["k"], ROUND, None, ALU.subtract))
            link(dve.scalar_tensor_tensor(out=pr["thr"], in0=pr["k"], scalar=-TWO_PI_HI, in1=pr["th"], op0=ALU.mult, op1=ALU.add))
            link(dve.scalar_tensor_tensor(out=pr["thr"], in0=pr["k"], scalar=-TWO_PI_LO, in1=pr["thr"], op0=ALU.mult, op1=ALU.add))
            link(ts(pr["phi"], pr["thr"], INV_2PI, None, ALU.mult))
            link(ts(pr["phi_hi"], pr["phi"], ROUND12, ROUND12, ALU.add, ALU.subtract))
            link(tt(pr["phi_lo"], pr["phi"], pr["phi_hi"], ALU.subtract))
            steps = C["steps"].unsqueeze(1).broadcast_to([P, ST, 32])

            def spread(v, n):
                return v.unsqueeze(2).broadcast_to([P, ST, n])

            low_parts(3)
            link(tt(phase_sin, steps, spread(pr["phi_hi"], 32), ALU.mult))
            link(ts(phase_tmp, phase_sin, ROUND, ROUND, ALU.add, ALU.subtract))
            link(tt(phase_sin, phase_sin, phase_tmp, ALU.subtract))
            link(tt(phase_tmp, steps, spread(pr["phi_lo"], 32), ALU.mult))
            link(tt(phase_sin, phase_sin, phase_tmp, ALU.add))
            link(ts(phase_cos, phase_sin, 0.25, None, ALU.add))
            link(ts(phase_tmp, phase_sin, ROUND, ROUND, ALU.add, ALU.subtract))
            post(tt(phase_sin, phase_sin, phase_tmp, ALU.subtract), "phases")
            link(ts(phase_tmp, phase_cos, ROUND, ROUND, ALU.add, ALU.subtract))
            post(tt(phase_cos, phase_cos, phase_tmp, ALU.subtract), "phases")
            low_parts(2)
            dve.wait_ge(S("mag"), 1)
            dve.wait_ge(S("trig"), 2)
            link(tt(pr["a_re"], pr["mag"], E[:, 0, :, 1], ALU.mult))
            link(tt(pr["a_im"], pr["mag"], E[:, 1, :, 1], ALU.mult))
            link(tt(pr["u"], lr, lr, ALU.mult))
            link(tt(pr["v"], li, li, ALU.mult))
            link(tt(pr["den"], pr["u"], pr["v"], ALU.add))
            link(dve.reciprocal(pr["w"], pr["den"]))
            link(tt(pr["zl_re"], lr, pr["w"], ALU.mult))
            link(tt(pr["zl_im"], li, pr["w"], ALU.mult))
            link(ts(pr["q"], pr["a_re"], -1.0, None, ALU.add))
            link(tt(pr["u"], pr["q"], pr["zl_re"], ALU.mult))
            link(tt(pr["v"], pr["a_im"], pr["zl_im"], ALU.mult))
            link(tt(pr["z_re"], pr["u"], pr["v"], ALU.add))
            link(tt(pr["u"], pr["a_im"], pr["zl_re"], ALU.mult))
            link(tt(pr["v"], pr["q"], pr["zl_im"], ALU.mult))
            link(tt(pr["z_im"], pr["u"], pr["v"], ALU.subtract))
            low_parts(4)
            dve.wait_ge(S("bc_in"), 48)
            dve.wait_ge(S("zeroed"), 2)
            m1 = phase_sin.rearrange("p s n -> p (s n)")[:, 0:512].rearrange("p (s c) -> p s c", s=ST)
            m2 = phase_sin.rearrange("p s n -> p (s n)")[:, 512:1024].rearrange("p (s c) -> p s c", s=ST)
            zr, zi = spread(pr["z_re"], 16), spread(pr["z_im"], 16)
            for e in range(2):
                link(tt(m1, braw[:, e], zr, ALU.mult))
                link(tt(m2, braw[:, 1 - e], zi, ALU.mult))
                for gl in range(2):
                    r = slice(64 * gl, 64 * gl + 64)
                    ins = tt(BX[r, e, :, 16 * gl:16 * gl + 16], m1[r], m2[r], ALU.subtract if e == 0 else ALU.add)
                    post(ins, "bx_done")
                    low_parts()
            for e in range(2):
                for gl in range(2):
                    r = slice(64 * gl, 64 * gl + 64)
                    ins = ts(CX[r, e, :, 16 * gl:16 * gl + 16], craw[r, e], -1.0 if e else 1.0, None, ALU.mult)
                    link(ins)
                low_parts()
            p1 = phase_cos.rearrange("p s n -> p (s n)")[:, 0:256].rearrange("p (s b) -> p s b", s=ST)
            p2 = phase_cos.rearrange("p s n -> p (s n)")[:, 256:512].rearrange("p (s b) -> p s b", s=ST)
            ar, ai = spread(pr["a_re"], DB), spread(pr["a_im"], DB)
            for e in range(2):
                link(tt(p1, h0[:, e], ar, ALU.mult))
                link(tt(p2, h0[:, 1 - e], ai, ALU.mult))
                link(tt(AH[:, e], p1, p2, ALU.subtract if e == 0 else ALU.add))
            post(dve.tensor_copy(rinv[:, 0:1], AH[:, 0, 0, 0:1]), "cx_done")
            low_parts(1)

            dve.wait_ge(S("x_in"), 16)
            dve.wait_ge(S("vec_in"), 16)
            inverse(0)
            dve.wait_ge(S("mod_ev"), 4 * NMOD0)
            g_pre = V["norm_pre"].rearrange("p (s k) -> p s k", s=4)
            g_post = V["norm_post"].rearrange("p (s k) -> p s k", s=4)
            norm_weights(0, g_pre[:, 0], None)
            modulated(0, 0, None)
            low_parts(3)

            def cosine(s):
                return TC[:, s].unsqueeze(2).broadcast_to([P, 2, 2, T])

            def sine(s):
                return TS[:, s].unsqueeze(2).broadcast_to([P, 2, 2, T])

            def y_read(f):
                dve.wait_ge(S("y_mm"), 2 * f + 2)
                post(dve.scalar_tensor_tensor(out=h[:, f, :], in0=h[:, f, :], scalar=V["ssm_d"][:, f:f + 1], in1=PS[:, 4, 0:T],
                                              op0=ALU.mult, op1=ALU.add), "y_read")

            for u in range(units):
                s = u % 2
                v = VS[s]
                left = [4 * len(mod_of_unit[u]) - (SPLIT if u == units - 1 else 0)]

                def piece():
                    if left[0]:
                        left[0] -= 1
                        low_parts()

                dve.wait_ge(S("u_mm"), u + 1)
                dve.wait_ge(S("tables"), 2 * u + 2)
                raw = PS[:, 0:4, 0:T].rearrange("p (i e) t -> p i e t", i=2)
                post(tt(t1, raw, cosine(s), ALU.mult), "u_read", own=False)
                post(tt(t2, raw, sine(s), ALU.mult), "u_read")
                piece()
                if u >= 2:
                    dve.wait_ge(S("y_mm"), u - 1)
                    dve.wait_ge(S("last_states"), 2 * (u - 1))
                link(tt(v[:, :, 0, :], t1[:, :, 0, :], t2[:, :, 1, :], ALU.add))
                piece()
                link(tt(v[:, :, 1, :], t1[:, :, 1, :], t2[:, :, 0, :], ALU.subtract))
                piece()
                first = v[:, :, :, SEQ::DS]
                link(tt(first, first, AH[:, :, 2 * u:2 * u + 2, :].rearrange("p e i b -> p i e b"), ALU.add))
                dve.wait_ge(S("decay"), u + 1)
                post(dve.tensor_tensor_scan(zf, decay, VSf[s], 0.0, ALU.mult, ALU.add), "scanned")
                piece()
                link(tt(t1, z, cosine(s), ALU.mult))
                piece()
                link(tt(t2, z, sine(s), ALU.mult))
                piece()
                link(tt(v[:, :, 0, :], t1[:, :, 0, :], t2[:, :, 1, :], ALU.subtract))
                post(tt(v[:, :, 1, :], t1[:, :, 1, :], t2[:, :, 0, :], ALU.add), "s_ready")
                piece()
                if u >= 2 and u % 2 == 0:
                    y_read((u - 2) // 2)
                low_parts(left[0])
            low_parts()
            for k in range(KT - 1):
                dve.wait_ge(S("g_ready"), k + 1)
                split(gb, h, k, "g_lo")
            y_read(7)
            low_parts(2)

            dve.wait_ge(S("g_ready"), KT)
            split(gb, h, KT - 1, "g_lo")
            dve.wait_ge(S("mod_ev"), 112)
            gate_weights(0, g_post[:, 0])
            for i, tile in ((1, 24), (2, 48), (3, 72)):
                norm_weights(tile, g_pre[:, i], g_post[:, i])
            norm_weights(96, V["norm_kv"], None)
            for m in range(KT):
                low_parts()
                dve.wait_ge(S("glu_ev"), m + 1)
                post(tt(wk[:, m, :], h[:, m, :], sig[:, m % 2, :], ALU.mult), "wk_done", own=(m == KT - 1))
            inverse(1)
            dve.wait_ge(S("x_in"), 32)
            added(1, 16, 0)
            inverse(2)
            modulated(2, 24, hb)
            ffn(0)
            dve.wait_ge(S("down0_ev"), KT)
            inverse(3)
            added(3, 40, 1)
            inverse(4)
            modulated(4, 96, hb_kv)
            dve.wait_ge(S("h_lo"), KT * nth_split[4])
            modulated(5, 48, None)
            low_parts(9)

            def rope(i, src, dst):
                dve.wait_ge(S("rope_mm"), i + 1)
                post(tt(rt1, PS[:, 4 + i % 2, 0:T], C["sin"], ALU.mult), "rope_read")
                link(tt(dst, src, C["cos"], ALU.mult))
                post(tt(dst, dst, rt1, ALU.add), "roped")

            for i, m in enumerate((4, 5, 8, 9)):
                rope(i, KV[:, m, :], KV[:, m, :])
            dve.wait_ge(S("kv_mm"), 12)
            for k in range(KT):
                dve.wait_ge(S("hp"), KT * (nth_mod[5] - 1) + k + 1)
                split(hb_kv, wk, k, "h_lo")
            low_parts(8)
            for m in range(KT):
                dve.wait_ge(S("q_ev"), m + 1)
                rope(4 + m, Qp[:, m, :], Qr[:, m, :])
            dve.wait_ge(S("spread_mm"), 1)
            pick = C["gate_pick"].unsqueeze(1).broadcast_to([P, 3 * DB, DS])
            link(tt(gx.rearrange("p c (b t) -> p (c b) t", b=DB), PS[:, 6, 0:192].rearrange("p (n t) -> p n t", t=DS), pick, ALU.mult))
            link(dve.tensor_reduce(gs.rearrange("p c b -> p (c b)"), gx.rearrange("p c (b t) -> p (c b) t", b=DB), AX, ALU.add))

            def by(v, n):
                return v.unsqueeze(2).broadcast_to([P, DB, n])

            pcv = PC[:, :, 0:NC]
            dve.wait_ge(S("c_mm"), 1)
            dve.wait_ge(S("small_zero"), 2)
            cpsum = PS[:, 7, 0:DB * NC].rearrange("p (b n) -> p b n", b=DB)
            link(dve.tensor_reduce(cmax, cpsum, AX, ALU.max))
            post(tt(pcv, cpsum, by(cmax, NC), ALU.subtract), "c_shift")
            dve.wait_ge(S("c_exp"), 1)
            link(dve.tensor_reduce(cs, pcv, AX, ALU.add))
            link(dve.reciprocal(cr, cs))
            link(tt(pcv, pcv, by(cr, NC), ALU.mult))
            link(tt(imp, PC[:, :, 4:57:4], PC[:, :, 5:58:4], ALU.add))
            link(tt(imp, imp, PC[:, :, 6:59:4], ALU.add))
            link(tt(imp2, PC[:, :, 3:56:4], PC[:, :, 7:60:4], ALU.add))
            post(dve.scalar_tensor_tensor(out=imp, in0=imp, scalar=2.0, in1=imp2, op0=ALU.mult, op1=ALU.add), "imp_ready")
            dve.wait_ge(S("imp_mm"), 1)
            total = PS[:, 6, 0:DB * NFREE].rearrange("p (b n) -> p b n", b=DB)
            blocks = C["blocks"].unsqueeze(1).broadcast_to([P, DB, NFREE])
            link(dve.tensor_reduce(imin, total, AX, ALU.min))
            link(tt(imp2, total, by(imin, NFREE), ALU.is_le))
            link(tt(imp2, imp2, blocks, ALU.mult))
            link(dve.tensor_reduce(imax, imp2, AX, ALU.max))
            link(tt(imp2, blocks, by(imax, NFREE), ALU.is_equal))
            post(ts(drop[:, :, 1:1 + NFREE], imp2, NEG, None, ALU.mult), "drop_done")
            link(tt(pcv, pcv, by(gs[:, 0, :], NC), ALU.mult))

            for j, (kind, a, qt) in enumerate(jobs):
                sc, s = SC[j % 2], j % 2
                dve.wait_ge(S("s_mm"), j + 1)
                if j >= 1:
                    dve.wait_ge(S("tr_mm"), groups_before[j - 1])
                if j >= 2:
                    dve.wait_ge(S("exp"), before(NX, j - 1))
                if kind == "prompt":
                    K = P * (qt + 1)
                    views = [sc[:, base:base + GQA * n].rearrange("p (g k) -> p g k", g=GQA) for base, n in ((2048, NCP), (0, K), (1024, K))]
                    mask = C["causal"][:, 2 * P - K:2 * P].unsqueeze(1).broadcast_to([P, GQA, K])
                    neg = C["cmp_neg"][:, NCP * qt:NCP * qt + NCP].unsqueeze(1).broadcast_to([P, GQA, NCP])
                    post(tt(views[0], PS[:, 4, 0:GQA * NCP].rearrange("p (g k) -> p g k", g=GQA), neg, ALU.add), "s_evd", own=False)
                    for br in (1, 2):
                        src = PS[:, 2 * br - 2:2 * br, :].rearrange("p c n -> p (c n)")[:, 0:GQA * K].rearrange("p (g k) -> p g k", g=GQA)
                        post(tt(views[br], src, mask, ALU.add), "s_evd")
                        if br == 1:
                            link(dve.tensor_reduce(nmax[:, s, 0:4], views[0], AX, ALU.max, negate=True))
                        post(dve.tensor_reduce(nmax[:, s, 4 * br:4 * br + 4], views[br], AX, ALU.max, negate=True), "nmax", own=False)
                else:
                    post(tt(sc[:, 0:1024].rearrange("p (n k) -> p n k", n=16), PS[:, 0:2, :].rearrange("p c n -> p (c n)").rearrange("p (n k) -> p n k", n=16),
                            drop[:, a, :].unsqueeze(2).broadcast_to([P, 16, 64]), ALU.add), "s_evd", own=False)
                    post(tt(sc[:, 1024:1032], PS[:, 3, 0:DS], C["new_mask"], ALU.add), "s_evd")
                    post(dve.tensor_reduce(nmax[:, s, 0:1], sc[:, 0:1032], AX, ALU.max, negate=True), "nmax", own=False)
                    post(tt(sc[:, 1032:1040], PS[:, 2, 0:DS], C["win_mask"], ALU.add), "s_evd")
                    post(dve.tensor_copy(sc[:, 1040:1544], PS[:, 2, DS:512]), "s_evd", own=False)
                    post(tt(sc[:, 1544:1552], PS[:, 3, DS:2 * DS], C["new_mask"], ALU.add), "s_evd")
                    post(dve.tensor_reduce(nmax[:, s, 1:2], sc[:, 1032:1552], AX, ALU.max, negate=True), "nmax", own=False)
                if kind == "prompt":
                    gate = gp[:, qt, :].rearrange("p (c m) -> p c m", c=3)[:, :, 4 * a:4 * a + 4]
                    fv = fac[:, s, :].rearrange("p (c g) -> p c g", c=3)
                    for lo_br, hi_br in ((0, 2), (2, 3)):
                        dve.wait_ge(S("exp"), before(NX, j) + 4 * hi_br)
                        link(dve.reciprocal(fac[:, s, 4 * lo_br:4 * hi_br], ssum[:, s, 4 * lo_br:4 * hi_br]))
                        post(tt(fv[:, lo_br:hi_br], fv[:, lo_br:hi_br], gate[:, lo_br:hi_br], ALU.mult), "fac")
                        if lo_br == 0:
                            f0 = fac[:, s, 0:4].unsqueeze(2).broadcast_to([P, GQA, NCP])
                            link(tt(views[0], views[0], f0, ALU.mult))
                            valid = C["cmp_valid"][:, NCP * qt:NCP * qt + NCP].unsqueeze(1).broadcast_to([P, GQA, NCP])
                            post(tt(views[0], views[0], valid, ALU.mult), "p_ready", own=False)
                        br = hi_br - 1
                        for g in range(GQA):
                            i = 4 * br + g
                            post(ts(views[br][:, g, :], views[br][:, g, :], fac[:, s, i:i + 1], None, ALU.mult), "p_ready", own=False)
                else:
                    for i, v in enumerate((sc[:, 0:1032], sc[:, 1032:1552])):
                        dve.wait_ge(S("exp"), before(NX, j) + i + 1)
                        link(dve.reciprocal(fac[:, s, i:i + 1], ssum[:, s, i:i + 1]))
                        post(tt(fac[:, s, i:i + 1], fac[:, s, i:i + 1], gs[:, i + 1, a:a + 1], ALU.mult), "fac")
                        post(ts(v, v, fac[:, s, i:i + 1], None, ALU.mult), "p_ready", own=False)
            low_parts(3)
            dve.wait_ge(S("o_ev"), before(NOE, len(jobs)))
            dve.wait_ge(S("pv_mm"), len(jobs))
            for k in range(KT):
                split(ob, O, k, "o_lo")
            low_parts(8)
            dve.wait_ge(S("o_ev2"), KT)
            inverse(6)
            added(6, 64, 2)
            inverse(7)
            modulated(7, 72, hb)
            ffn(1)
            dve.wait_ge(S("down1_ev"), KT)
            inverse(8)
            added(8, 88, 3)

def _weight_chunks(w, group):
    K, M = w.shape
    kt, mt = K // P, M // P
    return w.reshape(kt, P, mt // group, group, P).transpose(2, 1, 3, 0, 4).reshape(mt // group, P, group * kt * P)


def _features(v):
    t = v.reshape(*v.shape[:-1], v.shape[-1] // P, P)
    return t.transpose(t.ndim - 1, *range(t.ndim - 1)).reshape(P, -1)


def _constants():
    import numpy as np

    f = np.float32
    tab = {}
    tab["ident"] = np.eye(P, dtype=f)
    tab["ones"] = np.ones((P, P), f)
    half = HD // 2
    rot = np.zeros((P, P), f)
    for base in (0, HD):
        for m in range(half):
            rot[base + m + half, base + m] = -1.0
            rot[base + m, base + m + half] = 1.0
    tab["rot"] = rot
    r = np.arange(P)
    same_head = r[:, None] // (GQA * DS) == r[None, :] // (GQA * DS)
    tab["group_sum"] = (same_head & (r[:, None] % DS == r[None, :] % DS)).astype(f)
    spread = np.zeros((P, 3, P), f)
    for br in range(3):
        for h in range(NH):
            spread[br * NH + h, br, h * DS:(h + 1) * DS] = 1.0
    tab["gate_spread"] = spread.reshape(P, -1)
    pos = np.concatenate([np.arange(SEQ)] + [PAST + np.arange(DS)] * DB).astype(f)
    freqs = (f(10000.0) ** (-np.arange(half, dtype=f) / f(half))).astype(f)
    ang = (pos[None, :] * freqs[np.arange(P) % half][:, None]).astype(f)
    tab["cos"] = np.cos(ang).astype(f)
    tab["sin"] = np.sin(ang).astype(f)
    k = np.arange(P)
    tab["causal"] = np.concatenate([np.zeros((P, P), f), np.where(k[None, :] <= r[:, None], 0.0, NEG).astype(f)], 1)
    j = np.arange(DS)
    q = (r % DS)[:, None]
    tab["new_mask"] = np.where(j[None, :] <= q, 0.0, NEG).astype(f)
    tab["win_mask"] = np.where(j[None, :] > q, 0.0, NEG).astype(f)
    tab["gate_pick"] = (j[None, :] == q).astype(f)
    ends = np.arange(NCP) * 16 + 31
    valid = np.stack([ends[None, :] <= (r[:, None] + qt * P) for qt in range(2)], 1)
    tab["cmp_valid"] = valid.astype(f).reshape(P, -1)
    tab["cmp_neg"] = np.where(valid, 0.0, NEG).astype(f).reshape(P, -1)
    tab["blocks"] = np.broadcast_to(np.arange(1, NFREE + 1, dtype=f), (P, NFREE))
    run = np.ones(T, f)
    run[0] = 0.0
    run[SEQ::DS] = 0.0
    tab["scan_run"] = np.broadcast_to(run, (P, T))
    tab["steps"] = np.broadcast_to(np.concatenate([np.arange(16), 16 * np.arange(16)]).astype(f), (P, 32))
    assert {n: t.shape[1] for n, t in tab.items()} == dict(CONST)
    return np.concatenate([tab[n] for n, _ in CONST], 1).astype(f)


def _lay_out(i):
    import numpy as np

    i = {n: np.asarray(a) for n, a in i.items()}
    d = {"consts": _constants()}
    tokens = np.concatenate([i["x_prompt"].reshape(SEQ, D), i["x_sample"].reshape(DB * DS, D)], 0)
    d["x"] = _features(tokens).reshape(P, T, KT).transpose(0, 2, 1)
    d["c"] = _features(np.concatenate([i["c_prompt"], i["c_sample"]], 0)).reshape(P, NB, KT).transpose(0, 2, 1)
    d["page_table"] = i["page_table"].reshape(1, DB * NPG)
    pool = i["cache_nsa_paged"]
    n_phys = pool.shape[0]
    d["pool_cmp"] = pool[:, :, 0:2].reshape(n_phys, 64, 2, 2, KVH, HD).transpose(3, 0, 2, 5, 4, 1).reshape(2, n_phys, P, KVH * 64)
    d["pool_k"] = pool[:, :, 2].reshape(n_phys, PAGE, 2, 2, HD).transpose(0, 3, 4, 2, 1).reshape(n_phys, P, 2 * PAGE)
    d["pool_v"] = pool[:, :, 3].reshape(n_phys, PAGE, KVH * HD)
    win = i["cache_nsa_window"]
    d["win_k"] = win[:, :, 0].reshape(DB, WIN, 2, 2, HD).transpose(0, 3, 4, 2, 1).reshape(DB, P, 2 * WIN)
    d["win_v"] = win[:, :, 1].reshape(DB, WIN // P, P, KVH * HD).transpose(0, 2, 1, 3).reshape(DB, P, -1)
    def states(a):
        return a.reshape(ST, P).T

    d["lam"] = np.stack([states(i["ssm_lam_re"]), states(i["ssm_lam_im"])], 1).reshape(P, 2 * ST)
    d["log_dt"] = i["ssm_log_dt"].reshape(ST, 2).T.reshape(2, 1, ST)
    h0 = np.stack([i["state_ssm_re"], i["state_ssm_im"]], 0).reshape(2, DB, ST, P)
    d["ssm_h0"] = h0.transpose(3, 0, 2, 1).reshape(P, -1)
    b = np.stack([i["ssm_b_re"], i["ssm_b_im"]], 0).reshape(2, ST, P, 16)
    d["ssm_b"] = b.transpose(2, 0, 1, 3).reshape(P, -1)
    c = np.stack([i["ssm_c_re"], i["ssm_c_im"]], 0).reshape(2, ST, 2, 16, HD)
    d["ssm_c"] = c.transpose(2, 4, 0, 1, 3).reshape(P, -1)
    def pairs(a):
        return a.reshape(*a.shape[:-1], 2, FT, P).swapaxes(-2, -3).reshape(a.shape)

    conv_w = _features(pairs(i["ffn_conv_w"])).reshape(P, 2, 3, 2 * FT).transpose(0, 1, 3, 2)
    conv_b = _features(pairs(i["ffn_conv_b"]))
    pre = _features(pairs(i["state_ffn_conv"])).reshape(P, 2, 16, 2 * FT).transpose(0, 1, 3, 2)
    d["prefix"] = pre.reshape(P, 2, -1).transpose(1, 0, 2)
    pe = i["cmp_pe"].reshape(2, 16, 2, HD).transpose(2, 3, 0, 1).reshape(P, 32)
    vec = {
        "norm_pre": _features(i["norm_pre"]), "norm_post": _features(i["norm_post"]), "norm_kv": _features(i["norm_kv"]),
        "b_mod": np.concatenate([_features(i["b_mod"]), _features(i["b_mod_kv"])], 1), "ssm_d": _features(i["ssm_d"]),
        "b_glu": _features(i["b_glu"]), "conv_w": conv_w.reshape(P, -1), "conv_b": conv_b, "cmp_pe": pe,
        "cmp_b1": i["cmp_b1"].T, "cmp_w2": i["cmp_w2"].transpose(1, 0, 2).reshape(P, -1),
    }
    assert {n: t.shape[1] for n, t in vec.items()} == dict(VEC), {n: t.shape[1] for n, t in vec.items()}
    d["vec"] = np.concatenate([vec[n] for n, _ in VEC], 1)
    wm = i["w_mod"].reshape(4, D, 3 * D)
    d["w_mod"] = np.concatenate([_weight_chunks(wm[s], 4) for s in range(4)], 0)
    d["w_mod_kv"] = _weight_chunks(i["w_mod_kv"], 4)
    d["w_glu"] = _weight_chunks(i["w_glu"][0], 4)
    d["w_kv"] = _weight_chunks(i["w_kv"], 4)
    wq = i["w_qg"][0][:, :D].reshape(D, 2, 2, GQA, HD).transpose(0, 1, 3, 2, 4).reshape(D, D)
    d["w_q"] = _weight_chunks(wq, 4)
    d["w_gate"] = i["w_qg"][0][:, D:].reshape(KT, P, 3 * NH).transpose(1, 0, 2).reshape(P, -1)
    wo = i["w_o"][0].reshape(2, 2, GQA, HD, D).transpose(0, 2, 1, 3, 4).reshape(D, D)
    d["w_o"] = _weight_chunks(wo, 4)
    d["cmp_w1"] = i["cmp_w1"].reshape(2, 16, P, P).transpose(0, 2, 1, 3).reshape(2, P, 16 * P)
    up = pairs(i["ffn_w_up"])
    d["w_up"] = np.concatenate([_weight_chunks(up[l], 4) for l in range(2)], 0)
    d["w_down"] = np.concatenate([_weight_chunks(i["ffn_w_down"][l], 1) for l in range(2)], 0)
    return {n: np.ascontiguousarray(a) for n, a in d.items()}


def _rows(o):
    r = o.transpose(2, 1, 0).reshape(T, -1)
    return r[:SEQ], r[SEQ:]


def _returned(o):
    import numpy as np

    y_p, y_s = _rows(o["out_y"])
    kv_p, kv_s = (r.reshape(-1, 6, KVH, HD) for r in _rows(o["out_kv"]))
    ssm = o["out_ssm"].reshape(P, ST, 2, NB).transpose(2, 3, 1, 0).reshape(2, NB, 64, 64)
    conv = o["out_conv"].reshape(2, P, FT, 2, NB, 2).transpose(0, 4, 5, 3, 2, 1).reshape(2, NB, 2, 2 * FT * P)
    out = (
        y_p.reshape(1, SEQ, D), y_s.reshape(DB, DS, D),
        kv_p[:, :4].reshape(1, SEQ, 4, KVH, HD), kv_s[:, :4].reshape(DB, DS, 4, KVH, HD),
        kv_p[:, 4:].reshape(1, SEQ, 2, KVH, HD), kv_s[:, 4:].reshape(DB, DS, 2, KVH, HD),
        ssm[0, :1][None], ssm[1, :1][None], ssm[0, 1:][None], ssm[1, 1:][None],
        conv[:, :1], conv[:, 1:],
    )
    return tuple(np.ascontiguousarray(a) for a in out)


_OUTS = {"out_y": (P, KT, T), "out_kv": (P, 12, T), "out_ssm": (P, ST * 2 * NB), "out_conv": (2, P, 2 * FT * 2 * NB)}


def kernel(**inputs):
    import concourse.bacc as _bacc
    from concourse import mybir as _mybir
    from concourse.bass_utils import run_bass_kernel_spmd as _run

    nc = _bacc.Bacc("TRN2", target_bir_lowering=False, num_devices=1)
    arrays = _lay_out(inputs)
    dram = {n: nc.dram_tensor(n, a.shape, _mybir.dt.from_np(a.dtype), kind="ExternalInput").ap() for n, a in arrays.items()}
    for n, shape in _OUTS.items():
        dram[n] = nc.dram_tensor(n, shape, _mybir.dt.float32, kind="ExternalOutput").ap()
    build_step(nc, dram)
    r = _run(nc, [arrays], core_ids=[0])
    return _returned(r.results[0])
```
